# Optimizing a Trainium2 kernel written in Bass

```python
import jax, jax.numpy as jnp
from jax import lax
import numpy as np
import jax
import jax.numpy as jnp

D_MODEL = 1024
BATCH = 1
SEQ = 1024
DEPTH = 1

N_MIXERS = 4
EPS = 1e-6
CONV_WIDTH = 31
HGRN_EXPAND = 128
HGRN_HEADS = D_MODEL // HGRN_EXPAND
HGRN_CHUNK = 64
POOL_WINDOWS = (2, 4, 8, 16)
POOL_GROUPS = len(POOL_WINDOWS)
POOL_DIM = D_MODEL // POOL_GROUPS
SB_HEADS = 16
SB_HEAD_DIM = D_MODEL // SB_HEADS
SB_BLOCK = 128
MOE_GROUPS = 4
MOE_EXPERTS_PER_GROUP = 8
MOE_EXPERTS = MOE_GROUPS * MOE_EXPERTS_PER_GROUP
MOE_TOP_K = 2
MOE_HIDDEN = D_MODEL // 2
MOE_BLOCK = 128


def _n_layers_of(m):
    return (DEPTH - m + N_MIXERS - 1) // N_MIXERS

def rmsnorm(x, g):
    xf = x.astype(jnp.float32)
    y = xf * lax.rsqrt(jnp.mean(xf * xf, axis=-1, keepdims=True) + EPS) * g.astype(jnp.float32)
    return y.astype(x.dtype)

def layernorm(x, g, b):
    xf = x.astype(jnp.float32)
    mu = jnp.mean(xf, axis=-1, keepdims=True)
    xc = xf - mu
    y = xc * lax.rsqrt(jnp.mean(xc * xc, axis=-1, keepdims=True) + EPS) * g + b
    return y.astype(x.dtype)

def conformer_conv(h, w_in, b_in, w_dw, b_dw, ln_g, ln_b, w_out):
    u = h @ w_in + b_in
    a, gt = jnp.split(u, 2, axis=-1)
    u = a * jax.nn.sigmoid(gt)
    y = lax.conv_general_dilated(
        u, w_dw[:, None, :], window_strides=(1,),
        padding=[(CONV_WIDTH - 1, 0)],
        dimension_numbers=('NWC', 'WIO', 'NWC'),
        feature_group_count=D_MODEL) + b_dw
    y = jax.nn.silu(layernorm(y, ln_g, ln_b))
    return (y @ w_out).astype(h.dtype)

def hgrn_lower_bounds(logits):
    p = jax.nn.softmax(logits.astype(jnp.float32), axis=0)
    cum = jnp.cumsum(p, axis=0)
    return cum - cum[0:1]

def hgrn2(h, w_in, lb, norm_g, w_out):
    B, S, _ = h.shape
    H, dh, C = HGRN_HEADS, HGRN_EXPAND, HGRN_CHUNK
    n_chunk = S // C
    q, f, i_in, g = jnp.split((h @ w_in).astype(jnp.float32), 4, axis=-1)
    q = jax.nn.silu(q)
    forget = lb + (1.0 - lb) * jax.nn.sigmoid(f)
    log_f = jnp.log(forget)
    k = (1.0 - lb) * jax.nn.sigmoid(-f)

    def chunks(t):
        return t.reshape(B, n_chunk, C, H, dh).transpose(1, 0, 3, 2, 4)

    causal = jnp.tril(jnp.ones((C, C), bool))[:, :, None]

    def step(state, inp):
        qc, kc, vc, lfc = inp
        b = jnp.cumsum(lfc, axis=2)
        o_inter = jnp.einsum('bhtk,bhkv->bhtv', qc * jnp.exp(b), state)
        rel = jnp.where(causal, b[:, :, :, None, :] - b[:, :, None, :, :], -jnp.inf)
        scores = jnp.einsum('bhtk,bhsk,bhtsk->bhts', qc, kc, jnp.exp(rel))
        o_intra = jnp.einsum('bhts,bhsv->bhtv', scores, vc)
        b_end = b[:, :, -1:, :]
        state = (jnp.exp(b_end[:, :, 0, :, None]) * state
                 + jnp.einsum('bhsk,bhsv->bhkv', kc * jnp.exp(b_end - b), vc))
        return state, o_inter + o_intra

    state0 = jnp.zeros((B, H, dh, dh), jnp.float32)
    _, o = lax.scan(step, state0, (chunks(q), chunks(k), chunks(i_in), chunks(log_f)))
    o = o.transpose(1, 0, 3, 2, 4).reshape(B, S, H, dh)
    o = o * lax.rsqrt(jnp.mean(o * o, axis=-1, keepdims=True) + EPS) * norm_g.reshape(H, dh)
    o = o.reshape(B, S, D_MODEL) * jax.nn.silu(g)
    return (o.astype(h.dtype) @ w_out).astype(h.dtype)

def multiscale_pool(h, w_grp, b_grp, ls):
    B, S, _ = h.shape
    hf = h.astype(jnp.float32).reshape(B, S, POOL_GROUPS, POOL_DIM)
    cs0 = jnp.pad(jnp.cumsum(hf, axis=1), ((0, 0), (1, 0), (0, 0), (0, 0)))
    pos = jnp.arange(S)
    outs = []
    for gi, w in enumerate(POOL_WINDOWS):
        c_g = cs0[:, :, gi]
        upper = c_g[:, 1:]
        lower = jnp.pad(c_g, ((0, 0), (w - 1, 0), (0, 0)))[:, :S]
        count = jnp.minimum(pos + 1, w).astype(jnp.float32)[None, :, None]
        outs.append((upper - lower) / count - hf[:, :, gi])
    pooled = jnp.stack(outs, axis=2)
    y = jnp.einsum('bsgc,gcd->bsgd', pooled, w_grp.astype(jnp.float32))
    y = y.reshape(B, S, D_MODEL) + b_grp
    return (y * ls).astype(h.dtype)

def stick_breaking_attention(h, w_qkv, w_out):
    B, S, _ = h.shape
    qkv = (h @ w_qkv).reshape(B, S, 3, SB_HEADS, SB_HEAD_DIM)
    q = qkv[:, :, 0].transpose(0, 2, 1, 3)
    k = qkv[:, :, 1].transpose(0, 2, 1, 3)
    v = qkv[:, :, 2].transpose(0, 2, 1, 3)
    n_blk = S // SB_BLOCK
    q_blocks = q.reshape(B, SB_HEADS, n_blk, SB_BLOCK, SB_HEAD_DIM).transpose(2, 0, 1, 3, 4)
    key_pos = jnp.arange(S)
    scale = SB_HEAD_DIM ** -0.5

    def one_block(args):
        qb, bi = args
        z = jnp.einsum('bhtd,bhsd->bhts', qb, k).astype(jnp.float32) * scale
        q_pos = bi * SB_BLOCK + jnp.arange(SB_BLOCK)
        strict = key_pos[None, :] < q_pos[:, None]
        log_keep = jnp.where(strict, jax.nn.log_sigmoid(-z), 0.0)
        later = lax.cumsum(log_keep, axis=3, reverse=True) - log_keep
        weights = jnp.where(strict, jnp.exp(jax.nn.log_sigmoid(z) + later), 0.0)
        return jnp.einsum('bhts,bhsd->bhtd', weights.astype(v.dtype), v)

    o = lax.map(one_block, (q_blocks, jnp.arange(n_blk)))
    o = o.transpose(1, 0, 3, 2, 4).reshape(B, S, D_MODEL)
    return (o @ w_out).astype(h.dtype)

def hier_moe(h, w_rg, b_rg, w_re, b_re, w_gate, w_up, w_down):
    B, S, D = h.shape
    T = B * S
    xt = h.reshape(T, D)
    grp_logits = (xt @ w_rg + b_rg).astype(jnp.float32)
    grp = jnp.argmax(grp_logits, axis=-1)
    grp_p = jnp.take_along_axis(jax.nn.softmax(grp_logits, axis=-1), grp[:, None], axis=1)[:, 0]
    exp_logits = (xt @ w_re + b_re).astype(jnp.float32).reshape(T, MOE_GROUPS, MOE_EXPERTS_PER_GROUP)
    in_grp = jnp.take_along_axis(exp_logits, grp[:, None, None], axis=1)[:, 0]
    top_val, top_idx = lax.top_k(in_grp, MOE_TOP_K)
    gate = grp_p[:, None] * jax.nn.softmax(top_val, axis=-1)
    expert = grp[:, None] * MOE_EXPERTS_PER_GROUP + top_idx

    n_assign = T * MOE_TOP_K
    e_flat = expert.reshape(n_assign).astype(jnp.int32)
    g_flat = gate.reshape(n_assign)
    t_flat = jnp.repeat(jnp.arange(T, dtype=jnp.int32), MOE_TOP_K)
    order = jnp.argsort(e_flat)
    e_s, t_s, g_s = e_flat[order], t_flat[order], g_flat[order]
    counts = jnp.bincount(e_flat, length=MOE_EXPERTS).astype(jnp.int32)
    padded = ((counts + MOE_BLOCK - 1) // MOE_BLOCK) * MOE_BLOCK
    seg_start = jnp.cumsum(counts) - counts
    pad_end = jnp.cumsum(padded)
    pad_start = pad_end - padded
    dest = pad_start[e_s] + (jnp.arange(n_assign, dtype=jnp.int32) - seg_start[e_s])
    n_slots = n_assign + MOE_EXPERTS * MOE_BLOCK
    n_blk = n_slots // MOE_BLOCK
    slot_tok = jnp.full((n_slots,), T, jnp.int32).at[dest].set(t_s)
    slot_gate = jnp.zeros((n_slots,), jnp.float32).at[dest].set(g_s)
    blk_start = jnp.arange(n_blk, dtype=jnp.int32) * MOE_BLOCK
    blk_expert = jnp.minimum(jnp.searchsorted(pad_end, blk_start, side='right'),
                             MOE_EXPERTS - 1).astype(jnp.int32)
    x_pad = jnp.concatenate([xt, jnp.zeros((1, D), xt.dtype)], axis=0)
    xs = x_pad[slot_tok].reshape(n_blk, MOE_BLOCK, D)

    def run_block(args):
        xb, e = args
        hid = jax.nn.silu(xb @ w_gate[e]) * (xb @ w_up[e])
        return hid @ w_down[e]

    ys = lax.map(run_block, (xs, blk_expert)).reshape(n_slots, D)
    out = jnp.zeros((T + 1, D), jnp.float32).at[slot_tok].add(
        ys.astype(jnp.float32) * slot_gate[:, None])[:T]
    return out.reshape(B, S, D).astype(h.dtype)

def first_inputs(seed: int = 0) -> dict:
    key = jax.random.key(seed)
    ks = iter(jax.random.split(key, 40))

    def nrm(shape, scale):
        return jax.random.normal(next(ks), shape, jnp.float32) * scale

    D = D_MODEL
    NA, NB, NC, ND = (_n_layers_of(m) for m in range(N_MIXERS))
    inv = D ** -0.5
    E, F = MOE_EXPERTS, MOE_HIDDEN
    return {
        "x": nrm((BATCH, SEQ, D), 1.0),
        "c": nrm((BATCH, D), 1.0),
        "ada_w": nrm((DEPTH, D, 6 * D), 0.5 * inv),
        "ada_b": nrm((DEPTH, 6 * D), 0.02),
        "norm_mix_g": 1.0 + nrm((DEPTH, D), 0.05),
        "norm_ffn_g": 1.0 + nrm((DEPTH, D), 0.05),
        "final_g": 1.0 + nrm((D,), 0.05),
        "conv_w_in": nrm((NA, D, 2 * D), inv),
        "conv_b_in": nrm((NA, 2 * D), 0.02),
        "conv_w_dw": nrm((NA, CONV_WIDTH, D), CONV_WIDTH ** -0.5),
        "conv_b_dw": nrm((NA, D), 0.02),
        "conv_ln_g": 1.0 + nrm((NA, D), 0.05),
        "conv_ln_b": nrm((NA, D), 0.02),
        "conv_w_out": nrm((NA, D, D), inv),
        "hgrn_w_in": nrm((NB, D, 4 * D), inv),
        "hgrn_lb_logits": nrm((DEPTH, D), 0.5),
        "hgrn_norm_g": 1.0 + nrm((NB, D), 0.05),
        "hgrn_w_out": nrm((NB, D, D), inv),
        "pool_w": nrm((NC, POOL_GROUPS, POOL_DIM, POOL_DIM), POOL_DIM ** -0.5),
        "pool_b": nrm((NC, D), 0.02),
        "pool_scale": 1.0 + nrm((NC, D), 0.1),
        "sb_w_qkv": nrm((ND, D, 3 * D), inv),
        "sb_w_out": nrm((ND, D, D), inv),
        "moe_w_rg": nrm((DEPTH, D, MOE_GROUPS), inv),
        "moe_b_rg": nrm((DEPTH, MOE_GROUPS), 0.01),
        "moe_w_re": nrm((DEPTH, D, E), inv),
        "moe_b_re": nrm((DEPTH, E), 0.01),
        "moe_w_gate": nrm((DEPTH, E, D, F), inv),
        "moe_w_up": nrm((DEPTH, E, D, F), inv),
        "moe_w_down": nrm((DEPTH, E, F, D), F ** -0.5),
    }

def first_block(x, c, ada_w, ada_b, norm_mix_g, norm_ffn_g, final_g,
              conv_w_in, conv_b_in, conv_w_dw, conv_b_dw, conv_ln_g, conv_ln_b, conv_w_out,
              hgrn_w_in, hgrn_lb_logits, hgrn_norm_g, hgrn_w_out,
              pool_w, pool_b, pool_scale,
              sb_w_qkv, sb_w_out,
              moe_w_rg, moe_b_rg, moe_w_re, moe_b_re, moe_w_gate, moe_w_up, moe_w_down):
    c_act = jax.nn.silu(c)
    lb_all = hgrn_lower_bounds(hgrn_lb_logits)
    for i in range(DEPTH):
        m, j = i % N_MIXERS, i // N_MIXERS
        mod = c_act @ ada_w[i] + ada_b[i]
        sh1, sc1, g1, sh2, sc2, g2 = [t[:, None, :] for t in jnp.split(mod, 6, axis=-1)]
        h = rmsnorm(x, norm_mix_g[i]) * (1 + sc1) + sh1
        if m == 0:
            y = conformer_conv(h, conv_w_in[j], conv_b_in[j], conv_w_dw[j], conv_b_dw[j],
                               conv_ln_g[j], conv_ln_b[j], conv_w_out[j])
        elif m == 1:
            y = hgrn2(h, hgrn_w_in[j], lb_all[i], hgrn_norm_g[j], hgrn_w_out[j])
        elif m == 2:
            y = multiscale_pool(h, pool_w[j], pool_b[j], pool_scale[j])
        else:
            y = stick_breaking_attention(h, sb_w_qkv[j], sb_w_out[j])
        x = x + g1 * y
        h = rmsnorm(x, norm_ffn_g[i]) * (1 + sc2) + sh2
        x = x + g2 * hier_moe(h, moe_w_rg[i], moe_b_rg[i], moe_w_re[i], moe_b_re[i],
                              moe_w_gate[i], moe_w_up[i], moe_w_down[i])
    return rmsnorm(x, final_g)


ATT_HEADS = 8
ATT_KV_HEADS = 2
ATT_HEAD_DIM = 128
ATT_GROUP = ATT_HEADS // ATT_KV_HEADS
ROPE_THETA = 500000.0
ROPE_FRACTION = 4
IDX_HEADS = 4
IDX_DIM = 64
TOPK_MAX = 256
Q_BLOCK = 128
SSM_EXPAND = 2
SSM_D_INNER = SSM_EXPAND * D_MODEL
SSM_HEAD_DIM = 64
SSM_HEADS = SSM_D_INNER // SSM_HEAD_DIM
SSM_GROUPS = 4
SSM_STATE = 128
SSM_CONV = 4
SSM_CHUNK = 128
N_BRANCHES = 2

ATT_Q_DIM = ATT_HEADS * ATT_HEAD_DIM
ATT_KV_DIM = ATT_KV_HEADS * ATT_HEAD_DIM
ATT_ROT_DIM = ATT_HEAD_DIM // ROPE_FRACTION
IDX_ROT_DIM = IDX_DIM // ROPE_FRACTION
SSM_CONV_DIM = SSM_D_INNER + 2 * SSM_GROUPS * SSM_STATE
IN_SPLITS = (ATT_Q_DIM, ATT_KV_DIM, ATT_KV_DIM, ATT_Q_DIM, IDX_HEADS * IDX_DIM, IDX_DIM, IDX_HEADS,
             SSM_D_INNER, SSM_CONV_DIM, SSM_HEADS, N_BRANCHES * D_MODEL)
IN_DIM = sum(IN_SPLITS)


def _split_points():
    pts, acc = [], 0
    for s in IN_SPLITS[:-1]:
        acc += s
        pts.append(acc)
    return pts

def rms_norm(x, g):
    xf = x.astype(jnp.float32)
    y = xf * lax.rsqrt(jnp.mean(xf * xf, axis=-1, keepdims=True) + EPS)
    return y.astype(x.dtype) * g

def layer_norm(x, g, b):
    xf = x.astype(jnp.float32)
    mu = jnp.mean(xf, axis=-1, keepdims=True)
    var = jnp.mean(jnp.square(xf - mu), axis=-1, keepdims=True)
    return ((xf - mu) * lax.rsqrt(var + EPS)).astype(x.dtype) * g + b

def rope_tables(positions, rot_dim):
    inv = jnp.power(ROPE_THETA, -(jnp.arange(0, rot_dim, 2, dtype=jnp.float32) / rot_dim))
    ang = positions.astype(jnp.float32)[..., None] * inv
    return jnp.cos(ang)[:, :, None, :], jnp.sin(ang)[:, :, None, :]

def partial_rope(x, cos, sin):
    half = cos.shape[-1]
    rot = 2 * half
    x1 = x[..., :half].astype(jnp.float32)
    x2 = x[..., half:rot].astype(jnp.float32)
    r1 = x1 * cos - x2 * sin
    r2 = x2 * cos + x1 * sin
    return jnp.concatenate([r1.astype(x.dtype), r2.astype(x.dtype), x[..., rot:]], axis=-1)

def causal_depthwise_conv(u, w, b):
    ch = u.shape[-1]
    y = lax.conv_general_dilated(u, w[:, None, :].astype(u.dtype), window_strides=(1,),
                                 padding=[(SSM_CONV - 1, 0)],
                                 dimension_numbers=("NWC", "WIO", "NWC"),
                                 feature_group_count=ch)
    return y + b

def segsum(a):
    n = a.shape[-1]
    ar = jnp.broadcast_to(a[..., :, None], a.shape + (n,))
    ar = jnp.where(jnp.tril(jnp.ones((n, n), dtype=bool), -1), ar, 0.0)
    cs = jnp.cumsum(ar, axis=-2)
    return jnp.where(jnp.tril(jnp.ones((n, n), dtype=bool)), cs, -jnp.inf)

def ssd(xh, dt, a, bm, cm):
    bsz, s, h, p = xh.shape
    g, n = bm.shape[2], bm.shape[3]
    r = h // g
    nc, ln = s // SSM_CHUNK, SSM_CHUNK
    xc = (xh * dt[..., None]).reshape(bsz, nc, ln, g, r, p)
    adt = (dt * a).reshape(bsz, nc, ln, g, r).transpose(0, 1, 3, 4, 2)
    a_cum = jnp.cumsum(adt, axis=-1)
    bc = bm.reshape(bsz, nc, ln, g, n)
    cc = cm.reshape(bsz, nc, ln, g, n)
    decay = jnp.exp(segsum(adt))
    cb = jnp.einsum("bclgn,bcsgn->bcgls", cc, bc)
    y_diag = jnp.einsum("bcgls,bcgrls,bcsgrp->bclgrp", cb, decay, xc)
    decay_states = jnp.exp(a_cum[..., -1:] - a_cum)
    states = jnp.einsum("bclgn,bcgrl,bclgrp->bcgrpn", bc, decay_states, xc)
    chunk_decay = jnp.exp(a_cum[..., -1])

    def step(hstate, inp):
        st, dec = inp
        return dec[..., None, None] * hstate + st, hstate

    h0 = jnp.zeros((bsz, g, r, p, n), dtype=xc.dtype)
    _, prev = lax.scan(step, h0, (states.swapaxes(0, 1), chunk_decay.swapaxes(0, 1)))
    prev = prev.swapaxes(0, 1)
    y_off = jnp.einsum("bclgn,bcgrpn,bcgrl->bclgrp", cc, prev, jnp.exp(a_cum))
    return (y_diag + y_off).reshape(bsz, s, h, p)

def sparse_attention(q, k, v, q_idx, k_idx, w_idx):
    bsz, s = q.shape[0], q.shape[1]
    topk = min(TOPK_MAX, s // 4)
    nblk = s // Q_BLOCK
    scale = ATT_HEAD_DIM ** -0.5
    key_pos = jnp.arange(s)
    gather = jax.vmap(lambda arr, idx: arr[idx])

    def to_blocks(arr):
        return arr.reshape((bsz, nblk, Q_BLOCK) + arr.shape[2:]).swapaxes(0, 1)

    qg = q.reshape(bsz, s, ATT_KV_HEADS, ATT_GROUP, ATT_HEAD_DIM)

    def block(args):
        blk, qb, qib, wb = args
        qpos = blk * Q_BLOCK + jnp.arange(Q_BLOCK)
        causal = key_pos[None, :] <= qpos[:, None]
        logits = jnp.einsum("bthd,bsd->bths", qib, k_idx)
        score = jnp.einsum("bth,bths->bts", wb, jax.nn.relu(logits))
        score = jnp.where(causal[None], score, -jnp.inf)
        _, sel = lax.top_k(score, topk)
        valid = sel <= qpos[None, :, None]
        ks = gather(k, sel)
        vs = gather(v, sel)
        sc = jnp.einsum("btgrd,btjgd->btgrj", qb, ks).astype(jnp.float32) * scale
        sc = jnp.where(valid[:, :, None, None, :], sc, -jnp.inf)
        pr = jax.nn.softmax(sc, axis=-1).astype(vs.dtype)
        return jnp.einsum("btgrj,btjgd->btgrd", pr, vs)

    out = lax.map(block, (jnp.arange(nblk), to_blocks(qg), to_blocks(q_idx), to_blocks(w_idx)))
    return out.swapaxes(0, 1).reshape(bsz, s, ATT_Q_DIM)

def second_inputs(seed: int = 0) -> dict:
    key = jax.random.key(seed)
    ks = jax.random.split(key, 24)
    nrm = jax.random.normal
    f32 = jnp.float32
    dt0 = jnp.exp(jax.random.uniform(ks[14], (DEPTH, SSM_HEADS), dtype=f32)
                  * (np.log(0.1) - np.log(0.001)) + np.log(0.001))
    return {
        "x": nrm(ks[0], (BATCH, SEQ, D_MODEL), f32),
        "c": nrm(ks[1], (BATCH, D_MODEL), f32),
        "positions": jnp.broadcast_to(jnp.arange(SEQ, dtype=jnp.int32)[None, :], (BATCH, SEQ)),
        "ada_w": nrm(ks[2], (DEPTH, D_MODEL, 3 * D_MODEL), f32) * (0.5 * D_MODEL ** -0.5),
        "ada_b": nrm(ks[3], (DEPTH, 3 * D_MODEL), f32) * 0.01,
        "norm_g": 1.0 + 0.1 * nrm(ks[4], (DEPTH, D_MODEL), f32),
        "w_in": nrm(ks[5], (DEPTH, D_MODEL, IN_DIM), f32) * D_MODEL ** -0.5,
        "q_norm_g": 1.0 + 0.1 * nrm(ks[6], (DEPTH, ATT_HEAD_DIM), f32),
        "k_norm_g": 1.0 + 0.1 * nrm(ks[7], (DEPTH, ATT_HEAD_DIM), f32),
        "idx_k_ln_g": 1.0 + 0.1 * nrm(ks[8], (DEPTH, IDX_DIM), f32),
        "idx_k_ln_b": 0.01 * nrm(ks[9], (DEPTH, IDX_DIM), f32),
        "conv_w": nrm(ks[10], (DEPTH, SSM_CONV, SSM_CONV_DIM), f32) * SSM_CONV ** -0.5,
        "conv_b": 0.01 * nrm(ks[11], (DEPTH, SSM_CONV_DIM), f32),
        "dt_bias": dt0 + jnp.log(-jnp.expm1(-dt0)),
        "a_log": jnp.log(jax.random.uniform(ks[12], (DEPTH, SSM_HEADS), f32, 1.0, 16.0)),
        "d_skip": 1.0 + 0.1 * nrm(ks[13], (DEPTH, SSM_HEADS), f32),
        "ssm_norm_g": 1.0 + 0.1 * nrm(ks[15], (DEPTH, SSM_D_INNER), f32),
        "w_branch_att": nrm(ks[16], (DEPTH, ATT_Q_DIM, D_MODEL), f32) * ATT_Q_DIM ** -0.5,
        "w_branch_ssm": nrm(ks[17], (DEPTH, SSM_D_INNER, D_MODEL), f32) * SSM_D_INNER ** -0.5,
        "w_out": nrm(ks[18], (DEPTH, D_MODEL, D_MODEL), f32) * D_MODEL ** -0.5,
    }

def second_block(x, c, positions, ada_w, ada_b, norm_g, w_in, q_norm_g, k_norm_g, idx_k_ln_g, idx_k_ln_b,
              conv_w, conv_b, dt_bias, a_log, d_skip, ssm_norm_g, w_branch_att, w_branch_ssm, w_out):
    f32 = jnp.float32
    bsz, s, _ = x.shape
    cos_a, sin_a = rope_tables(positions, ATT_ROT_DIM)
    cos_i, sin_i = rope_tables(positions, IDX_ROT_DIM)
    pts = _split_points()
    for l in range(DEPTH):
        mod = jax.nn.silu(c) @ ada_w[l] + ada_b[l]
        shift, scale, gate = jnp.split(mod, 3, axis=-1)
        h = rms_norm(x, norm_g[l]) * (1.0 + scale[:, None, :]) + shift[:, None, :]
        proj = h @ w_in[l]
        (q, k, v, z_att, q_idx, k_idx, w_idx, z_ssm, xbc, dt_raw, gate_logits) = jnp.split(proj, pts, axis=-1)

        q = partial_rope(rms_norm(q.reshape(bsz, s, ATT_HEADS, ATT_HEAD_DIM), q_norm_g[l]), cos_a, sin_a)
        k = partial_rope(rms_norm(k.reshape(bsz, s, ATT_KV_HEADS, ATT_HEAD_DIM), k_norm_g[l]), cos_a, sin_a)
        v = v.reshape(bsz, s, ATT_KV_HEADS, ATT_HEAD_DIM)
        q_idx = partial_rope(q_idx.reshape(bsz, s, IDX_HEADS, IDX_DIM), cos_i, sin_i) * (IDX_DIM ** -0.5)
        k_idx = partial_rope(layer_norm(k_idx, idx_k_ln_g[l], idx_k_ln_b[l])[:, :, None, :], cos_i, sin_i)[:, :, 0, :]
        w_idx = w_idx * (IDX_HEADS ** -0.5)
        o_att = sparse_attention(q, k, v, q_idx, k_idx, w_idx) * jax.nn.silu(z_att)
        y_att = o_att @ w_branch_att[l]

        xbc = jax.nn.silu(causal_depthwise_conv(xbc, conv_w[l], conv_b[l]))
        xs, bm, cm = jnp.split(xbc, [SSM_D_INNER, SSM_D_INNER + SSM_GROUPS * SSM_STATE], axis=-1)
        xs = xs.reshape(bsz, s, SSM_HEADS, SSM_HEAD_DIM).astype(f32)
        dt = jax.nn.softplus(dt_raw.astype(f32) + dt_bias[l].astype(f32))
        a = -jnp.exp(a_log[l].astype(f32))
        y = ssd(xs, dt, a,
                bm.reshape(bsz, s, SSM_GROUPS, SSM_STATE).astype(f32),
                cm.reshape(bsz, s, SSM_GROUPS, SSM_STATE).astype(f32))
        y = y + d_skip[l].astype(f32)[:, None] * xs
        y = y.reshape(bsz, s, SSM_D_INNER).astype(x.dtype) * jax.nn.silu(z_ssm)
        y = rms_norm(y.reshape(bsz, s, SSM_GROUPS, SSM_D_INNER // SSM_GROUPS),
                     ssm_norm_g[l].reshape(SSM_GROUPS, SSM_D_INNER // SSM_GROUPS)).reshape(bsz, s, SSM_D_INNER)
        y_ssm = y @ w_branch_ssm[l]

        g_att, g_ssm = jnp.split(gate_logits, 2, axis=-1)
        merged = jax.nn.sigmoid(g_att) * y_att + jax.nn.sigmoid(g_ssm) * y_ssm
        x = x + gate[:, None, :] * (merged @ w_out[l])
    return x


def setup_inputs(seed=0):
    out = dict(first_inputs(seed))
    for name, value in second_inputs(seed + 1).items():
        if name != "x":
            out[name + "_2"] = value
    return out


def reference(
    x, c, ada_w, ada_b, norm_mix_g, norm_ffn_g, final_g, conv_w_in, conv_b_in, conv_w_dw,
    conv_b_dw, conv_ln_g, conv_ln_b, conv_w_out, hgrn_w_in, hgrn_lb_logits, hgrn_norm_g,
    hgrn_w_out, pool_w, pool_b, pool_scale, sb_w_qkv, sb_w_out, moe_w_rg, moe_b_rg, moe_w_re,
    moe_b_re, moe_w_gate, moe_w_up, moe_w_down, c_2, positions_2, ada_w_2, ada_b_2, norm_g_2,
    w_in_2, q_norm_g_2, k_norm_g_2, idx_k_ln_g_2, idx_k_ln_b_2, conv_w_2, conv_b_2, dt_bias_2,
    a_log_2, d_skip_2, ssm_norm_g_2, w_branch_att_2, w_branch_ssm_2, w_out_2,
):
    x = first_block(
        x, c, ada_w, ada_b, norm_mix_g, norm_ffn_g, final_g, conv_w_in, conv_b_in, conv_w_dw,
        conv_b_dw, conv_ln_g, conv_ln_b, conv_w_out, hgrn_w_in, hgrn_lb_logits, hgrn_norm_g,
        hgrn_w_out, pool_w, pool_b, pool_scale, sb_w_qkv, sb_w_out, moe_w_rg, moe_b_rg,
        moe_w_re, moe_b_re, moe_w_gate, moe_w_up, moe_w_down,
    )
    return second_block(
        x, c_2, positions_2, ada_w_2, ada_b_2, norm_g_2, w_in_2, q_norm_g_2, k_norm_g_2,
        idx_k_ln_g_2, idx_k_ln_b_2, conv_w_2, conv_b_2, dt_bias_2, a_log_2, d_skip_2,
        ssm_norm_g_2, w_branch_att_2, w_branch_ssm_2, w_out_2,
    )


_drawn_inputs = setup_inputs


def setup_inputs(seed=0):
    import zlib

    import numpy as np

    out = dict(_drawn_inputs(seed))
    spreads = {}
    factors = {'ada_b': 2.866,
     'norm_mix_g': 4.386,
     'norm_ffn_g': 2.873,
     'conv_b_in': 8.0,
     'conv_b_dw': 7.505,
     'conv_ln_g': 4.34,
     'conv_ln_b': 8.0,
     'moe_b_rg': 8.0,
     'moe_b_re': 8.0,
     'ada_b_2': 8.0,
     'q_norm_g_2': 8.0,
     'k_norm_g_2': 8.0,
     'idx_k_ln_g_2': 8.0,
     'idx_k_ln_b_2': 154.79,
     'conv_b_2': 8.0,
     'd_skip_2': 5.383,
     'ssm_norm_g_2': 3.398}
    for name, (base, spread) in spreads.items():
        noise = np.random.default_rng([zlib.crc32(name.encode()), seed]).standard_normal(out[name].shape)
        drawn = base * np.exp(spread * noise) if base else spread * noise
        out[name] = jnp.asarray(drawn.astype(out[name].dtype))
    for name, factor in factors.items():
        out[name] = (out[name] * factor).astype(out[name].dtype)
    return out
```

```python
import numpy as np
from contextlib import ExitStack

import concourse.bass as bass
from concourse import mybir

F32 = mybir.dt.float32
I32 = mybir.dt.int32
U32 = mybir.dt.uint32
BF16 = mybir.dt.bfloat16
ALU = mybir.AluOpType
ACT = mybir.ActivationFunctionType
AX = mybir.AxisListType

P = 128
D = 1024
S = 1024
KC = D // P
TT = S // P
HALF = 512
EPS = 1e-6
CONV = 31
GROUPS, PER_GROUP = 4, 8
EXPERTS = GROUPS * PER_GROUP
FFN = D // 2
SLOT_BLOCKS = 2 * S // P + EXPERTS
HEADS, KV_HEADS, HD = 8, 2, 128
IDX_HEADS, IDX_DIM = 4, 64
TOPK = 256
SSM_INNER, SSM_HEADS, SSM_HD, SSM_GROUPS, SSM_N, SSM_CONV = 2048, 32, 64, 4, 128, 4
HPG = SSM_HEADS // SSM_GROUPS
GW = HPG * SSM_HD
BIG = 1.0e30

PV_FIELDS = [
    ("ada_b", 48), ("norm_mix_g", 8), ("norm_ffn_g", 8), ("conv_b_in", 16), ("conv_w_dw", 8 * CONV),
    ("conv_b_dw", 8), ("conv_ln_g", 8), ("conv_ln_b", 8), ("ada_b_2", 24), ("norm_g_2", 8),
    ("conv_w_2", 24 * SSM_CONV), ("conv_b_2", 24), ("ssm_norm_g_2", 16), ("c", 8), ("c_2", 8),
]
PV_AT, PV_N = {}, 0
for _name, _n in PV_FIELDS:
    PV_AT[_name] = PV_N
    PV_N += _n

CONSTS = ["ident", "upto", "before", "after", "ones", "mean_d"]


def constant_tables():
    k, m = np.arange(P)[:, None], np.arange(P)[None, :]
    c = {
        "ident": k == m, "upto": k <= m, "before": k < m, "after": k > m,
        "ones": np.ones((P, P)), "mean_d": np.full((P, P), 1.0 / D),
    }
    table = np.stack([np.asarray(c[n], np.float32) for n in CONSTS], axis=1)
    freq = [np.power(500000.0, -(2.0 * np.arange(n // 2) / n)) for n in (HD // 4, IDX_DIM // 4)]
    return np.ascontiguousarray(table), np.concatenate(freq).astype(np.float32)


def row_constants():
    return np.concatenate([np.arange(GROUPS, 0, -1), np.arange(EXPERTS, 0, -1), np.arange(SLOT_BLOCKS)]) \
        .astype(np.float32)


def zero_fill(k, eng, zeros, done):
    first, parts = 2 * S // P, 4
    n = (SLOT_BLOCKS - first) // parts
    for i in range(parts):
        a = (first + i * n) * P
        eng.dma_start(k.slot_out[a:a + n * P, :].rearrange("(b p) d -> p b d", p=P),
                      zeros.unsqueeze(1).to_broadcast([P, n, D])).then_inc(done, 16)
    return 16 * parts


class Core:

    def __init__(self, nc, ctx, ins):
        self.nc, self.ctx, self.ins, self.sems = nc, ctx, ins, []

    def sb(self, name, shape, dtype=F32, ctx=None):
        return (ctx or self.ctx).enter_context(self.nc.sbuf_tensor(name, shape, dtype))

    def ps(self, name, shape, dtype=F32, ctx=None):
        return (ctx or self.ctx).enter_context(self.nc.psum_tensor(name, shape, dtype))

    def sem(self, name):
        self.sems.append(self.nc.alloc_semaphore(name))
        return self.sems[-1]

    def clear_semaphores(self):
        self.nc.clear_and_free_semaphores(self.sems)
        self.nc.all_engine_barrier()
        self.sems = []

    def const(self, name):
        return self.consts[:, CONSTS.index(name), :]

    def pv(self, name, i=0, n=1):
        at = PV_AT[name] + i
        return self.params[:, at:at + n]


def chain(eng, sem):
    count = [0]

    def step(ins):
        count[0] += 1
        ins.then_inc(sem, 1)
        eng.wait_ge(sem, count[0])

    return step


def modulation_stage(k):
    nc, ins = k.nc, k.ins
    chunk = HALF
    n1, n2 = 6 * D // chunk, 3 * D // chunk
    slots = 4
    with ExitStack() as ctx:
        ring = k.sb("ada_ring", [P, slots, KC, chunk], ctx=ctx)
        csilu = k.sb("csilu", [P, 2, KC], ctx=ctx)
        parts, mod_mm = k.sb("mod_parts", [P, 2, chunk], ctx=ctx), k.sem("mod_mm")
        mod_ps = k.ps("mod_ps", [P, 72], ctx=ctx)
        tables_in, x_in = k.sem("tables_in"), k.sem("x_in")
        ada_in = [k.sem(f"ada_in{i}") for i in range(slots)]
        ada_used, c_ready, mod_done = k.sem("ada_used"), k.sem("c_ready"), k.sem("mod_done")
        dve_step = k.sem("mod_dve_step")
        block = ctx.enter_context(nc.Block())

        @block.sync
        def _(sp):
            for j in range(n1 + n2):
                if j >= slots:
                    sp.wait_ge(ada_used, j - slots + 1)
                src = ins["ada_w"][:, j * chunk:(j + 1) * chunk] if j < n1 else \
                    ins["ada_w_2"][:, (j - n1) * chunk:(j - n1 + 1) * chunk]
                sp.dma_start(ring[:, j % slots], src.rearrange("(c p) n -> p c n", p=P)) \
                    .then_inc(ada_in[j % slots], 16)

        @block.scalar
        def _(act):
            act.dma_start(k.params[:, :], ins["params"]).then_inc(tables_in, 16)
            act.dma_start(k.consts[:, :, :], ins["consts"]).then_inc(tables_in, 16)
            act.dma_start(k.x_tok[:, :, :], ins["x"].rearrange("(t p) d -> p t d", p=P)).then_inc(x_in, 16)
            act.wait_ge(tables_in, 32)
            nc.scalar.activation(csilu[:, 0, :], k.pv("c", 0, KC), ACT.Silu)
            nc.scalar.activation(csilu[:, 1, :], k.pv("c_2", 0, KC), ACT.Silu).then_inc(c_ready, 1)

        @block.vector
        def _(dve):
            step = chain(dve, dve_step)
            dve.wait_ge(c_ready, 1)
            for j in range(n1 + n2):
                dve.wait_ge(ada_in[j % slots], 16 * (j // slots + 1))
                if j >= 2:
                    dve.wait_ge(mod_mm, j - 1)
                for c in range(KC):
                    src, scale = ring[:, j % slots, c, :], csilu[:, int(j >= n1), c:c + 1]
                    part = parts[:, j % 2, :]
                    if c == 0:
                        last = nc.vector.tensor_scalar(part, src, scale, None, ALU.mult)
                    else:
                        last = nc.vector.scalar_tensor_tensor(part, in0=src, scalar=scale, in1=part,
                                                              op0=ALU.mult, op1=ALU.add)
                    if c < KC - 1:
                        step(last)
                last.then_inc(ada_used, 1)
            dve.wait_ge(tables_in, 32)
            dve.wait_ge(x_in, 16)
            dve.wait_ge(mod_mm, n1 + n2)
            nc.vector.tensor_tensor(k.mod[:, 0:48], mod_ps[:, 0:48], k.pv("ada_b", 0, 48), ALU.add)
            step(nc.vector.tensor_tensor(k.mod[:, 48:72], mod_ps[:, 48:72], k.pv("ada_b_2", 0, 24), ALU.add))
            for n, (scale_at, gain) in enumerate(((8, "norm_mix_g"), (32, "norm_ffn_g"), (56, "norm_g_2"))):
                nc.vector.scalar_tensor_tensor(
                    k.gain[:, n * KC:(n + 1) * KC], in0=k.mod[:, scale_at:scale_at + KC], scalar=1.0,
                    in1=k.pv(gain, 0, KC), op0=ALU.add, op1=ALU.mult).then_inc(mod_done, 1)
            dve.wait_ge(mod_done, 3)

        @block.tensor
        def _(pe):
            pe.wait_ge(tables_in, 32)
            for j in range(n1 + n2):
                pe.wait_ge(ada_used, j + 1)
                for m in range(chunk // P):
                    col = j * (chunk // P) + m
                    last = nc.tensor.matmul(mod_ps[:, col:col + 1], lhsT=parts[:, j % 2, m * P:(m + 1) * P],
                                            rhs=k.const("ones")[:, 0:1], start=True, stop=True)
                last.then_inc(mod_mm, 1)


def norm_transpose_stage(k, name, src, gain, shift, dst, normed_dram=None, raw_dram=None):
    nc = k.nc
    with ExitStack() as ctx:
        normed = k.sb(f"{name}_normed", [P, TT, D], ctx=ctx)
        ss = k.sb(f"{name}_ss", [P, TT], ctx=ctx)
        banks = [k.ps(f"{name}_t{i}", [P, HALF], ctx=ctx) for i in range(4)]
        squared, var_ready, std_ready = k.sem(f"{name}_squared"), k.sem(f"{name}_var"), k.sem(f"{name}_std")
        normed_ready, transposed = k.sem(f"{name}_normed_ready"), k.sem(f"{name}_transposed")
        out_act, out_dve = k.sem(f"{name}_out_act"), k.sem(f"{name}_out_dve")
        dve_step, stored = k.sem(f"{name}_dve_step"), k.sem(f"{name}_stored")
        block = ctx.enter_context(nc.Block())
        groups = KC * 2

        @block.scalar
        def _(act):
            for t in range(TT):
                nc.scalar.activation(normed[:, t, :], src[:, t, :], ACT.Square,
                                     accum_out=ss[:, t:t + 1]).then_inc(squared, 1)
            act.wait_ge(var_ready, 1)
            nc.scalar.activation(ss[:, :], ss[:, :], ACT.Sqrt).then_inc(std_ready, 1)
            for g in range(0, groups, 2):
                act.wait_ge(transposed, g + 1)
                c, h = g // 2, g % 2
                nc.scalar.activation(dst[:, c, h * HALF:(h + 1) * HALF], banks[g % 4][:, :], ACT.Identity,
                                     bias=shift[:, c:c + 1], scale=gain[:, c:c + 1]).then_inc(out_act, 1)

        @block.vector
        def _(dve):
            step = chain(dve, dve_step)
            dve.wait_ge(squared, TT)
            nc.vector.tensor_scalar(ss[:, :], ss[:, :], 1.0 / D, EPS, ALU.mult, ALU.add).then_inc(var_ready, 1)
            dve.wait_ge(std_ready, 1)
            step(nc.vector.reciprocal(ss[:, :], ss[:, :]))
            for t in range(TT):
                nc.vector.tensor_scalar(normed[:, t, :], src[:, t, :], ss[:, t:t + 1], None,
                                        ALU.mult).then_inc(normed_ready, 1)
            for g in range(1, groups, 2):
                dve.wait_ge(transposed, g + 1)
                c, h = g // 2, g % 2
                nc.vector.tensor_scalar(dst[:, c, h * HALF:(h + 1) * HALF], banks[g % 4][:, :],
                                        gain[:, c:c + 1], shift[:, c:c + 1], ALU.mult, ALU.add) \
                    .then_inc(out_dve, 1)

        @block.tensor
        def _(pe):
            for g in range(groups):
                c, h = g // 2, g % 2
                if g >= 4:
                    pe.wait_ge((out_act, out_dve)[g % 2], (g - 4) // 2 + 1)
                for t in range(4):
                    if g < 2:
                        pe.wait_ge(normed_ready, 4 * h + t + 1)
                    last = nc.tensor.transpose(banks[g % 4][:, t * P:(t + 1) * P],
                                               normed[:, 4 * h + t, c * P:(c + 1) * P], k.const("ident"))
                last.then_inc(transposed, 1)

        if normed_dram is not None:
            @block.sync
            def _(sp):
                for t in range(TT):
                    sp.wait_ge(normed_ready, t + 1)
                    sp.dma_start(normed_dram[t * P:(t + 1) * P, :], normed[:, t, :]).then_inc(stored, 16)
                sp.wait_ge(stored, 16 * TT)

        if raw_dram is not None:
            @block.sync
            def _(sp):
                sp.dma_start(raw_dram.rearrange("(t p) d -> p t d", p=P), src[:, :, :]).then_inc(stored, 16)
                sp.wait_ge(stored, 16)


def conv_stage(k):
    nc, ins = k.nc, k.ins
    pad = CONV - 1
    with ExitStack() as ctx:
        w = k.sb("cw", [P, 2, 2, KC, P], ctx=ctx)
        u = k.sb("cu", [P, 2, pad + S], ctx=ctx)
        sig = k.sb("csig", [P, 2, S], ctx=ctx)
        part = k.sb("cpart", [P, S], ctx=ctx)
        tap = k.sb("ctap", [P, 2, S], ctx=ctx)
        acc = [[k.ps(f"c{n}{i}", [P, S], ctx=ctx) for i in range(2)] for n in "ag"]
        w_in = [k.sem(f"cw_in{i}") for i in range(2)]
        mm_done, sig_done, u_done, conv_done = k.sem("c_mm"), k.sem("c_sig"), k.sem("c_u"), k.sem("c_conv")
        pads, tap_done, tap_added, dve_step = k.sem("c_pads"), k.sem("c_tap"), k.sem("c_tap_added"), k.sem("c_dve")
        zeros, zero_sb, zeroed = k.sb("c_zeros", [P, D], ctx=ctx), k.sem("c_zero_sb"), k.sem("c_zeroed")
        pool_taps = 9
        block = ctx.enter_context(nc.Block())

        @block.sync
        def _(sp):
            for i in range(KC):
                if i >= 2:
                    sp.wait_ge(mm_done, i - 1)
                for n in range(2):
                    sp.dma_start(w[:, i % 2, n], ins["conv_w_in"][n * KC + i]).then_inc(w_in[i % 2], 16)
            sp.wait_ge(zero_sb, 1)
            sp.wait_ge(zeroed, zero_fill(k, sp, zeros[:, :], zeroed))

        @block.tensor
        def _(pe):
            for i in range(KC):
                pe.wait_ge(w_in[i % 2], 32 * (i // 2 + 1))
                if i >= 2:
                    pe.wait_ge(u_done, i - 1)
                for n in (1, 0):
                    for h in range(2):
                        for c in range(KC):
                            last = nc.tensor.matmul(acc[n][i % 2][:, h * HALF:(h + 1) * HALF],
                                                    lhsT=w[:, i % 2, n, c, :],
                                                    rhs=k.hT[:, c, h * HALF:(h + 1) * HALF],
                                                    start=c == 0, stop=c == KC - 1)
                last.then_inc(mm_done, 1)

        @block.scalar
        def _(act):
            for i in range(KC):
                act.wait_ge(mm_done, i + 1)
                if i >= 2:
                    act.wait_ge(u_done, i - 1)
                nc.scalar.activation(sig[:, i % 2], acc[1][i % 2][:, :], ACT.Sigmoid,
                                     bias=k.pv("conv_b_in", KC + i)).then_inc(sig_done, 1)
                act.wait_ge(u_done, i + 1)
                for j in range(pool_taps):
                    n = i * pool_taps + j
                    if n >= 2:
                        act.wait_ge(tap_added, n - 1)
                    nc.scalar.activation(tap[:, n % 2], u[:, i % 2, j:j + S], ACT.Copy,
                                         scale=k.pv("conv_w_dw", i * CONV + j)).then_inc(tap_done, 1)

        @block.gpsimd
        def _(pool):
            nc.gpsimd.memset(zeros[:, :], 0.0).then_inc(zero_sb, 1)
            for i in range(KC):
                for j in range(pool_taps):
                    n = i * pool_taps + j
                    pool.wait_ge(tap_done, n + 1)
                    if j == 0:
                        if i:
                            pool.wait_ge(conv_done, i)
                        nc.gpsimd.tensor_copy(part[:, :], tap[:, n % 2]).then_inc(tap_added, 1)
                    else:
                        pool.wait_ge(tap_added, n)
                        nc.gpsimd.tensor_tensor(part[:, :], part[:, :], tap[:, n % 2], ALU.add) \
                            .then_inc(tap_added, 1)

        @block.vector
        def _(dve):
            step = chain(dve, dve_step)
            for i in range(2):
                nc.vector.memset(u[:, i, 0:pad], 0.0).then_inc(pads, 1)
            dve.wait_ge(pads, 2)
            for i in range(KC):
                dve.wait_ge(sig_done, i + 1)
                if i >= 2:
                    dve.wait_ge(tap_done, (i - 1) * pool_taps)
                nc.vector.scalar_tensor_tensor(
                    u[:, i % 2, pad:pad + S], in0=acc[0][i % 2][:, :], scalar=k.pv("conv_b_in", i),
                    in1=sig[:, i % 2], op0=ALU.add, op1=ALU.mult).then_inc(u_done, 1)
                dve.wait_ge(u_done, i + 1)
                y = k.y[:, i, :]
                j = pool_taps
                step(nc.vector.tensor_scalar(y, u[:, i % 2, j:j + S], k.pv("conv_w_dw", i * CONV + j),
                                             k.pv("conv_b_dw", i), ALU.mult, ALU.add))
                for j in range(pool_taps + 1, CONV):
                    step(nc.vector.scalar_tensor_tensor(
                        y, in0=u[:, i % 2, j:j + S], scalar=k.pv("conv_w_dw", i * CONV + j), in1=y,
                        op0=ALU.mult, op1=ALU.add))
                dve.wait_ge(tap_added, (i + 1) * pool_taps)
                nc.vector.tensor_tensor(y, y, part[:, :], ALU.add).then_inc(conv_done, 1)


def conv_norm_stage(k):
    nc = k.nc
    with ExitStack() as ctx:
        sq = k.sb("ln_sq", [P, 2, S], ctx=ctx)
        rstd = k.sb("ln_rstd", [P, S], ctx=ctx)
        mean_ps, var_ps = k.ps("ln_mean", [P, S], ctx=ctx), k.ps("ln_var", [P, S], ctx=ctx)
        mean_done, centred, squared, sq_used = (k.sem(n) for n in ("ln_mean_done", "ln_centred", "ln_squared", "ln_sq_used"))
        var_sb, std_done, scaled, dve_step = (k.sem(n) for n in ("ln_var_sb", "ln_std", "ln_scaled", "ln_dve"))
        block = ctx.enter_context(nc.Block())

        @block.tensor
        def _(pe):
            for h in range(2):
                for c in range(KC):
                    last = nc.tensor.matmul(mean_ps[:, h * HALF:(h + 1) * HALF], lhsT=k.const("mean_d"),
                                            rhs=k.y[:, c, h * HALF:(h + 1) * HALF],
                                            start=c == 0, stop=c == KC - 1)
            last.then_inc(mean_done, 1)
            for c in range(KC):
                pe.wait_ge(squared, c + 1)
                for h in range(2):
                    last = nc.tensor.matmul(var_ps[:, h * HALF:(h + 1) * HALF], lhsT=k.const("mean_d"),
                                            rhs=sq[:, c % 2, h * HALF:(h + 1) * HALF],
                                            start=c == 0, stop=c == KC - 1)
                last.then_inc(sq_used, 1)

        @block.vector
        def _(dve):
            step = chain(dve, dve_step)
            dve.wait_ge(mean_done, 1)
            for c in range(KC):
                nc.vector.tensor_tensor(k.y[:, c, :], k.y[:, c, :], mean_ps[:, :], ALU.subtract).then_inc(centred, 1)
            dve.wait_ge(sq_used, KC)
            nc.vector.tensor_scalar(rstd[:, :], var_ps[:, :], EPS, None, ALU.add).then_inc(var_sb, 1)
            dve.wait_ge(std_done, 1)
            step(nc.vector.reciprocal(rstd[:, :], rstd[:, :]))
            for c in range(KC):
                dve.wait_ge(centred, c + 1)
                nc.vector.tensor_tensor(k.y[:, c, :], k.y[:, c, :], rstd[:, :], ALU.mult).then_inc(scaled, 1)

        @block.scalar
        def _(act):
            for c in range(KC):
                act.wait_ge(centred, c + 1)
                if c >= 2:
                    act.wait_ge(sq_used, c - 1)
                nc.scalar.activation(sq[:, c % 2], k.y[:, c, :], ACT.Square).then_inc(squared, 1)
            act.wait_ge(var_sb, 1)
            nc.scalar.activation(rstd[:, :], rstd[:, :], ACT.Sqrt).then_inc(std_done, 1)
            for c in range(KC):
                act.wait_ge(scaled, c + 1)
                nc.scalar.activation(k.y[:, c, :], k.y[:, c, :], ACT.Silu, bias=k.pv("conv_ln_b", c),
                                     scale=k.pv("conv_ln_g", c))


def token_projection_stage(k, name, actT, weight_dram, gate_cols, out_dram=None, x_from=None):
    nc = k.nc
    with ExitStack() as ctx:
        w = k.sb(f"{name}_w", [P, KC, D], ctx=ctx)
        gate = k.sb(f"{name}_gate", [P, D], ctx=ctx)
        gated = k.sb(f"{name}_gated", [P, 2, D], ctx=ctx)
        gate_ps = k.ps(f"{name}_gate_ps", [P, D], ctx=ctx)
        acc = [k.ps(f"{name}_ps{i}", [P, D], ctx=ctx) for i in range(3)]
        w_in, gate_mm, gate_sb = (k.sem(f"{name}_{n}") for n in ("w_in", "gate_mm", "gate_sb"))
        mm_done, gated_done, added, stored = (k.sem(f"{name}_{n}") for n in ("mm", "gated_done", "added", "stored"))
        x_in = k.sem(f"{name}_x_in")
        block = ctx.enter_context(nc.Block())

        @block.sync
        def _(sp):
            if x_from is not None:
                sp.dma_start(k.x_tok[:, :, :], x_from.rearrange("(t p) d -> p t d", p=P)).then_inc(x_in, 16)
            for c in range(KC):
                sp.dma_start(w[:, c, :], weight_dram[c * P:(c + 1) * P, :]).then_inc(w_in, 16)
            if out_dram is not None:
                for t in range(TT):
                    sp.wait_ge(added, t + 1)
                    sp.dma_start(out_dram[t * P:(t + 1) * P, :], k.x_tok[:, t, :]).then_inc(stored, 16)
                sp.wait_ge(stored, 16 * TT)

        @block.tensor
        def _(pe):
            for c in range(KC):
                last = nc.tensor.matmul(gate_ps[:, c * P:(c + 1) * P],
                                        lhsT=gate_cols[:, c:c + 1].to_broadcast([P, P]),
                                        rhs=k.const("ident"), start=True, stop=True)
            last.then_inc(gate_mm, 1)
            pe.wait_ge(w_in, 16 * KC)
            for t in range(TT):
                if t >= 3:
                    pe.wait_ge(gated_done, t - 2)
                for h in range(2):
                    for c in range(KC):
                        last = nc.tensor.matmul(acc[t % 3][:, h * HALF:(h + 1) * HALF],
                                                lhsT=actT[:, c, t * P:(t + 1) * P],
                                                rhs=w[:, c, h * HALF:(h + 1) * HALF],
                                                start=c == 0, stop=c == KC - 1)
                last.then_inc(mm_done, 1)

        @block.scalar
        def _(act):
            act.wait_ge(gate_mm, 1)
            nc.scalar.copy(gate[:, :], gate_ps[:, :]).then_inc(gate_sb, 1)

        @block.vector
        def _(dve):
            dve.wait_ge(gate_sb, 1)
            for t in range(TT):
                dve.wait_ge(mm_done, t + 1)
                if t >= 2:
                    dve.wait_ge(added, t - 1)
                nc.vector.tensor_tensor(gated[:, t % 2], acc[t % 3][:, :], gate[:, :], ALU.mult) \
                    .then_inc(gated_done, 1)

        @block.gpsimd
        def _(pool):
            if x_from is not None:
                pool.wait_ge(x_in, 16)
            for t in range(TT):
                pool.wait_ge(gated_done, t + 1)
                nc.gpsimd.tensor_tensor(k.x_tok[:, t, :], k.x_tok[:, t, :], gated[:, t % 2], ALU.add) \
                    .then_inc(added, 1)


def router_stage(k):
    nc, ins = k.nc, k.ins
    NL = GROUPS + EXPERTS
    with ExitStack() as ctx:
        sb = lambda n, s, d=F32: k.sb(f"r_{n}", s, d, ctx=ctx)
        wr, br, rows = sb("w", [P, KC, NL]), sb("b", [P, NL]), sb("rows", [P, NL + SLOT_BLOCKS])
        tokid, zeros = sb("tokid", [P, TT]), sb("zeros", [SLOT_BLOCKS, P])
        lg, el, tmp = sb("lg", [P, TT, NL]), sb("el", [P, TT, EXPERTS]), sb("tmp", [P, TT, EXPERTS])
        oh1, oh2, mask = sb("oh1", [P, TT, EXPERTS]), sb("oh2", [P, TT, EXPERTS]), sb("mask", [P, TT, EXPERTS])
        goh, gex = sb("goh", [P, TT, GROUPS]), sb("gex", [P, TT, GROUPS])
        c1, m1, m2, e2, gp = (sb(n, [P, TT]) for n in ("c1", "m1", "m2", "e2", "gp"))
        cnt, nb, cum, start, one = (sb(n, [P, EXPERTS]) for n in ("cnt", "nb", "cum", "start", "one"))
        dfull = sb("dfull", [P, TT, EXPERTS])
        dest_f = sb("dest_f", [P, 2, TT])
        le = sb("le", [P, SLOT_BLOCKS, EXPERTS])
        bef, pr = sb("bef", [P, SLOT_BLOCKS]), sb("pr", [P, SLOT_BLOCKS // 2])
        prs = sb("prs", [P, 1])
        table = sb("table", [SLOT_BLOCKS, P])
        lg_ps = k.ps("r_lg_ps", [P, TT, 64], ctx=ctx)
        pos_ps = k.ps("r_pos_ps", [P, TT, EXPERTS], ctx=ctx)
        cnt_ps = k.ps("r_cnt_ps", [P, EXPERTS], ctx=ctx)
        tab_ps = k.ps("r_tab_ps", [P, SLOT_BLOCKS], ctx=ctx)
        r_in, lg_done, ex_in, ex_done, e2_in, e2_done = (k.sem(f"r_{n}") for n in (
            "in", "lg_done", "ex_in", "ex_done", "e2_in", "e2_done"))
        mask_ready, pos_done, dest_ready, zero_sb, zeroed, scattered, tab_in, tab_done, dve_step = (
            k.sem(f"r_{n}") for n in ("mask_ready", "pos_done", "dest_ready", "zero_sb", "zeroed", "scattered",
                                      "tab_in", "tab_done", "dve_step"))
        desc_g, desc_e = rows[:, 0:GROUPS], rows[:, GROUPS:NL]
        viota = rows[:, NL:NL + SLOT_BLOCKS]
        block = ctx.enter_context(nc.Block())

        @block.sync
        def _(sp):
            sp.dma_start(wr[:, :, :], ins["router_w"].rearrange("(c p) n -> p c n", p=P)).then_inc(r_in, 16)
            sp.dma_start(br[:, :], ins["router_b"].partition_broadcast(P)).then_inc(r_in, 16)
            sp.dma_start(rows[:, :], ins["rows"].partition_broadcast(P)).then_inc(r_in, 16)
            sp.dma_start(tokid[:, :], ins["token_ids"]).then_inc(r_in, 16)
            sp.wait_ge(zero_sb, 1)
            sp.dma_start(k.table_dram.rearrange("(b p) o -> b (p o)", p=P), zeros[:, :]).then_inc(zeroed, 16)
            sp.wait_ge(scattered, 16 * 2 * TT)
            sp.dma_start(table[:, :], k.table_dram.rearrange("(b p) o -> b (p o)", p=P)).then_inc(tab_in, 16)

        @block.tensor
        def _(pe):
            pe.wait_ge(r_in, 64)
            for t in range(TT):
                for c in range(KC):
                    last = nc.tensor.matmul(lg_ps[:, t, 0:NL], lhsT=k.hT[:, c, t * P:(t + 1) * P],
                                            rhs=wr[:, c, :], start=c == 0, stop=c == KC - 1)
            last.then_inc(lg_done, 1)
            pe.wait_ge(mask_ready, 1)
            for t in range(TT):
                for j in range(t):
                    nc.tensor.matmul(pos_ps[:, t, :], lhsT=k.const("ones"), rhs=mask[:, j, :],
                                     start=j == 0, stop=False)
                nc.tensor.matmul(pos_ps[:, t, :], lhsT=k.const("before"), rhs=mask[:, t, :],
                                 start=t == 0, stop=True)
            for j in range(TT):
                last = nc.tensor.matmul(cnt_ps[:, :], lhsT=k.const("ones"), rhs=mask[:, j, :],
                                        start=j == 0, stop=j == TT - 1)
            last.then_inc(pos_done, 1)
            pe.wait_ge(tab_in, 16)
            nc.tensor.transpose(tab_ps[:, :], table[:, :], k.const("ident")[0:SLOT_BLOCKS, 0:SLOT_BLOCKS]) \
                .then_inc(tab_done, 1)

        @block.scalar
        def _(act):
            act.wait_ge(ex_in, 1)
            nc.scalar.activation(gex[:, :, :], gex[:, :, :], ACT.Exp).then_inc(ex_done, 1)
            act.wait_ge(e2_in, 1)
            nc.scalar.activation(e2[:, :], e2[:, :], ACT.Exp).then_inc(e2_done, 1)

        @block.vector
        def _(dve):
            step = chain(dve, dve_step)
            v = nc.vector

            def bc(x, n):
                return x.unsqueeze(len(x.shape)).to_broadcast([*x.shape, n])

            def first_max(scores, desc, n, top, onehot):
                step(v.tensor_reduce(top[:, :], scores, AX.X, ALU.max))
                step(v.tensor_tensor(onehot, scores, bc(top[:, :], n), ALU.is_equal))
                step(v.tensor_tensor(onehot, onehot, desc.unsqueeze(1).to_broadcast([P, TT, n]), ALU.mult))
                step(v.tensor_reduce(c1[:, :], onehot, AX.X, ALU.max))
                step(v.tensor_tensor(onehot, onehot, bc(c1[:, :], n), ALU.is_equal))

            step(v.memset(one[:, :], 1.0))
            v.memset(zeros[:, :], 0.0).then_inc(zero_sb, 1)
            dve.wait_ge(r_in, 64)
            dve.wait_ge(lg_done, 1)
            step(v.tensor_tensor(lg[:, :, :], lg_ps[:, :, 0:NL], br[:, :].unsqueeze(1).to_broadcast([P, TT, NL]),
                                 ALU.add))
            gl = lg[:, :, 0:GROUPS]
            first_max(gl, desc_g, GROUPS, m1, goh[:, :, :])
            v.tensor_tensor(gex[:, :, :], gl, bc(m1[:, :], GROUPS), ALU.subtract).then_inc(ex_in, 1)
            step(v.tensor_scalar(goh[:, :, :], goh[:, :, :], BIG, -BIG, ALU.mult, ALU.add))
            step(v.tensor_tensor(el[:, :, :].rearrange("p t (g e) -> p t g e", g=GROUPS),
                                 lg[:, :, GROUPS:NL].rearrange("p t (g e) -> p t g e", g=GROUPS),
                                 bc(goh[:, :, :], PER_GROUP), ALU.add))
            dve.wait_ge(ex_done, 1)
            step(v.tensor_reduce(gp[:, :], gex[:, :, :], AX.X, ALU.add))
            step(v.reciprocal(gp[:, :], gp[:, :]))
            first_max(el[:, :, :], desc_e, EXPERTS, m1, oh1[:, :, :])
            step(v.scalar_tensor_tensor(el[:, :, :], in0=oh1[:, :, :], scalar=-2 * BIG, in1=el[:, :, :],
                                        op0=ALU.mult, op1=ALU.add))
            first_max(el[:, :, :], desc_e, EXPERTS, m2, oh2[:, :, :])
            v.tensor_tensor(e2[:, :], m2[:, :], m1[:, :], ALU.subtract).then_inc(e2_in, 1)
            v.tensor_tensor(mask[:, :, :], oh1[:, :, :], oh2[:, :, :], ALU.add).then_inc(mask_ready, 1)
            dve.wait_ge(e2_done, 1)
            step(v.tensor_scalar(m1[:, :], e2[:, :], 1.0, None, ALU.add))
            step(v.reciprocal(m1[:, :], m1[:, :]))
            step(v.tensor_tensor(k.gates[:, 0, :], gp[:, :], m1[:, :], ALU.mult))
            step(v.tensor_tensor(k.gates[:, 1, :], k.gates[:, 0, :], e2[:, :], ALU.mult))
            dve.wait_ge(pos_done, 1)
            step(v.tensor_copy(cnt[:, :], cnt_ps[:, :]))
            step(v.tensor_scalar(nb[:, :], cnt[:, :], 0.0, None, ALU.is_gt))
            for m in range(1, S // P):
                step(v.scalar_tensor_tensor(nb[:, :], in0=cnt[:, :], scalar=float(m * P), in1=nb[:, :],
                                            op0=ALU.is_gt, op1=ALU.add))
            step(v.tensor_tensor_scan(cum[:, :], one[:, :], nb[:, :], 0.0, ALU.mult, ALU.add))
            step(v.tensor_tensor(start[:, :], cum[:, :], nb[:, :], ALU.subtract))
            step(v.tensor_scalar(start[:, :], start[:, :], float(P), None, ALU.mult))
            step(v.tensor_tensor(dfull[:, :, :], pos_ps[:, :, :],
                                 start[:, :].unsqueeze(1).to_broadcast([P, TT, EXPERTS]), ALU.add))
            for n, oh in enumerate((oh1, oh2)):
                step(v.tensor_tensor(tmp[:, :, :], oh[:, :, :], dfull[:, :, :], ALU.mult))
                step(v.tensor_reduce(dest_f[:, n, :], tmp[:, :, :], AX.X, ALU.add))
            v.tensor_copy(k.dest[:, :, :], dest_f[:, :, :]).then_inc(dest_ready, 1)
            step(v.tensor_tensor(le[:, :, :], cum[:, :].unsqueeze(1).to_broadcast([P, SLOT_BLOCKS, EXPERTS]),
                                 bc(viota, EXPERTS), ALU.is_le))
            step(v.tensor_reduce(bef[:, :], le[:, :, :], AX.X, ALU.add))
            step(v.tensor_scalar(bef[:, :], bef[:, :], float(EXPERTS - 1), None, ALU.min))
            step(v.tensor_copy(k.block_expert[:, :], bef[:, :]))
            step(v.tensor_scalar(pr[:, :], viota[:, 0:SLOT_BLOCKS // 2], 2.0, cum[:, EXPERTS - 1:EXPERTS],
                                 ALU.mult, ALU.is_lt))
            step(v.tensor_reduce(prs[:, :], pr[:, :], AX.X, ALU.add))
            step(v.tensor_scalar(prs[:, :], prs[:, :], -3.0, None, ALU.add))
            step(v.tensor_copy(k.pairs[:, :], prs[:, :]))
            dve.wait_ge(tab_done, 1)
            step(v.tensor_copy(k.slot_token[:, :], tab_ps[:, :]))

        @block.gpsimd
        def _(pool):
            pool.wait_ge(dest_ready, 1)
            pool.wait_ge(r_in, 64)
            pool.wait_ge(zeroed, 16)
            for n in range(2):
                for t in range(TT):
                    nc.gpsimd.indirect_dma_start(
                        out=k.table_dram, out_offset=bass.IndirectOffsetOnAxis(ap=k.dest[:, n, t:t + 1], axis=0),
                        in_=tokid[:, t:t + 1], in_offset=None).then_inc(scattered, 16)


def experts_stage(k):
    nc, ins = k.nc, k.ins
    gain, shift = k.gain[:, KC:2 * KC], k.mod[:, 3 * KC:4 * KC]
    FC = FFN // P
    least = 2 * S // P // 2
    with ExitStack() as ctx:
        sb = lambda n, s, d=F32: k.sb(f"m_{n}", s, d, ctx=ctx)
        wg, wu = sb("wg", [P, 2, KC, FFN]), sb("wu", [P, 2, KC, FFN])
        wd = sb("wd", [P, 2, FC, D])
        idx = sb("idx", [P, 2], U32)
        xg, xT = sb("xg", [P, 2, D]), sb("xT", [P, 2, KC, P])
        sg, hid, hidT, y = sb("sg", [P, FFN]), sb("hid", [P, FFN]), sb("hidT", [P, FC, P]), sb("y", [P, 2, D])
        xt_ps = [k.ps(f"m_xt{i}", [P, HALF], ctx=ctx) for i in range(2)]
        g_ps, u_ps, ht_ps = (k.ps(f"m_{n}_ps", [P, FFN], ctx=ctx) for n in ("g", "u", "ht"))
        y_ps = k.ps("m_y_ps", [P, D], ctx=ctx)
        two = lambda n: [k.sem(f"m_{n}{b}") for b in range(2)]
        g_in, u_in, d_in, x_in, y_stored = (two(n) for n in ("g_in", "u_in", "d_in", "x_in", "y_stored"))
        turn = k.sem("m_turn")
        idx_ready, xt_done, xt_sb, g_done, u_done, sg_done, hid_done, ht_done, ht_sb, y_done, y_act, y_dve = (
            k.sem(f"m_{n}") for n in ("idx_ready", "xt_done", "xt_sb", "g_done", "u_done", "sg_done",
                                      "hid_done", "ht_done", "ht_sb", "y_done", "y_act", "y_dve"))
        block = ctx.enter_context(nc.Block())

        def count(eng):
            return eng.value_load(k.pairs[0:1, 0:1], min_val=least - 3, max_val=SLOT_BLOCKS // 2 - 3) + 3

        @block.sync
        def _(sp):
            pairs = count(sp)

            def load(v, b, first):
                e = sp.value_load(k.block_expert[0:1, v:v + 1] if first else k.block_expert[0:1, bass.ds(v, 1)],
                                  min_val=0, max_val=EXPERTS - 1)
                if not first:
                    sp.wait_ge(g_done, v - 1)
                sp.dma_start(wg[:, b], ins["moe_w_gate"][bass.ds(e, 1)].rearrange("e (c p) n -> p (e c) n", p=P)) \
                    .then_inc(g_in[b], 16)
                if not first:
                    sp.wait_ge(u_done, v - 1)
                sp.dma_start(wu[:, b], ins["moe_w_up"][bass.ds(e, 1)].rearrange("e (c p) n -> p (e c) n", p=P)) \
                    .then_inc(u_in[b], 16)
                if not first:
                    sp.wait_ge(y_done, v - 1)
                sp.dma_start(wd[:, b], ins["moe_w_down"][bass.ds(e, 1)].rearrange("e (c p) n -> p (e c) n", p=P)) \
                    .then_inc(d_in[b], 16)

            for b in range(2):
                load(b, b, True)
            with sp.Fori(1, pairs) as i:
                for b in range(2):
                    load(2 * i + b, b, False)

        @block.gpsimd
        def _(pool):
            pairs = count(pool)

            def gather(column, b):
                nc.gpsimd.tensor_copy(idx[:, b:b + 1], column).then_inc(idx_ready, 1)

            def fetch(b):
                nc.gpsimd.indirect_dma_start(
                    out=xg[:, b, :], out_offset=None, in_=k.normed_dram,
                    in_offset=bass.IndirectOffsetOnAxis(ap=idx[:, b:b + 1], axis=0)).then_inc(x_in[b], 16)

            for b in range(2):
                gather(k.slot_token[:, b:b + 1], b)
                pool.wait_ge(idx_ready, b + 1)
                fetch(b)
            with pool.Fori(1, pairs) as i:
                for b in range(2):
                    pool.wait_ge(xt_done, 2 * i + b - 1)
                    gather(k.slot_token[:, bass.ds(2 * i + b, 1)], b)
                    pool.wait_ge(idx_ready, 2 * i + b + 1)
                    pool.sem_inc(turn, 1)
                    fetch(b)


        @block.tensor
        def _(pe):
            pairs = count(pe)

            def X(b, r):
                pe.wait_ge(x_in[b], 16 * r + 16)
                for c in range(KC):
                    last = nc.tensor.transpose(xt_ps[c // 4][:, (c % 4) * P:(c % 4 + 1) * P],
                                               xg[:, b, c * P:(c + 1) * P], k.const("ident"))
                last.then_inc(xt_done, 1)

            def G(n, b, r, first=False):
                pe.wait_ge(xt_sb, n + 1)
                pe.wait_ge(g_in[b], 16 * r + 16)
                if not first:
                    pe.wait_ge(sg_done, n)
                for c in range(KC):
                    last = nc.tensor.matmul(g_ps[:, :], lhsT=xT[:, b, c, :], rhs=wg[:, b, c, :],
                                            start=c == 0, stop=c == KC - 1)
                last.then_inc(g_done, 1)

            def U(b, r):
                pe.wait_ge(u_in[b], 16 * r + 16)
                for c in range(KC):
                    last = nc.tensor.matmul(u_ps[:, :], lhsT=xT[:, b, c, :], rhs=wu[:, b, c, :],
                                            start=c == 0, stop=c == KC - 1)
                last.then_inc(u_done, 1)

            def H(n):
                pe.wait_ge(hid_done, n + 1)
                for c in range(FC):
                    last = nc.tensor.transpose(ht_ps[:, c * P:(c + 1) * P], hid[:, c * P:(c + 1) * P],
                                               k.const("ident"))
                last.then_inc(ht_done, 1)

            def Y(n, b, r, first=False):
                pe.wait_ge(ht_sb, n + 1)
                pe.wait_ge(d_in[b], 16 * r + 16)
                if not first:
                    pe.wait_ge(y_act, n)
                    pe.wait_ge(y_dve, n)
                for h in range(2):
                    for c in range(FC):
                        last = nc.tensor.matmul(y_ps[:, h * HALF:(h + 1) * HALF], lhsT=hidT[:, c, :],
                                                rhs=wd[:, b, c, h * HALF:(h + 1) * HALF],
                                                start=c == 0, stop=c == FC - 1)
                last.then_inc(y_done, 1)

            X(0, 0)
            G(0, 0, 0, first=True)
            X(1, 0)
            U(0, 0)
            G(1, 1, 0)
            H(0)
            X(0, 1)
            U(1, 0)
            Y(0, 0, 0, first=True)
            with pe.Fori(1, pairs - 1) as i:
                for b in range(2):
                    n = 2 * i + b
                    G(n, b, i)
                    H(n - 1)
                    X(1 - b, i + b)
                    U(b, i)
                    Y(n - 1, 1 - b, i - 1 + b)
            n, i = 2 * (pairs - 1), pairs - 1
            G(n, 0, i)
            H(n - 1)
            X(1, i)
            U(0, i)
            Y(n - 1, 1, i - 1)
            G(n + 1, 1, i)
            H(n)
            U(1, i)
            Y(n, 0, i)
            H(n + 1)
            Y(n + 1, 1, i)

        @block.scalar
        def _(act):
            pairs = count(act)

            def silu(n, first=False):
                act.wait_ge(g_done, n + 1)
                if not first:
                    act.wait_ge(hid_done, n)
                nc.scalar.activation(sg[:, :], g_ps[:, :], ACT.Silu).then_inc(sg_done, 1)

            def hidden(n):
                act.wait_ge(ht_done, n + 1)
                nc.scalar.copy(hidT[:, :, :], ht_ps[:, :].rearrange("p (c q) -> p c q", q=P)).then_inc(ht_sb, 1)

            def out(n, b, r, first=False):
                act.wait_ge(y_done, n + 1)
                if not first:
                    act.wait_ge(y_stored[b], 32 * r)
                nc.scalar.copy(y[:, b, 0:HALF], y_ps[:, 0:HALF]).then_inc(y_act, 1)
                rows = slice(n * P, (n + 1) * P) if first else bass.ds(n * P, P)
                act.wait_ge(y_act, n + 1)
                act.dma_start(k.slot_out[rows, 0:HALF], y[:, b, 0:HALF]).then_inc(y_stored[b], 16)
                act.wait_ge(y_dve, n + 1)
                act.dma_start(k.slot_out[rows, HALF:D], y[:, b, HALF:D]).then_inc(y_stored[b], 16)

            silu(0, first=True)
            silu(1)
            hidden(0)
            out(0, 0, 0, first=True)
            silu(2)
            hidden(1)
            out(1, 1, 0, first=True)
            silu(3)
            hidden(2)
            out(2, 0, 1)
            with act.Fori(2, pairs) as i:
                for b in range(2):
                    n = 2 * i + b
                    silu(n)
                    hidden(n - 1)
                    out(n - 1, 1 - b, i - 1 + b)
            n = 2 * pairs - 1
            hidden(n)
            out(n, 1, pairs - 1)
            for b in range(2):
                act.wait_ge(y_stored[b], 32 * pairs)
            act.sem_inc(turn, 1)

        @block.vector
        def _(dve):
            pairs = count(dve)

            def turned(n, b):
                dve.wait_ge(xt_done, n + 1)
                for c in range(KC):
                    last = nc.vector.tensor_scalar(xT[:, b, c, :], xt_ps[c // 4][:, (c % 4) * P:(c % 4 + 1) * P],
                                                   gain[:, c:c + 1], shift[:, c:c + 1], ALU.mult, ALU.add)
                last.then_inc(xt_sb, 1)

            def hidden(n):
                dve.wait_ge(sg_done, n + 1)
                dve.wait_ge(u_done, n + 1)
                nc.vector.tensor_tensor(hid[:, :], sg[:, :], u_ps[:, :], ALU.mult).then_inc(hid_done, 1)

            def out(n, b, r, first=False):
                dve.wait_ge(y_done, n + 1)
                if not first:
                    dve.wait_ge(y_stored[b], 32 * r)
                nc.vector.tensor_copy(y[:, b, HALF:D], y_ps[:, HALF:D]).then_inc(y_dve, 1)

            turned(0, 0)
            turned(1, 1)
            hidden(0)
            turned(2, 0)
            hidden(1)
            out(0, 0, 0, first=True)
            turned(3, 1)
            hidden(2)
            out(1, 1, 0, first=True)
            turned(4, 0)
            hidden(3)
            out(2, 0, 1)
            with dve.Fori(2, pairs - 1) as i:
                for b in range(2):
                    n = 2 * i + b
                    turned(n + 1, 1 - b)
                    hidden(n)
                    out(n - 1, 1 - b, i - 1 + b)
            n, i = 2 * (pairs - 1), pairs - 1
            turned(n + 1, 1)
            hidden(n)
            out(n - 1, 1, i - 1)
            hidden(n + 1)
            out(n, 0, i)
            out(n + 1, 1, i)


def combine_stage(k):
    nc, ins = k.nc, k.ins
    with ExitStack() as ctx:
        sb = lambda n, s, d=F32: k.sb(f"b_{n}", s, d, ctx=ctx)
        rows = sb("rows", [P, 2, 2, D])
        part = sb("part", [P, 2, D])
        gate, final = sb("gate", [P, D]), sb("final", [P, D])
        sq, ss = sb("sq", [P, 2, D]), sb("ss", [P, TT])
        gate_ps = k.ps("b_gate_ps", [P, D], ctx=ctx)
        gate_mm, gate_sb, f_in, summed, added, squared, var, std, dve_step = (k.sem(f"b_{n}") for n in (
            "gate_mm", "gate_sb", "f_in", "summed", "added", "squared", "var", "std", "dve_step"))
        row_in = [k.sem(f"b_row_in{b}") for b in range(2)]
        rows_used = k.sem("b_rows_used")
        block = ctx.enter_context(nc.Block())

        @block.sync
        def _(sp):
            sp.dma_start(final[:, :], ins["final_g"].partition_broadcast(P)).then_inc(f_in, 16)

        @block.gpsimd
        def _(pool):
            def gather(t):
                if t >= 2:
                    pool.wait_ge(rows_used, t - 1)
                for n in range(2):
                    nc.gpsimd.indirect_dma_start(
                        out=rows[:, t % 2, n, :], out_offset=None, in_=k.slot_out,
                        in_offset=bass.IndirectOffsetOnAxis(ap=k.dest[:, n, t:t + 1], axis=0)).then_inc(row_in[t % 2], 16)
            gather(0)
            for t in range(TT):
                if t + 1 < TT:
                    gather(t + 1)
                pool.wait_ge(summed, t + 1)
                nc.gpsimd.tensor_tensor(k.x_tok[:, t, :], k.x_tok[:, t, :], part[:, t % 2], ALU.add).then_inc(added, 1)

        @block.tensor
        def _(pe):
            for c in range(KC):
                last = nc.tensor.matmul(gate_ps[:, c * P:(c + 1) * P],
                                        lhsT=k.mod[:, 5 * KC + c:5 * KC + c + 1].to_broadcast([P, P]),
                                        rhs=k.const("ident"), start=True, stop=True)
            last.then_inc(gate_mm, 1)

        @block.scalar
        def _(act):
            act.wait_ge(gate_mm, 1)
            nc.scalar.copy(gate[:, :], gate_ps[:, :]).then_inc(gate_sb, 1)
            for t in range(TT):
                act.wait_ge(added, t + 1)
                if t >= 2:
                    act.wait_ge(squared, t - 1)
                nc.scalar.activation(sq[:, t % 2], k.x_tok[:, t, :], ACT.Square,
                                     accum_out=ss[:, t:t + 1]).then_inc(squared, 1)
            act.wait_ge(var, 1)
            nc.scalar.activation(ss[:, :], ss[:, :], ACT.Sqrt).then_inc(std, 1)

        @block.vector
        def _(dve):
            step = chain(dve, dve_step)
            dve.wait_ge(gate_sb, 1)
            for t in range(TT):
                dve.wait_ge(row_in[t % 2], 32 * (t // 2 + 1))
                if t >= 2:
                    dve.wait_ge(added, t - 1)
                r = rows[:, t % 2]
                step(nc.vector.tensor_scalar(r[:, 0, :], r[:, 0, :], k.gates[:, 0, t:t + 1], None, ALU.mult))
                step(nc.vector.scalar_tensor_tensor(r[:, 0, :], in0=r[:, 1, :], scalar=k.gates[:, 1, t:t + 1],
                                                    in1=r[:, 0, :], op0=ALU.mult, op1=ALU.add))
                last = nc.vector.tensor_tensor(part[:, t % 2], r[:, 0, :], gate[:, :], ALU.mult)
                last.then_inc(summed, 1)
                dve.wait_ge(summed, t + 1)
                dve.sem_inc(rows_used, 1)
            dve.wait_ge(squared, TT)
            nc.vector.tensor_scalar(ss[:, :], ss[:, :], 1.0 / D, EPS, ALU.mult, ALU.add).then_inc(var, 1)
            dve.wait_ge(std, 1)
            step(nc.vector.reciprocal(ss[:, :], ss[:, :]))
            dve.wait_ge(f_in, 16)
            for t in range(TT):
                nc.vector.scalar_tensor_tensor(k.x_tok[:, t, :], in0=k.x_tok[:, t, :], scalar=ss[:, t:t + 1],
                                               in1=final[:, :], op0=ALU.mult, op1=ALU.mult)


def alloc_routing(k, ctx):
    k.dest = k.sb("dest", [P, 2, TT], U32, ctx=ctx)
    k.gates = k.sb("gates", [P, 2, TT], ctx=ctx)
    k.slot_token = k.sb("slot_token", [P, SLOT_BLOCKS], U32, ctx=ctx)
    k.block_expert = k.sb("block_expert", [P, SLOT_BLOCKS], I32, ctx=ctx)
    k.pairs = k.sb("pairs", [P, 1], I32, ctx=ctx)
    k.normed_dram = k.nc.dram_tensor("normed_tokens", (S, D), F32, kind="Internal").ap()
    k.table_dram = k.nc.dram_tensor("slot_table", (SLOT_BLOCKS * P, 1), F32, kind="Internal").ap()
    k.slot_out = k.nc.dram_tensor("slot_out", (SLOT_BLOCKS * P, D), F32, kind="Internal").ap()


QK_HEADS = HEADS + KV_HEADS
TOKEN_COLS = 1536 + 356
ROPE_A, ROPE_I = HD // 4 // 2, IDX_DIM // 4 // 2


def qkv_stage(k):
    nc, ins = k.nc, k.ins
    with ExitStack() as ctx:
        sb = lambda n, s, d=F32: k.sb(f"q_{n}", s, d, ctx=ctx)
        w_q, w_rest = k.g_att, k.z_att
        raw = sb("raw", [P, 2, TOKEN_COLS])
        sq = sb("sq", [P, QK_HEADS * HD])
        gq = sb("gq", [P, 2, HD])
        lnr = sb("lnr", [P, 2, IDX_DIM])
        pos_i, pos = sb("pos_i", [P, TT], I32), sb("pos", [P, TT])
        nf = ROPE_A + ROPE_I
        freq, ang, turns = sb("freq", [P, nf]), sb("ang", [P, TT, nf]), sb("turns", [P, TT, nf])
        sin, cos = sb("sin", [P, TT, nf]), sb("cos", [P, TT, nf])
        ss, mu = sb("ss", [P, 2, QK_HEADS + 1]), sb("mu", [P, 2])
        kc_, kd, ksq = sb("kc", [P, 2, IDX_DIM]), sb("kd", [P, 2, 2, IDX_DIM]), sb("ksq", [P, IDX_DIM])
        ra, rb, rc, rd = (sb(f"rot{n}", [P, QK_HEADS, ROPE_A]) for n in range(4))
        mm = [k.ps(f"q_mm{i}", [P, HALF], ctx=ctx) for i in range(4)]
        tp = [k.ps(f"q_tp{i}", [P, HALF], ctx=ctx) for i in range(4)]
        w_in, small_in, mm_done, raw_done, tr_done, tr_out = (k.sem(f"q_{n}") for n in (
            "w_in", "small_in", "mm_done", "raw_done", "tr_done", "tr_out"))
        sq_done, var, std, scaled, gained, ready, ang_ready, trig, dve_step, pool_step = (k.sem(f"q_{n}") for n in (
            "sq_done", "var", "std", "scaled", "gained", "ready", "ang_ready", "trig", "dve_step", "pool_step"))
        spans = [(0, 512), (512, 1024), (1024, 1536), (1536, TOKEN_COLS)]
        evac = (1, 2, 4, 5)
        block = ctx.enter_context(nc.Block())

        @block.sync
        def _(sp):
            sp.dma_start(pos_i[:, :], ins["positions"]).then_inc(small_in, 16)
            sp.dma_start(freq[:, :], ins["freq"].partition_broadcast(P)).then_inc(small_in, 16)
            sp.dma_start(gq[:, 0, :], ins["q_norm_g"].partition_broadcast(P)).then_inc(small_in, 16)
            sp.dma_start(gq[:, 1, :], ins["k_norm_g"].partition_broadcast(P)).then_inc(small_in, 16)
            sp.dma_start(lnr[:, 0, :], ins["idx_ln_g"].partition_broadcast(P)).then_inc(small_in, 16)
            sp.dma_start(lnr[:, 1, :], ins["idx_ln_b"].partition_broadcast(P)).then_inc(small_in, 16)
            for c in range(KC):
                rows = ins["w_tok"][c * P:(c + 1) * P, :]
                sp.dma_start(w_q[:, c, :], rows[:, 0:S]).then_inc(w_in, 16)
                sp.dma_start(w_rest[:, c, 0:TOKEN_COLS - S], rows[:, S:TOKEN_COLS]).then_inc(w_in, 16)

        @block.tensor
        def _(pe):
            pe.wait_ge(w_in, 32 * KC)

            def transposes(t):
                pe.wait_ge(ready, t + 1)
                if t:
                    pe.wait_ge(tr_out, 4 * t)
                s = t % 2
                for n in range(13):
                    src = raw[:, s, n * HD:(n + 1) * HD] if n < 10 else \
                        raw[:, s, 1536 + (n - 10) * P:1536 + (n - 9) * P] if n < 12 else \
                        kd[:, s].rearrange("p a d -> p (a d)")
                    last = nc.tensor.transpose(tp[n // 4][:, (n % 4) * P:(n % 4 + 1) * P], src, k.const("ident"))
                    if n % 4 == 3 or n == 12:
                        last.then_inc(tr_done, 1)

            for t in range(TT):
                for n, (a, b) in enumerate(spans):
                    w_n = w_q[:, :, a:b] if n < 2 else w_rest[:, :, a - S:b - S]
                    if t:
                        pe.wait_ge(raw_done, 5 * (t - 1) + evac[n])
                    for c in range(KC):
                        last = nc.tensor.matmul(mm[n][:, 0:b - a], lhsT=k.hT[:, c, t * P:(t + 1) * P],
                                                rhs=w_n[:, c, :], start=c == 0, stop=c == KC - 1)
                    last.then_inc(mm_done, 1)
                if t:
                    transposes(t - 1)
            transposes(TT - 1)

        @block.scalar
        def _(act):
            act.wait_ge(ang_ready, 1)
            nc.scalar.activation(sin[:, :, :], sin[:, :, :], ACT.Sin)
            nc.scalar.activation(cos[:, :, :], cos[:, :, :], ACT.Sin).then_inc(trig, 1)

            def out(t):
                span = slice(t * P, (t + 1) * P)
                for n, (dst, width) in enumerate((
                        (k.qT[:, 0:4, span], 4), (k.qT[:, 4:8, span], 4), (None, 4), (k.kidxT[:, span], 1))):
                    act.wait_ge(tr_done, 4 * t + n + 1)
                    src = tp[n][:, 0:width * P]
                    if n == 2:
                        r = src.rearrange("p (a q) -> p a q", q=P)
                        nc.scalar.copy(k.kT[:, :, span], r[:, 0:2, :])
                        last = nc.scalar.copy(k.qidxT[:, :, span], r[:, 2:4, :])
                    elif n == 3:
                        last = nc.scalar.copy(dst, src)
                    else:
                        last = nc.scalar.copy(dst, src.rearrange("p (a q) -> p a q", q=P))
                    last.then_inc(tr_out, 1)

            for t in range(TT):
                if t >= 2:
                    act.wait_ge(tr_done, 4 * (t - 1))
                for n, (a, b) in enumerate(spans):
                    act.wait_ge(mm_done, 4 * t + n + 1)
                    if n == 2:
                        nc.scalar.copy(raw[:, t % 2, a:a + 256], mm[n][:, 0:256]).then_inc(raw_done, 1)
                        nc.scalar.copy(k.v_tok[:, t, :], mm[n][:, 256:512]).then_inc(raw_done, 1)
                    else:
                        nc.scalar.copy(raw[:, t % 2, a:b], mm[n][:, 0:b - a]).then_inc(raw_done, 1)
                act.wait_ge(var, t + 1)
                nc.scalar.activation(ss[:, t % 2], ss[:, t % 2], ACT.Sqrt).then_inc(std, 1)
                if t:
                    out(t - 1)
            out(TT - 1)

        @block.gpsimd
        def _(pool):
            pool.wait_ge(small_in, 96)
            for t in range(TT):
                qk = raw[:, t % 2, 0:QK_HEADS * HD]
                pool.wait_ge(raw_done, 5 * t + 3)
                if t:
                    pool.wait_ge(var, t)
                nc.gpsimd.tensor_tensor(sq[:, :], qk, qk, ALU.mult).then_inc(sq_done, 1)
                pool.wait_ge(scaled, t + 1)
                heads = qk.rearrange("p (h d) -> p h d", d=HD)
                for n, (a, b) in enumerate(((0, HEADS), (HEADS, QK_HEADS))):
                    nc.gpsimd.tensor_tensor(heads[:, a:b, :], heads[:, a:b, :],
                                            gq[:, n, :].unsqueeze(1).to_broadcast([P, b - a, HD]), ALU.mult) \
                        .then_inc(gained, 1)

        @block.vector
        def _(dve):
            step = chain(dve, dve_step)
            v = nc.vector
            dve.wait_ge(small_in, 96)
            step(v.tensor_copy(pos[:, :], pos_i[:, :]))
            step(v.tensor_tensor(ang[:, :, :], pos[:, :].unsqueeze(2).to_broadcast([P, TT, nf]),
                                 freq[:, :].unsqueeze(1).to_broadcast([P, TT, nf]), ALU.mult))
            step(v.tensor_scalar(turns[:, :, :], ang[:, :, :], float(1 / (2 * np.pi)), None, ALU.mult))
            step(v.tensor_scalar(turns[:, :, :], turns[:, :, :], 12582912.0, None, ALU.add))
            step(v.tensor_scalar(turns[:, :, :], turns[:, :, :], -12582912.0, None, ALU.add))
            c1 = 6.28125
            c2 = float(np.float32(np.round((2 * np.pi - c1) * 2 ** 21) / 2 ** 21))
            for part in (c1, c2, 2 * np.pi - c1 - c2):
                step(v.scalar_tensor_tensor(ang[:, :, :].rearrange("p t f -> p (t f)"),
                                            in0=turns[:, :, :].rearrange("p t f -> p (t f)"), scalar=float(-part),
                                            in1=ang[:, :, :].rearrange("p t f -> p (t f)"),
                                            op0=ALU.mult, op1=ALU.add))
            step(v.tensor_scalar(sin[:, :, :], ang[:, :, :], 3.1415925, -3.1415925, ALU.min, ALU.max))
            step(v.scalar_tensor_tensor(cos[:, :, :].rearrange("p t f -> p (t f)"),
                                        in0=sin[:, :, :].rearrange("p t f -> p (t f)"), scalar=-1.0,
                                        in1=sin[:, :, :].rearrange("p t f -> p (t f)"), op0=ALU.mult, op1=ALU.max))
            v.tensor_scalar(cos[:, :, :], cos[:, :, :], -1.0, float(np.pi / 2), ALU.mult, ALU.add).then_inc(ang_ready, 1)
            dve.wait_ge(trig, 1)

            def rope(x, heads, half, at, t):
                cs = cos[:, t, at:at + half].unsqueeze(1).to_broadcast([P, heads, half])
                sn = sin[:, t, at:at + half].unsqueeze(1).to_broadcast([P, heads, half])
                x1, x2 = x[:, :, 0:half], x[:, :, half:2 * half]
                a, b, c, d = (r[:, 0:heads, 0:half] for r in (ra, rb, rc, rd))
                v.tensor_tensor(a, x1, cs, ALU.mult)
                v.tensor_tensor(b, x2, sn, ALU.mult)
                v.tensor_tensor(c, x2, cs, ALU.mult)
                step(v.tensor_tensor(d, x1, sn, ALU.mult))
                v.tensor_tensor(x1, a, b, ALU.subtract)
                step(v.tensor_tensor(x2, c, d, ALU.add))

            for t in range(TT):
                s = t % 2
                r = raw[:, s, :]
                heads = r[:, 0:QK_HEADS * HD].rearrange("p (h d) -> p h d", d=HD)
                qi = r[:, 1536:1792].rearrange("p (h d) -> p h d", d=IDX_DIM)
                ki = r[:, 1792:1856]
                dve.wait_ge(raw_done, 5 * t + 5)
                step(v.tensor_scalar(k.widx[:, t, :], r[:, 1856:1860], float(IDX_HEADS ** -0.5 * IDX_DIM ** -0.5),
                                     None, ALU.mult))
                v.tensor_copy(k.dt_raw[:, t, :], r[:, 1860:1892])
                step(v.tensor_reduce(mu[:, s:s + 1], ki, AX.X, ALU.add))
                step(v.tensor_scalar(mu[:, s:s + 1], mu[:, s:s + 1], -1.0 / IDX_DIM, None, ALU.mult))
                step(v.tensor_scalar(kc_[:, s], ki, mu[:, s:s + 1], None, ALU.add))
                step(v.tensor_tensor(ksq[:, :], kc_[:, s], kc_[:, s], ALU.mult))
                step(v.tensor_reduce(ss[:, s, 10:11], ksq[:, :], AX.X, ALU.add))
                step(v.tensor_scalar(ss[:, s, 10:11], ss[:, s, 10:11], 1.0 / IDX_DIM, EPS, ALU.mult, ALU.add))
                dve.wait_ge(sq_done, t + 1)
                step(v.tensor_reduce(ss[:, s, 0:10], sq[:, :].rearrange("p (h d) -> p h d", d=HD), AX.X, ALU.add))
                v.tensor_scalar(ss[:, s, 0:10], ss[:, s, 0:10], 1.0 / HD, EPS, ALU.mult, ALU.add).then_inc(var, 1)
                dve.wait_ge(std, t + 1)
                step(v.reciprocal(ss[:, s], ss[:, s]))
                v.tensor_tensor(heads, heads, ss[:, s, 0:10].unsqueeze(2).to_broadcast([P, QK_HEADS, HD]),
                                ALU.mult).then_inc(scaled, 1)
                step(v.scalar_tensor_tensor(kc_[:, s], in0=kc_[:, s], scalar=ss[:, s, 10:11], in1=lnr[:, 0, :],
                                            op0=ALU.mult, op1=ALU.mult))
                step(v.tensor_tensor(kc_[:, s], kc_[:, s], lnr[:, 1, :], ALU.add))
                rope(kc_[:, s].unsqueeze(1), 1, ROPE_I, ROPE_A, t)
                rope(qi, IDX_HEADS, ROPE_I, ROPE_A, t)
                if t >= 2:
                    dve.wait_ge(tr_done, 4 * (t - 1))
                step(v.tensor_copy(kd[:, s], kc_[:, s].unsqueeze(1).to_broadcast([P, 2, IDX_DIM])))
                dve.wait_ge(gained, 2 * t + 2)
                rope(heads, QK_HEADS, ROPE_A, 0, t)
                dve.sem_inc(ready, 1)


def causal(b):
    n = (b + 1) * P
    return n, b * (b + 1) // 2 * P


def select_stage(k):
    nc, ins = k.nc, k.ins
    first = TOPK // P
    NEVER = -3.0e38
    with ExitStack() as ctx:
        sb = lambda n, s, d=F32: k.sb(f"s_{n}", s, d, ctx=ctx)
        w = sb("w", [P, 2, KC, P])
        rl, tmp, work, best = sb("rl", [P, 2, S]), sb("tmp", [P, S]), sb("work", [P, 2, S]), sb("best", [P, 2, 8])
        future = sb("future", [P, P])
        sc_ps = [k.ps(f"s_sc{i}", [P, S], ctx=ctx) for i in range(2)]
        pj_ps = [k.ps(f"s_pj{i}", [P, S], ctx=ctx) for i in range(2)]
        w_in = [k.sem(f"s_w_in{i}") for i in range(2)]
        pj_done, pj_out, sc_done, relu, used, scored, picked, fut, dve_step, pool_step = (k.sem(f"s_{n}") for n in (
            "pj_done", "pj_out", "sc_done", "relu", "used", "scored", "picked", "fut", "dve_step", "pool_step"))
        blocks = list(range(first, TT))
        jobs = [(dst, func, n) for dst, func in ((k.z_att, ACT.Silu), (k.g_att, ACT.Sigmoid)) for n in range(KC)]
        share = [range(16 * i // len(blocks), 16 * (i + 1) // len(blocks)) for i in range(len(blocks))]
        block = ctx.enter_context(nc.Block())

        @block.sync
        def _(sp):
            for j in range(len(jobs)):
                if j >= 2:
                    sp.wait_ge(pj_done, j - 1)
                sp.dma_start(w[:, j % 2], ins["w_gates"][j]).then_inc(w_in[j % 2], 16)

        @block.tensor
        def _(pe):
            for i, b in enumerate(blocks):
                n, _ = causal(b)
                for h in range(IDX_HEADS):
                    m = i * IDX_HEADS + h
                    if m >= 2:
                        pe.wait_ge(relu, m - 1)
                    rows = slice(IDX_DIM * (h % 2), IDX_DIM * (h % 2 + 1))
                    for a in range(0, n, HALF):
                        e = min(n, a + HALF)
                        last = nc.tensor.matmul(sc_ps[m % 2][:, a:e], lhsT=k.qidxT[rows, h // 2, b * P:(b + 1) * P],
                                                rhs=k.kidxT[rows, a:e], start=True, stop=True)
                    last.then_inc(sc_done, 1)
                for j in share[i]:
                    pe.wait_ge(w_in[j % 2], 16 * (j // 2 + 1))
                    if j >= 2:
                        pe.wait_ge(pj_out, j - 1)
                    for a in range(0, S, HALF):
                        for c in range(KC):
                            last = nc.tensor.matmul(pj_ps[j % 2][:, a:a + HALF], lhsT=w[:, j % 2, c, :],
                                                    rhs=k.hT[:, c, a:a + HALF], start=c == 0, stop=c == KC - 1)
                    last.then_inc(pj_done, 1)

        @block.scalar
        def _(act):
            for i, b in enumerate(blocks):
                n, _ = causal(b)
                for h in range(IDX_HEADS):
                    m = i * IDX_HEADS + h
                    act.wait_ge(sc_done, m + 1)
                    if m >= 2:
                        act.wait_ge(used, m - 1)
                    nc.scalar.activation(rl[:, m % 2, 0:n], sc_ps[m % 2][:, 0:n], ACT.Relu).then_inc(relu, 1)
                for j in share[i]:
                    dst, func, n_ = jobs[j]
                    act.wait_ge(pj_done, j + 1)
                    nc.scalar.activation(dst[:, n_, :], pj_ps[j % 2][:, :], func).then_inc(pj_out, 1)

        @block.gpsimd
        def _(pool):
            step = chain(pool, pool_step)
            nc.gpsimd.tensor_scalar(future[:, :], k.const("before"), -BIG, None, ALU.mult).then_inc(fut, 1)
            pool.wait_ge(fut, 1)
            for i, b in enumerate(blocks):
                n, _ = causal(b)
                wk = work[:, i % 2, 0:n]
                if i >= 2:
                    pool.wait_ge(picked, i - 1)
                for h in range(IDX_HEADS):
                    m = i * IDX_HEADS + h
                    pool.wait_ge(relu, m + 1)
                    dst = wk if h == 0 else tmp[:, 0:n]
                    nc.gpsimd.tensor_scalar(dst, rl[:, m % 2, 0:n], k.widx[:, b, h:h + 1], None,
                                            ALU.mult).then_inc(used, 1)
                    pool.wait_ge(used, m + 1)
                    if h:
                        step(nc.gpsimd.tensor_tensor(wk, wk, tmp[:, 0:n], ALU.add))
                nc.gpsimd.tensor_tensor(work[:, i % 2, b * P:n], work[:, i % 2, b * P:n], future[:, :],
                                        ALU.add).then_inc(scored, 1)

        @block.vector
        def _(dve):
            step = chain(dve, dve_step)
            v = nc.vector
            dve.wait_ge(fut, 1)
            for b in range(first):
                n, at = causal(b)
                if b:
                    v.memset(k.bias[:, at:at + b * P], 0.0)
                v.tensor_copy(k.bias[:, at + b * P:at + n], future[:, :])
            for i, b in enumerate(blocks):
                n, at = causal(b)
                wk = work[:, i % 2, 0:n]
                dve.wait_ge(scored, i + 1)
                for r in range(TOPK // 8):
                    step(v.max(best[:, r % 2], wk))
                    step(v.match_replace(wk, best[:, r % 2], wk, NEVER))
                v.tensor_scalar(k.bias[:, at:at + n], wk, NEVER / 2, -BIG, ALU.is_gt, ALU.mult).then_inc(picked, 1)
            dve.wait_ge(picked, len(blocks))


def attention_stage(k):
    nc = k.nc
    scale = float(HD ** -0.5)
    with ExitStack() as ctx:
        sb = lambda n, s, d=F32: k.sb(f"a_{n}", s, d, ctx=ctx)
        sm, pT = sb("sm", [P, 2, S]), sb("pT", [P, 2, S])
        mx, nb, rs = sb("mx", [P, 2]), sb("nb", [P, 2]), sb("rs", [P, 2])
        s_ps = [k.ps(f"a_s{i}", [P, S], ctx=ctx) for i in range(2)]
        t_ps = k.ps("a_t", [P, S], ctx=ctx)
        o_ps = [k.ps(f"a_o{i}", [P, P], ctx=ctx) for i in range(2)]
        s_done, masked, neg, exped, scaled, t_done, t_out, o_done, o_out, dve_step = (k.sem(f"a_{n}") for n in (
            "s_done", "masked", "neg", "exped", "scaled", "t_done", "t_out", "o_done", "o_out", "dve_step"))
        jobs = [(b, h) for b in range(TT) for h in range(HEADS)]
        block = ctx.enter_context(nc.Block())

        @block.tensor
        def _(pe):
            def scores(m):
                b, h = jobs[m]
                n, _ = causal(b)
                if m >= 2:
                    pe.wait_ge(masked, m - 1)
                for a in range(0, n, HALF):
                    e = min(n, a + HALF)
                    last = nc.tensor.matmul(s_ps[m % 2][:, a:e], lhsT=k.qT[:, h, b * P:(b + 1) * P],
                                            rhs=k.kT[:, h // (HEADS // KV_HEADS), a:e], start=True, stop=True)
                last.then_inc(s_done, 1)

            def transposes(m):
                b, h = jobs[m]
                pe.wait_ge(scaled, m + 1)
                if m:
                    pe.wait_ge(t_out, m)
                for j in range(b + 1):
                    last = nc.tensor.transpose(t_ps[:, j * P:(j + 1) * P], sm[:, m % 2, j * P:(j + 1) * P],
                                               k.const("ident"))
                last.then_inc(t_done, 1)

            def values(m):
                b, h = jobs[m]
                pe.wait_ge(t_out, m + 1)
                if m >= 2:
                    pe.wait_ge(o_out, m - 1)
                kv = h // (HEADS // KV_HEADS)
                for j in range(b + 1):
                    last = nc.tensor.matmul(o_ps[m % 2][:, :], lhsT=k.v_tok[:, j, kv * HD:(kv + 1) * HD],
                                            rhs=pT[:, m % 2, j * P:(j + 1) * P], start=j == 0, stop=j == b)
                last.then_inc(o_done, 1)

            for m in range(-2, len(jobs)):
                if m + 2 < len(jobs):
                    scores(m + 2)
                if 0 <= m + 1 < len(jobs):
                    transposes(m + 1)
                if m >= 0:
                    values(m)

        @block.scalar
        def _(act):
            def exps(m):
                n, _ = causal(jobs[m][0])
                act.wait_ge(neg, m + 1)
                nc.scalar.activation(sm[:, m % 2, 0:n], sm[:, m % 2, 0:n], ACT.Exp, bias=nb[:, m % 2:m % 2 + 1],
                                     scale=scale, accum_out=rs[:, m % 2:m % 2 + 1]).then_inc(exped, 1)

            for m in range(-2, len(jobs)):
                if 0 <= m + 1 < len(jobs):
                    n, _ = causal(jobs[m + 1][0])
                    act.wait_ge(t_done, m + 2)
                    if m + 1 >= 2:
                        act.wait_ge(o_done, m)
                    nc.scalar.copy(pT[:, (m + 1) % 2, 0:n], t_ps[:, 0:n]).then_inc(t_out, 1)
                if m + 2 < len(jobs):
                    exps(m + 2)

        @block.vector
        def _(dve):
            step = chain(dve, dve_step)
            v = nc.vector

            def out(m):
                b, h = jobs[m]
                dve.wait_ge(o_done, m + 1)
                z = k.z_att[:, h, b * P:(b + 1) * P]
                nc.vector.tensor_tensor(z, o_ps[m % 2][:, :], z, ALU.mult).then_inc(o_out, 1)

            def mask(m):
                n, at = causal(jobs[m][0])
                s = m % 2
                dve.wait_ge(s_done, m + 1)
                if m >= 2:
                    dve.wait_ge(t_done, m - 1)
                v.tensor_tensor_reduce(out=sm[:, s, 0:n], in0=s_ps[s][:, 0:n], in1=k.bias[:, at:at + n], scale=1.0,
                                       scalar=-3.0e38, op0=ALU.add, op1=ALU.max,
                                       accum_out=mx[:, s:s + 1]).then_inc(masked, 1)
                dve.wait_ge(masked, m + 1)
                v.tensor_scalar(nb[:, s:s + 1], mx[:, s:s + 1], -scale, None, ALU.mult).then_inc(neg, 1)

            def normalise(m):
                n, _ = causal(jobs[m][0])
                s = m % 2
                dve.wait_ge(exped, m + 1)
                step(v.reciprocal(rs[:, s:s + 1], rs[:, s:s + 1]))
                v.tensor_scalar(sm[:, s, 0:n], sm[:, s, 0:n], rs[:, s:s + 1], None, ALU.mult).then_inc(scaled, 1)

            for m in range(-2, len(jobs)):
                if 0 <= m + 1 < len(jobs):
                    normalise(m + 1)
                if m + 2 < len(jobs):
                    mask(m + 2)
                if m >= 0:
                    out(m)


def branch_att_stage(k):
    nc, ins = k.nc, k.ins
    with ExitStack() as ctx:
        w = k.sb("ba_w", [P, 2, KC, P], ctx=ctx)
        acc = [k.ps(f"ba_ps{i}", [P, S], ctx=ctx) for i in range(2)]
        w_in = [k.sem(f"ba_w_in{i}") for i in range(2)]
        done, out = k.sem("ba_done"), k.sem("ba_out")
        block = ctx.enter_context(nc.Block())

        @block.sync
        def _(sp):
            for j in range(KC):
                if j >= 2:
                    sp.wait_ge(done, j - 1)
                sp.dma_start(w[:, j % 2], ins["w_branch_att"][j]).then_inc(w_in[j % 2], 16)

        @block.tensor
        def _(pe):
            for j in range(KC):
                pe.wait_ge(w_in[j % 2], 16 * (j // 2 + 1))
                if j >= 2:
                    pe.wait_ge(out, j - 1)
                for a in range(0, S, HALF):
                    for c in range(KC):
                        last = nc.tensor.matmul(acc[j % 2][:, a:a + HALF], lhsT=w[:, j % 2, c, :],
                                                rhs=k.z_att[:, c, a:a + HALF], start=c == 0, stop=c == KC - 1)
                last.then_inc(done, 1)

        @block.vector
        def _(dve):
            for j in range(KC):
                dve.wait_ge(done, j + 1)
                nc.vector.tensor_tensor(k.g_att[:, j, :], acc[j % 2][:, :], k.g_att[:, j, :], ALU.mult).then_inc(out, 1)


def step_sizes_stage(k):
    nc, ins = k.nc, k.ins
    with ExitStack() as ctx:
        sb = lambda n, s=(P, TT, SSM_HEADS), d=F32: k.sb(f"d_{n}", list(s), d, ctx=ctx)
        rows = sb("rows", (P, 2, SSM_HEADS))
        x, u, w1, lnw, eq = sb("x"), sb("u"), sb("w1"), sb("lnw"), sb("eq")
        sums = [k.ps(f"d_ps{i}", [P, TT, SSM_HEADS], ctx=ctx) for i in range(3)]
        r_in, a_done, absx, exped, plus, logged, adt_ready, summed, expsum, dve_step = (k.sem(f"d_{n}") for n in (
            "r_in", "a_done", "absx", "exped", "plus", "logged", "adt_ready", "summed", "expsum", "dve_step"))
        block = ctx.enter_context(nc.Block())

        @block.sync
        def _(sp):
            sp.dma_start(rows[:, 0, :], ins["dt_bias"].partition_broadcast(P)).then_inc(r_in, 16)
            sp.dma_start(rows[:, 1, :], ins["a_log"].partition_broadcast(P)).then_inc(r_in, 16)
            sp.dma_start(k.d_skip[:, :], ins["d_skip"].partition_broadcast(P)).then_inc(r_in, 16)

        @block.scalar
        def _(act):
            act.wait_ge(r_in, 48)
            nc.scalar.activation(rows[:, 1, :], rows[:, 1, :], ACT.Exp).then_inc(a_done, 1)
            act.wait_ge(absx, 1)
            nc.scalar.activation(u[:, :, :], u[:, :, :], ACT.Exp).then_inc(exped, 1)
            act.wait_ge(plus, 1)
            nc.scalar.activation(lnw[:, :, :], w1[:, :, :], ACT.Ln).then_inc(logged, 1)
            act.wait_ge(summed, 1)
            for src, dst in zip(sums, (k.e_cum, k.e_after, k.e_all)):
                last = nc.scalar.activation(dst[:, :, :], src[:, :, :], ACT.Exp)
            last.then_inc(expsum, 1)

        @block.tensor
        def _(pe):
            pe.wait_ge(adt_ready, 1)
            for n, tri in enumerate(("upto", "after", "ones")):
                last = nc.tensor.matmul(sums[n][:, :, :].rearrange("p t h -> p (t h)"), lhsT=k.const(tri),
                                        rhs=k.adt[:, :, :].rearrange("p t h -> p (t h)"), start=True, stop=True)
            last.then_inc(summed, 1)

        @block.vector
        def _(dve):
            step = chain(dve, dve_step)
            v = nc.vector
            row = lambda n: rows[:, n, :].unsqueeze(1).to_broadcast([P, TT, SSM_HEADS])
            dve.wait_ge(r_in, 48)
            step(v.tensor_tensor(x[:, :, :], k.dt_raw[:, :, :], row(0), ALU.add))
            step(v.tensor_scalar(u[:, :, :], x[:, :, :], -1.0, None, ALU.mult))
            v.tensor_tensor(u[:, :, :], u[:, :, :], x[:, :, :], ALU.min).then_inc(absx, 1)
            dve.wait_ge(exped, 1)
            v.tensor_scalar(w1[:, :, :], u[:, :, :], 1.0, None, ALU.add).then_inc(plus, 1)
            dve.wait_ge(logged, 1)
            dve.wait_ge(plus, 1)
            step(v.tensor_scalar(w1[:, :, :], w1[:, :, :], -1.0, None, ALU.add))
            step(v.tensor_scalar(eq[:, :, :], w1[:, :, :], 0.0, None, ALU.is_equal))
            step(v.tensor_tensor(w1[:, :, :], w1[:, :, :], eq[:, :, :], ALU.add))
            step(v.tensor_tensor(lnw[:, :, :], lnw[:, :, :], eq[:, :, :], ALU.add))
            step(v.reciprocal(w1[:, :, :], w1[:, :, :]))
            step(v.tensor_tensor(lnw[:, :, :], lnw[:, :, :], w1[:, :, :], ALU.mult))
            step(v.tensor_tensor(lnw[:, :, :], lnw[:, :, :], u[:, :, :], ALU.mult))
            step(v.tensor_scalar(x[:, :, :], x[:, :, :], 0.0, None, ALU.max))
            step(v.tensor_tensor(k.dt[:, :, :], x[:, :, :], lnw[:, :, :], ALU.add))
            dve.wait_ge(a_done, 1)
            step(v.tensor_tensor(k.adt[:, :, :], k.dt[:, :, :], row(1), ALU.mult))
            step(v.tensor_scalar(k.adt[:, :, :], k.adt[:, :, :], -1.0, None, ALU.mult))
            dve.sem_inc(adt_ready, 1)
            dve.wait_ge(expsum, 1)
            step(v.tensor_tensor(k.e_after[:, :, :], k.e_after[:, :, :], k.dt[:, :, :], ALU.mult))


def ssm_inputs_stage(k, g):
    nc, ins = k.nc, k.ins
    pad = SSM_CONV - 1
    tiles = [4 * g + n for n in range(4)] + [16 + g, 20 + g]
    with ExitStack() as ctx:
        sb = lambda n, s, d=F32: k.sb(f"i{g}_{n}", s, d, ctx=ctx)
        w, wz = sb("w", [P, 2, KC, P]), sb("wz", [P, KC, GW])
        u, xf = sb("u", [P, 2, pad + S]), sb("xf", [P, 2, S])
        pj = [k.ps(f"i{g}_pj{i}", [P, S], ctx=ctx) for i in range(2)]
        tr = [k.ps(f"i{g}_tr{i}", [P, HALF], ctx=ctx) for i in range(2)]
        zp = [k.ps(f"i{g}_z{i}", [P, GW], ctx=ctx) for i in range(2)]
        w_in = [k.sem(f"i{g}_w_in{i}") for i in range(2)]
        z_in, pads, pj_done, u_done, conv, act_done, tr_done, tr_out, z_done, z_out, dve_step = (
            k.sem(f"i{g}_{n}") for n in ("z_in", "pads", "pj_done", "u_done", "conv", "act_done", "tr_done",
                                        "tr_out", "z_done", "z_out", "dve_step"))
        dsts = [xf[:, 0], xf[:, 1], xf[:, 0], xf[:, 1], k.BT[:, :], k.CT[:, :]]
        block = ctx.enter_context(nc.Block())

        @block.sync
        def _(sp):
            for j, tile in enumerate(tiles):
                if j >= 2:
                    sp.wait_ge(pj_done, j - 1)
                sp.dma_start(w[:, j % 2], ins["w_xbc"][tile]).then_inc(w_in[j % 2], 16)
                if j == 1:
                    sp.dma_start(wz[:, :, :], ins["w_z"][:, g * GW:(g + 1) * GW].rearrange("(c p) n -> p c n", p=P)) \
                        .then_inc(z_in, 16)

        @block.tensor
        def _(pe):
            def transposes(j):
                pe.wait_ge(act_done, j + 1)
                for h in range(2):
                    if 2 * j + h >= 2:
                        pe.wait_ge(tr_out, 2 * j + h - 1)
                    for t in range(4):
                        last = nc.tensor.transpose(tr[h][:, t * P:(t + 1) * P],
                                                   dsts[j][:, (4 * h + t) * P:(4 * h + t + 1) * P], k.const("ident"))
                    last.then_inc(tr_done, 1)

            def z(t):
                if t == 0:
                    pe.wait_ge(z_in, 16)
                if t >= 2:
                    pe.wait_ge(z_out, t - 1)
                for c in range(KC):
                    last = nc.tensor.matmul(zp[t % 2][:, :], lhsT=k.hT[:, c, t * P:(t + 1) * P], rhs=wz[:, c, :],
                                            start=c == 0, stop=c == KC - 1)
                last.then_inc(z_done, 1)

            for j in range(6):
                pe.wait_ge(w_in[j % 2], 16 * (j // 2 + 1))
                if j >= 2:
                    pe.wait_ge(u_done, j - 1)
                for a in range(0, S, HALF):
                    for c in range(KC):
                        last = nc.tensor.matmul(pj[j % 2][:, a:a + HALF], lhsT=w[:, j % 2, c, :],
                                                rhs=k.hT[:, c, a:a + HALF], start=c == 0, stop=c == KC - 1)
                last.then_inc(pj_done, 1)
                if j:
                    transposes(j - 1)
            for t in range(TT):
                z(t)

        @block.vector
        def _(dve):
            step = chain(dve, dve_step)
            v = nc.vector
            for i in range(2):
                v.memset(u[:, i, 0:pad], 0.0).then_inc(pads, 1)
            dve.wait_ge(pads, 2)
            for j, tile in enumerate(tiles):
                dve.wait_ge(u_done, j + 1)
                if j >= 2 and j < 4:
                    dve.wait_ge(tr_done, 2 * (j - 1))
                tap = lambda i: k.pv("conv_w_2", tile * SSM_CONV + i)
                step(v.tensor_scalar(dsts[j], u[:, j % 2, 0:S], tap(0), None, ALU.mult))
                for i in range(1, SSM_CONV):
                    last = v.scalar_tensor_tensor(dsts[j], in0=u[:, j % 2, i:i + S], scalar=tap(i), in1=dsts[j],
                                                  op0=ALU.mult, op1=ALU.add)
                    if i < SSM_CONV - 1:
                        step(last)
                last.then_inc(conv, 1)

        @block.scalar
        def _(act):
            def activate(j):
                act.wait_ge(conv, j + 1)
                nc.scalar.activation(dsts[j], dsts[j], ACT.Silu, bias=k.pv("conv_b_2", tiles[j])).then_inc(act_done, 1)

            def out(j):
                for h in range(2):
                    act.wait_ge(tr_done, 2 * j + h + 1)
                    dst = k.x_ssm[:, 4 * h:4 * h + 4, j * P:(j + 1) * P] if j < 4 else k.B_tok[:, 4 * h:4 * h + 4, :]
                    nc.scalar.copy(dst, tr[h][:, :].rearrange("p (t q) -> p t q", q=P)).then_inc(tr_out, 1)

            for j in range(6):
                act.wait_ge(pj_done, j + 1)
                if j >= 2:
                    act.wait_ge(conv, j - 1)
                nc.scalar.copy(u[:, j % 2, pad:pad + S], pj[j % 2][:, :]).then_inc(u_done, 1)
                if j:
                    activate(j - 1)
                if j >= 2:
                    out(j - 2)
            activate(5)
            out(4)
            for t in range(TT):
                act.wait_ge(z_done, t + 1)
                nc.scalar.activation(k.z_ssm[:, t, :], zp[t % 2][:, :], ACT.Silu).then_inc(z_out, 1)


def ssm_scan_stage(k, g):
    nc, ins = k.nc, k.ins
    heads = slice(g * HPG, (g + 1) * HPG)
    with ExitStack() as ctx:
        sb = lambda n, s, d=F32: k.sb(f"y{g}_{n}", s, d, ctx=ctx)
        xdt, xds = sb("xdt", [P, 2, HPG, SSM_HD]), sb("xds", [P, 2, HPG, SSM_HD])
        A, E = sb("A", [P, 2, HPG, P]), sb("E", [P, 2, HPG * P])
        M = E[:, :, :].rearrange("p s (h l) -> p s h l", l=P)
        cbm, state, xd = sb("cbm", [P, 2, P]), sb("state", [P, GW]), sb("xd", [P, 2, HPG, SSM_HD])
        yo, ss = sb("yo", [P, GW]), sb("ss", [P, TT])
        w = sb("w", [P, 4, D])
        yT = k.x_ssm[:, :, :].rearrange("p (c a) n -> p c (a n)", c=4)
        misc = k.ps(f"y{g}_cb", [P, HALF], ctx=ctx)
        seg = k.ps(f"y{g}_seg", [P, HPG * P], ctx=ctx)
        yd_ps, yo_ps, st_ps = (k.ps(f"y{g}_{n}", [P, GW], ctx=ctx) for n in ("yd_ps", "yo_ps", "st_ps"))
        br = k.ps(f"y{g}_br", [P, S], ctx=ctx)
        names = ("w_in", "pool_in", "A_done", "seg_done", "cb_done", "E_done", "cbm_done", "M_done", "yd_done",
                 "yo_done", "st_done", "state_done", "yo_read", "y_done", "var", "std", "normed", "tr_done",
                 "tr_out", "br_done", "br_out", "dve_step", "xd_done", "yd_read")
        q = {n: k.sem(f"y{g}_{n}") for n in names}
        block = ctx.enter_context(nc.Block())

        def per_head(x, t, n=SSM_HD):
            return x[:, t, heads].unsqueeze(2).to_broadcast([P, HPG, n])

        @block.sync
        def _(sp):
            sp.dma_start(w[:, :, :], ins["w_branch_ssm"][g * GW:(g + 1) * GW, :].rearrange("(c p) n -> p c n", p=P)) \
                .then_inc(q["w_in"], 16)

        @block.gpsimd
        def _(pool):
            for t in range(TT):
                s = t % 2
                xs = k.x_ssm[:, t, :].rearrange("p (h d) -> p h d", d=SSM_HD)
                if t >= 2:
                    pool.wait_ge(q["seg_done"], t - 1)
                nc.gpsimd.tensor_tensor(A[:, s], per_head(k.adt, t, P),
                                        k.const("after").unsqueeze(1).to_broadcast([P, HPG, P]), ALU.mult) \
                    .then_inc(q["A_done"], 1)
                if t >= 2:
                    pool.wait_ge(q["yd_done"], t - 1)
                    pool.wait_ge(q["st_done"], t - 1)
                    pool.wait_ge(q["y_done"], t - 1)
                nc.gpsimd.tensor_tensor(xdt[:, s], xs, per_head(k.dt, t), ALU.mult)
                nc.gpsimd.tensor_tensor(xds[:, s], xs, per_head(k.e_after, t), ALU.mult).then_inc(q["pool_in"], 1)
                nc.gpsimd.tensor_tensor(xd[:, s], xs,
                                        k.d_skip[:, heads].unsqueeze(2).to_broadcast([P, HPG, SSM_HD]),
                                        ALU.mult).then_inc(q["xd_done"], 1)

        @block.tensor
        def _(pe):
            def segments(t):
                span = slice(t * P, (t + 1) * P)
                pe.wait_ge(q["A_done"], t + 1)
                if t:
                    pe.wait_ge(q["E_done"], t)
                for h in range(HPG):
                    last = nc.tensor.matmul(seg[:, h * P:(h + 1) * P], lhsT=A[:, t % 2, h, :], rhs=k.const("upto"),
                                            start=True, stop=True)
                last.then_inc(q["seg_done"], 1)
                if t:
                    pe.wait_ge(q["cbm_done"], t)
                nc.tensor.matmul(misc[:, 0:P], lhsT=k.BT[:, span], rhs=k.CT[:, span], start=True, stop=True) \
                    .then_inc(q["cb_done"], 1)

            segments(0)
            for t in range(TT):
                s = t % 2
                span = slice(t * P, (t + 1) * P)
                if t + 1 < TT:
                    segments(t + 1)
                pe.wait_ge(q["pool_in"], t + 1)
                if t:
                    pe.wait_ge(q["state_done"], t)
                    pe.wait_ge(q["yo_read"], t)
                    nc.tensor.matmul(yo_ps[:, :], lhsT=k.CT[:, span], rhs=state[:, :], start=True, stop=True) \
                        .then_inc(q["yo_done"], 1)
                nc.tensor.matmul(st_ps[:, :], lhsT=k.B_tok[:, t, :], rhs=xds[:, s].rearrange("p h d -> p (h d)"),
                                 start=True, stop=True).then_inc(q["st_done"], 1)
                pe.wait_ge(q["M_done"], t + 1)
                if t:
                    pe.wait_ge(q["yd_read"], t)
                for h in range(HPG):
                    last = nc.tensor.matmul(yd_ps[:, h * SSM_HD:(h + 1) * SSM_HD], lhsT=M[:, s, h, :],
                                            rhs=xdt[:, s, h, :], start=True, stop=True)
                last.then_inc(q["yd_done"], 1)
            for t in range(TT):
                pe.wait_ge(q["normed"], t + 1)
                if t >= 2:
                    pe.wait_ge(q["tr_out"], 4 * (t - 1))
                bank = (yd_ps, yo_ps)[t % 2]
                for c in range(4):
                    last = nc.tensor.transpose(bank[:, c * P:(c + 1) * P], k.z_ssm[:, t, c * P:(c + 1) * P],
                                               k.const("ident"))
                last.then_inc(q["tr_done"], 1)
            pe.wait_ge(q["tr_out"], 4 * TT)
            pe.wait_ge(q["w_in"], 16)
            for m in range(KC):
                bank = (br, seg)[m % 2]
                if m >= 2:
                    pe.wait_ge(q["br_out"], m - 1)
                for a in range(0, S, HALF):
                    for c in range(4):
                        last = nc.tensor.matmul(bank[:, a:a + HALF], lhsT=w[:, c, m * P:(m + 1) * P],
                                                rhs=yT[:, c, a:a + HALF], start=c == 0, stop=c == 3)
                last.then_inc(q["br_done"], 1)

        @block.scalar
        def _(act):
            for t in range(TT):
                act.wait_ge(q["seg_done"], t + 1)
                if t >= 2:
                    act.wait_ge(q["yd_done"], t - 1)
                nc.scalar.activation(E[:, t % 2], seg[:, :], ACT.Exp).then_inc(q["E_done"], 1)
            act.wait_ge(q["var"], 1)
            nc.scalar.activation(ss[:, :], ss[:, :], ACT.Sqrt).then_inc(q["std"], 1)
            for t in range(TT):
                act.wait_ge(q["tr_done"], t + 1)
                bank = (yd_ps, yo_ps)[t % 2]
                for c in range(4):
                    nc.scalar.activation(yT[:, c, t * P:(t + 1) * P], bank[:, c * P:(c + 1) * P], ACT.Copy,
                                         scale=k.pv("ssm_norm_g_2", 4 * g + c)).then_inc(q["tr_out"], 1)

        @block.vector
        def _(dve):
            step = chain(dve, q["dve_step"])
            v = nc.vector
            for t in range(TT):
                s = t % 2
                dve.wait_ge(q["cb_done"], t + 1)
                if t:
                    pass
                v.tensor_tensor(cbm[:, s], misc[:, 0:P], k.const("upto"), ALU.mult).then_inc(q["cbm_done"], 1)
                dve.wait_ge(q["cbm_done"], t + 1)
                dve.wait_ge(q["E_done"], t + 1)
                v.tensor_tensor(M[:, s], E[:, s].rearrange("p (h l) -> p h l", l=P),
                                cbm[:, s].unsqueeze(1).to_broadcast([P, HPG, P]), ALU.mult).then_inc(q["M_done"], 1)
                dve.wait_ge(q["st_done"], t + 1)
                if t == 0:
                    v.tensor_copy(state[:, :], st_ps[:, :]).then_inc(q["state_done"], 1)
                else:
                    sh = state[:, :].rearrange("p (h d) -> p h d", d=SSM_HD)
                    dve.wait_ge(q["yo_done"], t)
                    step(v.tensor_tensor(sh, sh, per_head(k.e_all, t), ALU.mult))
                    v.tensor_tensor(state[:, :], state[:, :], st_ps[:, :], ALU.add).then_inc(q["state_done"], 1)
                y = yo[:, :]
                yh = y.rearrange("p (h d) -> p h d", d=SSM_HD)
                xdf = xd[:, s].rearrange("p h d -> p (h d)")
                dve.wait_ge(q["xd_done"], t + 1)
                if t:
                    dve.wait_ge(q["yo_done"], t)
                    step(v.tensor_tensor(yh, yo_ps[:, :].rearrange("p (h d) -> p h d", d=SSM_HD),
                                         per_head(k.e_cum, t), ALU.mult))
                    step(v.tensor_tensor(y, y, xdf, ALU.add))
                    xdf = y
                dve.sem_inc(q["yo_read"], 1)
                dve.wait_ge(q["yd_done"], t + 1)
                v.tensor_tensor(y, yd_ps[:, :], xdf, ALU.add).then_inc(q["yd_read"], 1)
                dve.wait_ge(q["yd_read"], t + 1)
                step(v.tensor_tensor(k.z_ssm[:, t, :], k.z_ssm[:, t, :], y, ALU.mult))
                v.tensor_tensor_reduce(out=y, in0=k.z_ssm[:, t, :], in1=k.z_ssm[:, t, :], scale=1.0, scalar=0.0,
                                       op0=ALU.mult, op1=ALU.add, accum_out=ss[:, t:t + 1]).then_inc(q["y_done"], 1)
                dve.wait_ge(q["y_done"], t + 1)
            v.tensor_scalar(ss[:, :], ss[:, :], 1.0 / GW, EPS, ALU.mult, ALU.add).then_inc(q["var"], 1)
            dve.wait_ge(q["std"], 1)
            step(v.reciprocal(ss[:, :], ss[:, :]))
            for t in range(TT):
                v.tensor_scalar(k.z_ssm[:, t, :], k.z_ssm[:, t, :], ss[:, t:t + 1], None, ALU.mult) \
                    .then_inc(q["normed"], 1)
            for m in range(KC):
                bank = (br, seg)[m % 2]
                dve.wait_ge(q["br_done"], m + 1)
                if g == 0:
                    v.tensor_copy(k.y_ssm[:, m, :], bank[:, :]).then_inc(q["br_out"], 1)
                else:
                    v.tensor_tensor(k.y_ssm[:, m, :], k.y_ssm[:, m, :], bank[:, :], ALU.add).then_inc(q["br_out"], 1)


def merge_stage(k):
    nc, ins = k.nc, k.ins
    with ExitStack() as ctx:
        w = k.sb("mg_w", [P, 2, KC, P], ctx=ctx)
        sig = k.sb("mg_sig", [P, 2, S], ctx=ctx)
        acc = [k.ps(f"mg_ps{i}", [P, S], ctx=ctx) for i in range(2)]
        w_in = [k.sem(f"mg_w_in{i}") for i in range(2)]
        done, out, mul, added = (k.sem(f"mg_{n}") for n in ("done", "out", "mul", "added"))
        block = ctx.enter_context(nc.Block())

        @block.sync
        def _(sp):
            for j in range(KC):
                if j >= 2:
                    sp.wait_ge(done, j - 1)
                sp.dma_start(w[:, j % 2], ins["w_gates"][2 * KC + j]).then_inc(w_in[j % 2], 16)

        @block.tensor
        def _(pe):
            for j in range(KC):
                pe.wait_ge(w_in[j % 2], 16 * (j // 2 + 1))
                if j >= 2:
                    pe.wait_ge(out, j - 1)
                for a in range(0, S, HALF):
                    for c in range(KC):
                        last = nc.tensor.matmul(acc[j % 2][:, a:a + HALF], lhsT=w[:, j % 2, c, :],
                                                rhs=k.hT[:, c, a:a + HALF], start=c == 0, stop=c == KC - 1)
                last.then_inc(done, 1)

        @block.scalar
        def _(act):
            for j in range(KC):
                act.wait_ge(done, j + 1)
                if j >= 2:
                    act.wait_ge(added, j - 1)
                nc.scalar.activation(sig[:, j % 2], acc[j % 2][:, :], ACT.Sigmoid).then_inc(out, 1)

        @block.vector
        def _(dve):
            for j in range(KC):
                dve.wait_ge(out, j + 1)
                nc.vector.tensor_tensor(sig[:, j % 2], sig[:, j % 2], k.y_ssm[:, j, :], ALU.mult).then_inc(mul, 1)
                dve.wait_ge(mul, j + 1)
                nc.vector.tensor_tensor(k.g_att[:, j, :], k.g_att[:, j, :], sig[:, j % 2], ALU.add).then_inc(added, 1)


def mixer_program(nc, ins, out):
    with ExitStack() as ctx:
        k = Core(nc, ctx, ins)
        k.params, k.consts = k.sb("params", [P, PV_N]), k.sb("consts", [P, len(CONSTS), P])
        k.mod, k.gain = k.sb("mod", [P, 9 * KC]), k.sb("gain", [P, 3 * KC])
        k.x_dram = nc.dram_tensor("x_second", (S, D), F32, kind="Internal").ap()
        k.hT = k.sb("hT", [P, KC, S])
        with ExitStack() as first:
            k.x_tok = k.sb("x_tok", [P, TT, D], ctx=first)
            alloc_routing(k, first)
            modulation_stage(k)
            with ExitStack() as c:
                k.y = k.sb("conv_y", [P, KC, S], ctx=c)
                norm_transpose_stage(k, "mix", k.x_tok, k.gain[:, 0:KC], k.mod[:, 0:KC], k.hT)
                conv_stage(k)
                conv_norm_stage(k)
                token_projection_stage(k, "co", k.y, ins["conv_w_out"], k.mod[:, 2 * KC:3 * KC])
            norm_transpose_stage(k, "ffn", k.x_tok, k.gain[:, KC:2 * KC], k.mod[:, 3 * KC:4 * KC], k.hT,
                                 normed_dram=k.normed_dram)
            k.clear_semaphores()
            router_stage(k)
            experts_stage(k)
            combine_stage(k)
            norm_transpose_stage(k, "two", k.x_tok, k.gain[:, 2 * KC:3 * KC], k.mod[:, 6 * KC:7 * KC], k.hT,
                                 raw_dram=k.x_dram)
        k.clear_semaphores()
        second_block(k)
        with ExitStack() as c:
            k.x_tok = k.sb("x_tok2", [P, TT, D], ctx=c)
            token_projection_stage(k, "fin", k.g_att, ins["w_out_2"], k.mod[:, 8 * KC:9 * KC], out_dram=out,
                                   x_from=k.x_dram)


def second_block(k):
    ctx = k.ctx
    k.dt_raw, k.widx = k.sb("dt_raw", [P, TT, SSM_HEADS]), k.sb("widx", [P, TT, IDX_HEADS])
    k.g_att = k.sb("g_att", [P, KC, S])
    with ExitStack() as att:
        k.z_att = k.sb("z_att", [P, KC, S], ctx=att)
        k.qT, k.kT = k.sb("qT", [P, HEADS, S], ctx=att), k.sb("kT", [P, KV_HEADS, S], ctx=att)
        k.v_tok = k.sb("v_tok", [P, TT, KV_HEADS * HD], ctx=att)
        k.bias = k.sb("bias", [P, TT * (TT + 1) // 2 * P], BF16, ctx=att)
        with ExitStack() as idx:
            k.qidxT, k.kidxT = k.sb("qidxT", [P, 2, S], ctx=idx), k.sb("kidxT", [P, S], ctx=idx)
            qkv_stage(k)
            select_stage(k)
        attention_stage(k)
        branch_att_stage(k)
    k.clear_semaphores()
    with ExitStack() as s:
        k.dt, k.adt, k.e_cum, k.e_after, k.e_all = (
            k.sb(n, [P, TT, SSM_HEADS], ctx=s) for n in ("dt", "adt", "e_cum", "e_after", "e_all"))
        k.d_skip = k.sb("d_skip", [P, SSM_HEADS], ctx=s)
        k.y_ssm = k.sb("y_ssm", [P, KC, S], ctx=s)
        step_sizes_stage(k)
        with ExitStack() as grp:
            k.x_ssm, k.z_ssm = k.sb("x_ssm", [P, TT, GW], ctx=grp), k.sb("z_ssm", [P, TT, GW], ctx=grp)
            k.B_tok = k.sb("B_tok", [P, TT, SSM_N], ctx=grp)
            k.BT, k.CT = k.sb("BT", [P, S], ctx=grp), k.sb("CT", [P, S], ctx=grp)
            for g in range(SSM_GROUPS):
                ssm_inputs_stage(k, g)
                ssm_scan_stage(k, g)
                k.clear_semaphores()
        merge_stage(k)


def layout(inputs):
    f = np.ascontiguousarray
    d = {n: np.asarray(v) for n, v in inputs.items()}

    def columns(name, n):
        v = d[name]
        if name == "conv_w_dw":
            return v[0].reshape(CONV, KC, P).transpose(2, 1, 0).reshape(P, n)
        if name == "conv_w_2":
            return v[0].reshape(SSM_CONV, 24, P).transpose(2, 1, 0).reshape(P, n)
        return v.reshape(-1, P).T

    def tiles(w):
        return f(w.reshape(KC, P, w.shape[1] // P, P).transpose(2, 1, 0, 3))

    q0, z0, i0, zs0, x0, dt0, g0 = 0, 1536, 2560, 2884, 4932, 8004, 8036
    w = d["w_in_2"][0]
    consts, freq = constant_tables()
    return {
        "x": d["x"][0], "params": f(np.concatenate([columns(n, m) for n, m in PV_FIELDS], axis=1)),
        "consts": consts, "freq": freq, "rows": row_constants(),
        "token_ids": f(np.arange(S, dtype=np.float32).reshape(TT, P).T),
        "ada_w": d["ada_w"][0], "ada_w_2": d["ada_w_2"][0],
        "conv_w_in": tiles(d["conv_w_in"][0]), "conv_w_out": d["conv_w_out"][0],
        "router_w": f(np.concatenate([d["moe_w_rg"][0], d["moe_w_re"][0]], axis=1)),
        "router_b": f(np.concatenate([d["moe_b_rg"][0], d["moe_b_re"][0]])),
        "moe_w_gate": d["moe_w_gate"][0], "moe_w_up": d["moe_w_up"][0], "moe_w_down": d["moe_w_down"][0],
        "final_g": d["final_g"], "positions": f(d["positions_2"][0].reshape(TT, P).T),
        "q_norm_g": d["q_norm_g_2"][0], "k_norm_g": d["k_norm_g_2"][0],
        "idx_ln_g": d["idx_k_ln_g_2"][0], "idx_ln_b": d["idx_k_ln_b_2"][0],
        "w_tok": f(np.concatenate([w[:, q0:z0], w[:, i0:zs0], w[:, dt0:g0]], axis=1)),
        "w_gates": tiles(np.concatenate([w[:, z0:i0], w[:, g0:]], axis=1)),
        "w_xbc": tiles(w[:, x0:dt0]), "w_z": f(w[:, zs0:x0]),
        "dt_bias": d["dt_bias_2"][0], "a_log": d["a_log_2"][0], "d_skip": d["d_skip_2"][0],
        "w_branch_att": tiles(d["w_branch_att_2"][0]), "w_branch_ssm": d["w_branch_ssm_2"][0],
        "w_out_2": d["w_out_2"][0],
    }


def kernel(**inputs):
    import concourse.bacc as bacc
    from concourse.bass_utils import run_bass_kernel_spmd

    nc = bacc.Bacc("TRN2", target_bir_lowering=False, num_devices=1)
    arrays, ins = {}, {}
    for name, a in layout(inputs).items():
        arrays[f"in_{name}"] = a
        ins[name] = nc.dram_tensor(f"in_{name}", a.shape, mybir.dt.from_np(a.dtype), kind="ExternalInput").ap()
    out = nc.dram_tensor("out_x", (S, D), F32, kind="ExternalOutput").ap()
    mixer_program(nc, ins, out)
    r = run_bass_kernel_spmd(nc, [arrays], core_ids=[0])
    return r.results[0]["out_x"].reshape(1, S, D)
```

```python
import numpy as np
from contextlib import ExitStack

import concourse.bass as bass
from concourse import mybir

F32 = mybir.dt.float32
I32 = mybir.dt.int32
U32 = mybir.dt.uint32
BF16 = mybir.dt.bfloat16
F16 = mybir.dt.float16
ALU = mybir.AluOpType
ACT = mybir.ActivationFunctionType
AX = mybir.AxisListType

P = 128
D = 1024
S = 1024
KC = D // P
TT = S // P
HALF = 512
EPS = 1e-6
CONV = 31
GROUPS, PER_GROUP = 4, 8
EXPERTS = GROUPS * PER_GROUP
FFN = D // 2
SLOT_BLOCKS = 2 * S // P + EXPERTS
HEADS, KV_HEADS, HD = 8, 2, 128
IDX_HEADS, IDX_DIM = 4, 64
TOPK = 256
SSM_INNER, SSM_HEADS, SSM_HD, SSM_GROUPS, SSM_N, SSM_CONV = 2048, 32, 64, 4, 128, 4
HPG = SSM_HEADS // SSM_GROUPS
GW = HPG * SSM_HD
BIG = 1.0e30
W_UP = 256.0

PV_FIELDS = [
    ("ada_b", 48), ("norm_mix_g", 8), ("norm_ffn_g", 8), ("conv_b_in", 16), ("conv_w_dw", 8 * CONV),
    ("conv_b_dw", 8), ("conv_ln_g", 8), ("conv_ln_b", 8), ("ada_b_2", 24), ("norm_g_2", 8),
    ("conv_w_2", 24 * SSM_CONV), ("conv_b_2", 24), ("ssm_norm_g_2", 16), ("c", 8), ("c_2", 8),
]
PV_AT, PV_N = {}, 0
for _name, _n in PV_FIELDS:
    PV_AT[_name] = PV_N
    PV_N += _n

CONSTS = ["ident", "upto", "before", "after", "ones", "mean_d"]


def constant_tables():
    k, m = np.arange(P)[:, None], np.arange(P)[None, :]
    c = {
        "ident": k == m, "upto": k <= m, "before": k < m, "after": k > m,
        "ones": np.ones((P, P)), "mean_d": np.full((P, P), 1.0 / D),
    }
    table = np.stack([np.asarray(c[n], np.float32) for n in CONSTS], axis=1)
    freq = [np.power(500000.0, -(2.0 * np.arange(n // 2) / n)) for n in (HD // 4, IDX_DIM // 4)]
    return np.ascontiguousarray(table), np.concatenate(freq).astype(np.float32)


def row_constants():
    return np.concatenate([np.arange(GROUPS, 0, -1), np.arange(EXPERTS, 0, -1), np.arange(SLOT_BLOCKS)]) \
        .astype(np.float32)


def zero_fill(k, eng, zeros, done):
    first, parts = 2 * S // P, 4
    n = (SLOT_BLOCKS - first) // parts
    for i in range(parts):
        a = (first + i * n) * P
        eng.dma_start(k.slot_out[a:a + n * P, :].rearrange("(b p) d -> p b d", p=P),
                      zeros.unsqueeze(1).to_broadcast([P, n, D])).then_inc(done, 16)
    return 16 * parts


class Core:

    def __init__(self, nc, ctx, ins):
        self.nc, self.ctx, self.ins, self.sems = nc, ctx, ins, []

    def sb(self, name, shape, dtype=F32, ctx=None):
        return (ctx or self.ctx).enter_context(self.nc.sbuf_tensor(name, shape, dtype))

    def ps(self, name, shape, dtype=F32, ctx=None):
        return (ctx or self.ctx).enter_context(self.nc.psum_tensor(name, shape, dtype))

    def sem(self, name):
        self.sems.append(self.nc.alloc_semaphore(name))
        return self.sems[-1]

    def clear_semaphores(self):
        self.nc.clear_and_free_semaphores(self.sems)
        self.nc.all_engine_barrier()
        self.sems = []

    def const(self, name):
        return self.consts[:, CONSTS.index(name), :]

    def pv(self, name, i=0, n=1):
        at = PV_AT[name] + i
        return self.params[:, at:at + n]


def chain(eng, sem):
    count = [0]

    def step(ins):
        count[0] += 1
        ins.then_inc(sem, 1)
        eng.wait_ge(sem, count[0])

    return step



def product(nc, out, lhsT, rhs, start, stop):
    (lh, ll), (rh, rl) = lhsT, rhs
    nc.tensor.matmul(out, lhsT=lh, rhs=rh, start=start, stop=False)
    nc.tensor.matmul(out, lhsT=lh, rhs=rl, start=False, stop=False)
    return nc.tensor.matmul(out, lhsT=ll, rhs=rh, start=False, stop=stop)


def part(pair, *index):
    return tuple(pair[(slice(None), n, *index)] for n in range(2))


def modulation_stage(k):
    nc, ins = k.nc, k.ins
    chunk = HALF
    n1, n2 = 6 * D // chunk, 3 * D // chunk
    slots = 4
    with ExitStack() as ctx:
        ring = k.sb("ada_ring", [P, slots, KC, chunk], ctx=ctx)
        csilu = k.sb("csilu", [P, 2, KC], ctx=ctx)
        parts, mod_mm = k.sb("mod_parts", [P, 2, chunk], ctx=ctx), k.sem("mod_mm")
        mod_ps = k.ps("mod_ps", [P, 72], ctx=ctx)
        tables_in, x_in = k.sem("tables_in"), k.sem("x_in")
        ada_in = [k.sem(f"ada_in{i}") for i in range(slots)]
        ada_used, c_ready, mod_done = k.sem("ada_used"), k.sem("c_ready"), k.sem("mod_done")
        dve_step = k.sem("mod_dve_step")
        block = ctx.enter_context(nc.Block())

        @block.sync
        def _(sp):
            for j in range(n1 + n2):
                if j >= slots:
                    sp.wait_ge(ada_used, j - slots + 1)
                src = ins["ada_w"][:, j * chunk:(j + 1) * chunk] if j < n1 else \
                    ins["ada_w_2"][:, (j - n1) * chunk:(j - n1 + 1) * chunk]
                sp.dma_start(ring[:, j % slots], src.rearrange("(c p) n -> p c n", p=P)) \
                    .then_inc(ada_in[j % slots], 16)

        @block.scalar
        def _(act):
            act.dma_start(k.params[:, :], ins["params"]).then_inc(tables_in, 16)
            act.dma_start(k.consts[:, :, :], ins["consts"]).then_inc(tables_in, 16)
            act.dma_start(k.x_tok[:, :, :], ins["x"].rearrange("(t p) d -> p t d", p=P)).then_inc(x_in, 16)
            act.wait_ge(tables_in, 32)
            nc.scalar.activation(csilu[:, 0, :], k.pv("c", 0, KC), ACT.Silu)
            nc.scalar.activation(csilu[:, 1, :], k.pv("c_2", 0, KC), ACT.Silu).then_inc(c_ready, 1)

        @block.vector
        def _(dve):
            step = chain(dve, dve_step)
            dve.wait_ge(c_ready, 1)
            for j in range(n1 + n2):
                dve.wait_ge(ada_in[j % slots], 16 * (j // slots + 1))
                if j >= 2:
                    dve.wait_ge(mod_mm, j - 1)
                for c in range(KC):
                    src, scale = ring[:, j % slots, c, :], csilu[:, int(j >= n1), c:c + 1]
                    part = parts[:, j % 2, :]
                    if c == 0:
                        last = nc.vector.tensor_scalar(part, src, scale, None, ALU.mult)
                    else:
                        last = nc.vector.scalar_tensor_tensor(part, in0=src, scalar=scale, in1=part,
                                                              op0=ALU.mult, op1=ALU.add)
                    if c < KC - 1:
                        step(last)
                last.then_inc(ada_used, 1)
            dve.wait_ge(tables_in, 32)
            dve.wait_ge(x_in, 16)
            dve.wait_ge(mod_mm, n1 + n2)
            nc.vector.tensor_tensor(k.mod[:, 0:48], mod_ps[:, 0:48], k.pv("ada_b", 0, 48), ALU.add)
            step(nc.vector.tensor_tensor(k.mod[:, 48:72], mod_ps[:, 48:72], k.pv("ada_b_2", 0, 24), ALU.add))
            for n, (scale_at, gain) in enumerate(((8, "norm_mix_g"), (32, "norm_ffn_g"), (56, "norm_g_2"))):
                nc.vector.scalar_tensor_tensor(
                    k.gain[:, n * KC:(n + 1) * KC], in0=k.mod[:, scale_at:scale_at + KC], scalar=1.0,
                    in1=k.pv(gain, 0, KC), op0=ALU.add, op1=ALU.mult).then_inc(mod_done, 1)
            dve.wait_ge(mod_done, 3)

        @block.tensor
        def _(pe):
            pe.wait_ge(tables_in, 32)
            for j in range(n1 + n2):
                pe.wait_ge(ada_used, j + 1)
                for m in range(chunk // P):
                    col = j * (chunk // P) + m
                    last = nc.tensor.matmul(mod_ps[:, col:col + 1], lhsT=parts[:, j % 2, m * P:(m + 1) * P],
                                            rhs=k.const("ones")[:, 0:1], start=True, stop=True)
                last.then_inc(mod_mm, 1)


def norm_transpose_stage(k, name, src, gain, shift, normed_dram=None, raw_dram=None):
    nc = k.nc
    with ExitStack() as ctx:
        normed = k.sb(f"{name}_normed", [P, TT, D], ctx=ctx)
        full = k.sb(f"{name}_full", [P, 4, HALF], ctx=ctx)
        ss = k.sb(f"{name}_ss", [P, TT], ctx=ctx)
        banks = [k.ps(f"{name}_t{i}", [P, HALF], ctx=ctx) for i in range(4)]
        squared, var_ready, std_ready = k.sem(f"{name}_squared"), k.sem(f"{name}_var"), k.sem(f"{name}_std")
        normed_ready, transposed = k.sem(f"{name}_normed_ready"), k.sem(f"{name}_transposed")
        high_out, full_out, low_out = k.sem(f"{name}_high"), k.sem(f"{name}_full_out"), k.sem(f"{name}_low")
        dve_step, stored = k.sem(f"{name}_dve_step"), k.sem(f"{name}_stored")
        block = ctx.enter_context(nc.Block())
        groups = KC * 2

        def at(g):
            return g // 2, slice(g % 2 * HALF, (g % 2 + 1) * HALF)

        @block.scalar
        def _(act):
            for t in range(TT):
                nc.scalar.activation(normed[:, t, :], src[:, t, :], ACT.Square,
                                     accum_out=ss[:, t:t + 1]).then_inc(squared, 1)
            act.wait_ge(var_ready, 1)
            nc.scalar.activation(ss[:, :], ss[:, :], ACT.Sqrt).then_inc(std_ready, 1)
            for g in range(groups):
                act.wait_ge(full_out, g + 1)
                c, span = at(g)
                nc.scalar.copy(k.hT[:, 0, c, span], full[:, g % 4]).then_inc(high_out, 1)

        @block.vector
        def _(dve):
            step = chain(dve, dve_step)
            dve.wait_ge(squared, TT)
            nc.vector.tensor_scalar(ss[:, :], ss[:, :], 1.0 / D, EPS, ALU.mult, ALU.add).then_inc(var_ready, 1)
            dve.wait_ge(std_ready, 1)
            step(nc.vector.reciprocal(ss[:, :], ss[:, :]))
            for t in range(TT):
                nc.vector.tensor_scalar(normed[:, t, :], src[:, t, :], ss[:, t:t + 1], None,
                                        ALU.mult).then_inc(normed_ready, 1)
            for g in range(groups):
                dve.wait_ge(transposed, g + 1)
                c, span = at(g)
                if g >= 4:
                    dve.wait_ge(low_out, g - 3)
                nc.vector.tensor_scalar(full[:, g % 4], banks[g % 4][:, :],
                                        gain[:, c:c + 1], shift[:, c:c + 1], ALU.mult, ALU.add) \
                    .then_inc(full_out, 1)

        @block.gpsimd
        def _(pool):
            for g in range(groups):
                c, span = at(g)
                pool.wait_ge(full_out, g + 1)
                pool.wait_ge(high_out, g + 1)
                nc.gpsimd.tensor_tensor(k.hT[:, 1, c, span], full[:, g % 4], k.hT[:, 0, c, span],
                                        ALU.subtract).then_inc(low_out, 1)

        @block.tensor
        def _(pe):
            for g in range(groups):
                c, h = g // 2, g % 2
                if g >= 4:
                    pe.wait_ge(full_out, g - 3)
                for t in range(4):
                    if g < 2:
                        pe.wait_ge(normed_ready, 4 * h + t + 1)
                    last = nc.tensor.transpose(banks[g % 4][:, t * P:(t + 1) * P],
                                               normed[:, 4 * h + t, c * P:(c + 1) * P], k.const("ident"))
                last.then_inc(transposed, 1)

        if normed_dram is not None:
            @block.sync
            def _(sp):
                for t in range(TT):
                    sp.wait_ge(normed_ready, t + 1)
                    sp.dma_start(normed_dram[t * P:(t + 1) * P, :], normed[:, t, :]).then_inc(stored, 16)
                sp.wait_ge(stored, 16 * TT)

        if raw_dram is not None:
            @block.sync
            def _(sp):
                sp.dma_start(raw_dram.rearrange("(t p) d -> p t d", p=P), src[:, :, :]).then_inc(stored, 16)
                sp.wait_ge(stored, 16)


def high_part(nc, out, w):
    return nc.scalar.activation(out, w, ACT.Copy, scale=W_UP)


def low_part(nc, out, w, high):
    return nc.vector.scalar_tensor_tensor(out, in0=w, scalar=W_UP, in1=high, op0=ALU.mult, op1=ALU.subtract)


def conv_stage(k):
    nc, ins = k.nc, k.ins
    pad = CONV - 1
    with ExitStack() as ctx:
        w = k.sb("cw", [P, 2, 2, KC, P], ctx=ctx)
        ws = k.sb("cws", [P, 2, 2, 2, KC, P], F16, ctx=ctx)
        b_up, w_down = k.sb("cb_up", [P, KC], ctx=ctx), k.sb("cw_down", [P, KC * CONV], ctx=ctx)
        u = k.sb("cu", [P, 2, pad + S], ctx=ctx)
        sig = k.sb("csig", [P, 2, S], ctx=ctx)
        pool_sum = k.sb("cpool_sum", [P, S], ctx=ctx)
        tap = k.sb("ctap", [P, 2, S], ctx=ctx)
        acc = [[k.ps(f"c{n}{i}", [P, S], ctx=ctx) for i in range(2)] for n in "ag"]
        w_in = [k.sem(f"cw_in{i}") for i in range(2)]
        mm_done, sig_done, u_done, conv_done = k.sem("c_mm"), k.sem("c_sig"), k.sem("c_u"), k.sem("c_conv")
        pads, tap_done, tap_added, dve_step = k.sem("c_pads"), k.sem("c_tap"), k.sem("c_tap_added"), k.sem("c_dve")
        zeros, zero_sb, zeroed = k.sb("c_zeros", [P, D], ctx=ctx), k.sem("c_zero_sb"), k.sem("c_zeroed")
        high, low, params_up = k.sem("c_high"), k.sem("c_low"), k.sem("c_params_up")
        pool_taps = 9
        block = ctx.enter_context(nc.Block())

        @block.sync
        def _(sp):
            for i in range(KC):
                if i >= 2:
                    sp.wait_ge(low, i - 1)
                    sp.wait_ge(high, i - 1)
                for n in range(2):
                    sp.dma_start(w[:, i % 2, n], ins["conv_w_in"][n * KC + i]).then_inc(w_in[i % 2], 16)
            sp.wait_ge(zero_sb, 1)
            sp.wait_ge(zeroed, zero_fill(k, sp, zeros[:, :], zeroed))

        @block.tensor
        def _(pe):
            for i in range(KC):
                pe.wait_ge(high, i + 1)
                pe.wait_ge(low, i + 1)
                if i >= 2:
                    pe.wait_ge(u_done, i - 1)
                for n in (1, 0):
                    for h in range(2):
                        for c in range(KC):
                            last = product(nc, acc[n][i % 2][:, h * HALF:(h + 1) * HALF],
                                           part(ws, i % 2, n, c), part(k.hT, c, slice(h * HALF, (h + 1) * HALF)),
                                           c == 0, c == KC - 1)
                last.then_inc(mm_done, 1)

        @block.scalar
        def _(act):
            def split(i):
                act.wait_ge(w_in[i % 2], 32 * (i // 2 + 1))
                if i >= 2:
                    act.wait_ge(mm_done, i - 1)
                high_part(nc, ws[:, 0, i % 2], w[:, i % 2]).then_inc(high, 1)

            split(0)
            for i in range(KC):
                if i + 1 < KC:
                    split(i + 1)
                act.wait_ge(mm_done, i + 1)
                if i >= 2:
                    act.wait_ge(u_done, i - 1)
                nc.scalar.activation(sig[:, i % 2], acc[1][i % 2][:, :], ACT.Sigmoid, scale=1.0 / W_UP,
                                     bias=k.pv("conv_b_in", KC + i)).then_inc(sig_done, 1)
                act.wait_ge(u_done, i + 1)
                for j in range(pool_taps):
                    n = i * pool_taps + j
                    if n >= 2:
                        act.wait_ge(tap_added, n - 1)
                    nc.scalar.activation(tap[:, n % 2], u[:, i % 2, j:j + S], ACT.Copy,
                                         scale=w_down[:, i * CONV + j:i * CONV + j + 1]).then_inc(tap_done, 1)

        @block.gpsimd
        def _(pool):
            nc.gpsimd.memset(zeros[:, :], 0.0).then_inc(zero_sb, 1)
            for i in range(KC):
                for j in range(pool_taps):
                    n = i * pool_taps + j
                    pool.wait_ge(tap_done, n + 1)
                    if j == 0:
                        if i:
                            pool.wait_ge(conv_done, i)
                        nc.gpsimd.tensor_copy(pool_sum[:, :], tap[:, n % 2]).then_inc(tap_added, 1)
                    else:
                        pool.wait_ge(tap_added, n)
                        nc.gpsimd.tensor_tensor(pool_sum[:, :], pool_sum[:, :], tap[:, n % 2], ALU.add) \
                            .then_inc(tap_added, 1)

        @block.vector
        def _(dve):
            step = chain(dve, dve_step)
            for i in range(2):
                nc.vector.memset(u[:, i, 0:pad], 0.0).then_inc(pads, 1)
            nc.vector.tensor_scalar(b_up[:, :], k.pv("conv_b_in", 0, KC), W_UP, None, ALU.mult).then_inc(pads, 1)
            nc.vector.tensor_scalar(w_down[:, :], k.pv("conv_w_dw", 0, KC * CONV), 1.0 / W_UP, None,
                                    ALU.mult).then_inc(pads, 1)
            dve.wait_ge(pads, 4)

            def split(i):
                dve.wait_ge(high, i + 1)
                low_part(nc, ws[:, 1, i % 2].rearrange("p a c q -> p (a c q)"),
                         w[:, i % 2].rearrange("p a c q -> p (a c q)"),
                         ws[:, 0, i % 2].rearrange("p a c q -> p (a c q)")).then_inc(low, 1)

            split(0)
            for i in range(KC):
                if i + 1 < KC:
                    split(i + 1)
                dve.wait_ge(sig_done, i + 1)
                if i >= 2:
                    dve.wait_ge(tap_done, (i - 1) * pool_taps)
                nc.vector.scalar_tensor_tensor(
                    u[:, i % 2, pad:pad + S], in0=acc[0][i % 2][:, :], scalar=b_up[:, i:i + 1],
                    in1=sig[:, i % 2], op0=ALU.add, op1=ALU.mult).then_inc(u_done, 1)
                dve.wait_ge(u_done, i + 1)
                y = k.y[:, i, :]
                j = pool_taps
                step(nc.vector.tensor_scalar(y, u[:, i % 2, j:j + S], w_down[:, i * CONV + j:i * CONV + j + 1],
                                             k.pv("conv_b_dw", i), ALU.mult, ALU.add))
                for j in range(pool_taps + 1, CONV):
                    step(nc.vector.scalar_tensor_tensor(
                        y, in0=u[:, i % 2, j:j + S], scalar=w_down[:, i * CONV + j:i * CONV + j + 1], in1=y,
                        op0=ALU.mult, op1=ALU.add))
                dve.wait_ge(tap_added, (i + 1) * pool_taps)
                nc.vector.tensor_tensor(y, y, pool_sum[:, :], ALU.add).then_inc(conv_done, 1)


def conv_norm_stage(k):
    nc, ins = k.nc, k.ins
    with ExitStack() as ctx:
        sq = k.sb("ln_sq", [P, 4, HALF], ctx=ctx)
        rstd = k.sb("ln_rstd", [P, 2, HALF], ctx=ctx)
        mean_ps, var_ps = k.ps("ln_mean", [P, 2, HALF], ctx=ctx), k.ps("ln_var", [P, 2, HALF], ctx=ctx)
        mean_done, centred, squared, sq_used = (k.sem(n) for n in ("ln_mean_done", "ln_centred", "ln_squared", "ln_sq_used"))
        var_sb, std_done, scaled, activated, high, dve_step = (
            k.sem(n) for n in ("ln_var_sb", "ln_std", "ln_scaled", "ln_activated", "ln_high", "ln_dve"))
        block = ctx.enter_context(nc.Block())
        pieces = [(h, c) for h in range(2) for c in range(KC)]
        y = lambda h, c: k.y[:, c, h * HALF:(h + 1) * HALF]

        @block.sync
        def _(sp):
            for c in range(KC):
                sp.dma_start(k.next_w[:, c, :], ins["conv_w_out"][c * P:(c + 1) * P, :]).then_inc(k.next_w_in, 16)

        @block.tensor
        def _(pe):
            for h, c in pieces:
                last = nc.tensor.matmul(mean_ps[:, h, :], lhsT=k.const("mean_d"), rhs=y(h, c),
                                        start=c == 0, stop=c == KC - 1)
                if c == KC - 1:
                    last.then_inc(mean_done, 1)
            for n, (h, c) in enumerate(pieces):
                pe.wait_ge(squared, n + 1)
                nc.tensor.matmul(var_ps[:, h, :], lhsT=k.const("mean_d"), rhs=sq[:, n % 4], start=c == 0,
                                 stop=c == KC - 1).then_inc(sq_used, 1)

        @block.vector
        def _(dve):
            step = chain(dve, dve_step)
            for n, (h, c) in enumerate(pieces):
                dve.wait_ge(mean_done, h + 1)
                nc.vector.tensor_tensor(y(h, c), y(h, c), mean_ps[:, h, :], ALU.subtract).then_inc(centred, 1)
            for h in range(2):
                dve.wait_ge(sq_used, KC * (h + 1))
                nc.vector.tensor_scalar(rstd[:, h], var_ps[:, h, :], EPS, None, ALU.add).then_inc(var_sb, 1)
                dve.wait_ge(std_done, h + 1)
                step(nc.vector.reciprocal(rstd[:, h], rstd[:, h]))
                for c in range(KC):
                    dve.wait_ge(centred, KC * h + c + 1)
                    nc.vector.tensor_tensor(y(h, c), y(h, c), rstd[:, h], ALU.mult).then_inc(scaled, 1)
            for n, (h, c) in enumerate(pieces):
                dve.wait_ge(high, n + 1)
                nc.vector.tensor_tensor(k.hT[:, 1, c, h * HALF:(h + 1) * HALF], y(h, c),
                                        k.hT[:, 0, c, h * HALF:(h + 1) * HALF], ALU.subtract)

        @block.scalar
        def _(act):
            for n, (h, c) in enumerate(pieces):
                act.wait_ge(centred, n + 1)
                if n >= 4:
                    act.wait_ge(sq_used, n - 3)
                nc.scalar.activation(sq[:, n % 4], y(h, c), ACT.Square).then_inc(squared, 1)
            for h in range(2):
                act.wait_ge(var_sb, h + 1)
                nc.scalar.activation(rstd[:, h], rstd[:, h], ACT.Sqrt).then_inc(std_done, 1)
            for n, (h, c) in enumerate(pieces):
                act.wait_ge(scaled, n + 1)
                nc.scalar.activation(y(h, c), y(h, c), ACT.Silu, bias=k.pv("conv_ln_b", c),
                                     scale=k.pv("conv_ln_g", c)).then_inc(activated, 1)

        @block.gpsimd
        def _(pool):
            for n, (h, c) in enumerate(pieces):
                pool.wait_ge(activated, n + 1)
                nc.gpsimd.tensor_copy(k.hT[:, 0, c, h * HALF:(h + 1) * HALF], y(h, c)).then_inc(high, 1)


def token_projection_stage(k, name, actT, gate_cols, out_dram=None, x_from=None):
    nc, w = k.nc, k.next_w
    with ExitStack() as ctx:
        ws = k.sb(f"{name}_ws", [P, 2, KC, D], F16, ctx=ctx)
        gate = k.sb(f"{name}_gate", [P, D], ctx=ctx)
        gated = k.sb(f"{name}_gated", [P, 2, D], ctx=ctx)
        gate_ps = k.ps(f"{name}_gate_ps", [P, D], ctx=ctx)
        acc = [k.ps(f"{name}_ps{i}", [P, D], ctx=ctx) for i in range(3)]
        gate_mm, gate_sb, high, low = (k.sem(f"{name}_{n}") for n in ("gate_mm", "gate_sb", "high", "low"))
        mm_done, gated_done, added, stored = (k.sem(f"{name}_{n}") for n in ("mm", "gated_done", "added", "stored"))
        x_in = k.sem(f"{name}_x_in")
        block = ctx.enter_context(nc.Block())

        @block.sync
        def _(sp):
            if x_from is not None:
                sp.dma_start(k.x_tok[:, :, :], x_from.rearrange("(t p) d -> p t d", p=P)).then_inc(x_in, 16)
            if out_dram is not None:
                for t in range(TT):
                    sp.wait_ge(added, t + 1)
                    sp.dma_start(out_dram[t * P:(t + 1) * P, :], k.x_tok[:, t, :]).then_inc(stored, 16)
                sp.wait_ge(stored, 16 * TT)

        @block.tensor
        def _(pe):
            for c in range(KC):
                last = nc.tensor.matmul(gate_ps[:, c * P:(c + 1) * P],
                                        lhsT=gate_cols[:, c:c + 1].to_broadcast([P, P]),
                                        rhs=k.const("ident"), start=True, stop=True)
            last.then_inc(gate_mm, 1)

            def products(t, c):
                for h in range(2):
                    last = product(nc, acc[t % 3][:, h * HALF:(h + 1) * HALF],
                                   part(actT, c, slice(t * P, (t + 1) * P)),
                                   part(ws, c, slice(h * HALF, (h + 1) * HALF)), c == 0, c == KC - 1)
                return last

            for c in range(KC):
                pe.wait_ge(high, c + 1)
                pe.wait_ge(low, c + 1)
                for t in range(3):
                    last = products(t, c)
                    if c == KC - 1:
                        last.then_inc(mm_done, 1)
            for t in range(3, TT):
                pe.wait_ge(gated_done, t - 2)
                for c in range(KC):
                    last = products(t, c)
                last.then_inc(mm_done, 1)

        @block.scalar
        def _(act):
            act.wait_ge(k.next_w_in, 16 * KC)
            for c in range(KC):
                high_part(nc, ws[:, 0, c, :], w[:, c, :]).then_inc(high, 1)
            act.wait_ge(gate_mm, 1)
            nc.scalar.activation(gate[:, :], gate_ps[:, :], ACT.Copy, scale=1.0 / W_UP).then_inc(gate_sb, 1)

        @block.vector
        def _(dve):
            for c in range(KC):
                dve.wait_ge(high, c + 1)
                low_part(nc, ws[:, 1, c, :], w[:, c, :], ws[:, 0, c, :]).then_inc(low, 1)
            dve.wait_ge(gate_sb, 1)
            for t in range(TT):
                dve.wait_ge(mm_done, t + 1)
                if t >= 2:
                    dve.wait_ge(added, t - 1)
                nc.vector.tensor_tensor(gated[:, t % 2], acc[t % 3][:, :], gate[:, :], ALU.mult) \
                    .then_inc(gated_done, 1)

        @block.gpsimd
        def _(pool):
            if x_from is not None:
                pool.wait_ge(x_in, 16)
            for t in range(TT):
                pool.wait_ge(gated_done, t + 1)
                nc.gpsimd.tensor_tensor(k.x_tok[:, t, :], k.x_tok[:, t, :], gated[:, t % 2], ALU.add) \
                    .then_inc(added, 1)


def router_stage(k):
    nc, ins = k.nc, k.ins
    NL = GROUPS + EXPERTS
    with ExitStack() as ctx:
        sb = lambda n, s, d=F32: k.sb(f"r_{n}", s, d, ctx=ctx)
        ws = sb("ws", [P, 2, KC, NL], F16)
        wr, br, rows = sb("w", [P, KC, NL]), sb("b", [P, NL]), sb("rows", [P, NL + SLOT_BLOCKS])
        tokid, zeros = sb("tokid", [P, TT]), sb("zeros", [SLOT_BLOCKS, P])
        lg, el, tmp = sb("lg", [P, TT, NL]), sb("el", [P, TT, EXPERTS]), sb("tmp", [P, TT, EXPERTS])
        oh1, oh2, mask = sb("oh1", [P, TT, EXPERTS]), sb("oh2", [P, TT, EXPERTS]), sb("mask", [P, TT, EXPERTS])
        goh, gex = sb("goh", [P, TT, GROUPS]), sb("gex", [P, TT, GROUPS])
        c1, m1, m2, e2, gp = (sb(n, [P, TT]) for n in ("c1", "m1", "m2", "e2", "gp"))
        cnt, nb, cum, start, one = (sb(n, [P, EXPERTS]) for n in ("cnt", "nb", "cum", "start", "one"))
        dfull = sb("dfull", [P, TT, EXPERTS])
        dest_f = sb("dest_f", [P, 2, TT])
        le = sb("le", [P, SLOT_BLOCKS, EXPERTS])
        bef, pr = sb("bef", [P, SLOT_BLOCKS]), sb("pr", [P, SLOT_BLOCKS // 2])
        prs = sb("prs", [P, 1])
        table = sb("table", [SLOT_BLOCKS, P])
        lg_ps = k.ps("r_lg_ps", [P, TT, 64], ctx=ctx)
        pos_ps = k.ps("r_pos_ps", [P, TT, EXPERTS], ctx=ctx)
        cnt_ps = k.ps("r_cnt_ps", [P, EXPERTS], ctx=ctx)
        tab_ps = k.ps("r_tab_ps", [P, SLOT_BLOCKS], ctx=ctx)
        r_in, lg_done, ex_in, ex_done, e2_in, e2_done = (k.sem(f"r_{n}") for n in (
            "in", "lg_done", "ex_in", "ex_done", "e2_in", "e2_done"))
        mask_ready, pos_done, dest_ready, zero_sb, zeroed, scattered, tab_in, tab_done, dve_step = (
            k.sem(f"r_{n}") for n in ("mask_ready", "pos_done", "dest_ready", "zero_sb", "zeroed", "scattered",
                                      "tab_in", "tab_done", "dve_step"))
        split = k.sem("r_split")
        desc_g, desc_e = rows[:, 0:GROUPS], rows[:, GROUPS:NL]
        viota = rows[:, NL:NL + SLOT_BLOCKS]
        block = ctx.enter_context(nc.Block())

        @block.sync
        def _(sp):
            sp.dma_start(wr[:, :, :], ins["router_w"].rearrange("(c p) n -> p c n", p=P)).then_inc(r_in, 16)
            sp.dma_start(br[:, :], ins["router_b"].partition_broadcast(P)).then_inc(r_in, 16)
            sp.dma_start(rows[:, :], ins["rows"].partition_broadcast(P)).then_inc(r_in, 16)
            sp.dma_start(tokid[:, :], ins["token_ids"]).then_inc(r_in, 16)
            sp.wait_ge(zero_sb, 1)
            sp.dma_start(k.table_dram.rearrange("(b p) o -> b (p o)", p=P), zeros[:, :]).then_inc(zeroed, 16)
            sp.wait_ge(scattered, 16 * 2 * TT)
            sp.dma_start(table[:, :], k.table_dram.rearrange("(b p) o -> b (p o)", p=P)).then_inc(tab_in, 16)

        @block.tensor
        def _(pe):
            pe.wait_ge(r_in, 64)
            pe.wait_ge(split, 2)
            for t in range(TT):
                for c in range(KC):
                    last = product(nc, lg_ps[:, t, 0:NL], part(k.hT, c, slice(t * P, (t + 1) * P)),
                                   part(ws, c), c == 0, c == KC - 1)
            last.then_inc(lg_done, 1)
            pe.wait_ge(mask_ready, 1)
            for t in range(TT):
                for j in range(t):
                    nc.tensor.matmul(pos_ps[:, t, :], lhsT=k.const("ones"), rhs=mask[:, j, :],
                                     start=j == 0, stop=False)
                nc.tensor.matmul(pos_ps[:, t, :], lhsT=k.const("before"), rhs=mask[:, t, :],
                                 start=t == 0, stop=True)
            for j in range(TT):
                last = nc.tensor.matmul(cnt_ps[:, :], lhsT=k.const("ones"), rhs=mask[:, j, :],
                                        start=j == 0, stop=j == TT - 1)
            last.then_inc(pos_done, 1)
            pe.wait_ge(tab_in, 16)
            nc.tensor.transpose(tab_ps[:, :], table[:, :], k.const("ident")[0:SLOT_BLOCKS, 0:SLOT_BLOCKS]) \
                .then_inc(tab_done, 1)

        @block.scalar
        def _(act):
            act.wait_ge(r_in, 64)
            high_part(nc, ws[:, 0], wr[:, :, :]).then_inc(split, 1)
            act.wait_ge(ex_in, 1)
            nc.scalar.activation(gex[:, :, :], gex[:, :, :], ACT.Exp).then_inc(ex_done, 1)
            act.wait_ge(e2_in, 1)
            nc.scalar.activation(e2[:, :], e2[:, :], ACT.Exp).then_inc(e2_done, 1)

        @block.vector
        def _(dve):
            step = chain(dve, dve_step)
            v = nc.vector

            def bc(x, n):
                return x.unsqueeze(len(x.shape)).to_broadcast([*x.shape, n])

            def first_max(scores, desc, n, top, onehot):
                step(v.tensor_reduce(top[:, :], scores, AX.X, ALU.max))
                step(v.tensor_tensor(onehot, scores, bc(top[:, :], n), ALU.is_equal))
                step(v.tensor_tensor(onehot, onehot, desc.unsqueeze(1).to_broadcast([P, TT, n]), ALU.mult))
                step(v.tensor_reduce(c1[:, :], onehot, AX.X, ALU.max))
                step(v.tensor_tensor(onehot, onehot, bc(c1[:, :], n), ALU.is_equal))

            step(v.memset(one[:, :], 1.0))
            v.memset(zeros[:, :], 0.0).then_inc(zero_sb, 1)
            dve.wait_ge(r_in, 64)
            dve.wait_ge(split, 1)
            low_part(nc, ws[:, 1].rearrange("p c n -> p (c n)"), wr[:, :, :].rearrange("p c n -> p (c n)"),
                     ws[:, 0].rearrange("p c n -> p (c n)")).then_inc(split, 1)
            dve.wait_ge(lg_done, 1)
            step(v.tensor_scalar(lg[:, :, :], lg_ps[:, :, 0:NL], 1.0 / W_UP, None, ALU.mult))
            step(v.tensor_tensor(lg[:, :, :], lg[:, :, :], br[:, :].unsqueeze(1).to_broadcast([P, TT, NL]), ALU.add))
            gl = lg[:, :, 0:GROUPS]
            first_max(gl, desc_g, GROUPS, m1, goh[:, :, :])
            v.tensor_tensor(gex[:, :, :], gl, bc(m1[:, :], GROUPS), ALU.subtract).then_inc(ex_in, 1)
            step(v.tensor_scalar(goh[:, :, :], goh[:, :, :], BIG, -BIG, ALU.mult, ALU.add))
            step(v.tensor_tensor(el[:, :, :].rearrange("p t (g e) -> p t g e", g=GROUPS),
                                 lg[:, :, GROUPS:NL].rearrange("p t (g e) -> p t g e", g=GROUPS),
                                 bc(goh[:, :, :], PER_GROUP), ALU.add))
            dve.wait_ge(ex_done, 1)
            step(v.tensor_reduce(gp[:, :], gex[:, :, :], AX.X, ALU.add))
            step(v.reciprocal(gp[:, :], gp[:, :]))
            first_max(el[:, :, :], desc_e, EXPERTS, m1, oh1[:, :, :])
            step(v.scalar_tensor_tensor(el[:, :, :], in0=oh1[:, :, :], scalar=-2 * BIG, in1=el[:, :, :],
                                        op0=ALU.mult, op1=ALU.add))
            first_max(el[:, :, :], desc_e, EXPERTS, m2, oh2[:, :, :])
            v.tensor_tensor(e2[:, :], m2[:, :], m1[:, :], ALU.subtract).then_inc(e2_in, 1)
            v.tensor_tensor(mask[:, :, :], oh1[:, :, :], oh2[:, :, :], ALU.add).then_inc(mask_ready, 1)
            dve.wait_ge(e2_done, 1)
            step(v.tensor_scalar(m1[:, :], e2[:, :], 1.0, None, ALU.add))
            step(v.reciprocal(m1[:, :], m1[:, :]))
            step(v.tensor_tensor(k.gates[:, 0, :], gp[:, :], m1[:, :], ALU.mult))
            step(v.tensor_tensor(k.gates[:, 1, :], k.gates[:, 0, :], e2[:, :], ALU.mult))
            dve.wait_ge(pos_done, 1)
            step(v.tensor_copy(cnt[:, :], cnt_ps[:, :]))
            step(v.tensor_scalar(nb[:, :], cnt[:, :], 0.0, None, ALU.is_gt))
            for m in range(1, S // P):
                step(v.scalar_tensor_tensor(nb[:, :], in0=cnt[:, :], scalar=float(m * P), in1=nb[:, :],
                                            op0=ALU.is_gt, op1=ALU.add))
            step(v.tensor_tensor_scan(cum[:, :], one[:, :], nb[:, :], 0.0, ALU.mult, ALU.add))
            step(v.tensor_tensor(start[:, :], cum[:, :], nb[:, :], ALU.subtract))
            step(v.tensor_scalar(start[:, :], start[:, :], float(P), None, ALU.mult))
            step(v.tensor_tensor(dfull[:, :, :], pos_ps[:, :, :],
                                 start[:, :].unsqueeze(1).to_broadcast([P, TT, EXPERTS]), ALU.add))
            for n, oh in enumerate((oh1, oh2)):
                step(v.tensor_tensor(tmp[:, :, :], oh[:, :, :], dfull[:, :, :], ALU.mult))
                step(v.tensor_reduce(dest_f[:, n, :], tmp[:, :, :], AX.X, ALU.add))
            v.tensor_copy(k.dest[:, :, :], dest_f[:, :, :]).then_inc(dest_ready, 1)
            step(v.tensor_tensor(le[:, :, :], cum[:, :].unsqueeze(1).to_broadcast([P, SLOT_BLOCKS, EXPERTS]),
                                 bc(viota, EXPERTS), ALU.is_le))
            step(v.tensor_reduce(bef[:, :], le[:, :, :], AX.X, ALU.add))
            step(v.tensor_scalar(bef[:, :], bef[:, :], float(EXPERTS - 1), None, ALU.min))
            step(v.tensor_copy(k.block_expert[:, :], bef[:, :]))
            step(v.tensor_scalar(pr[:, :], viota[:, 0:SLOT_BLOCKS // 2], 2.0, cum[:, EXPERTS - 1:EXPERTS],
                                 ALU.mult, ALU.is_lt))
            step(v.tensor_reduce(prs[:, :], pr[:, :], AX.X, ALU.add))
            step(v.tensor_scalar(prs[:, :], prs[:, :], -3.0, None, ALU.add))
            step(v.tensor_copy(k.pairs[:, :], prs[:, :]))
            dve.wait_ge(tab_done, 1)
            step(v.tensor_copy(k.slot_token[:, :], tab_ps[:, :]))

        @block.gpsimd
        def _(pool):
            pool.wait_ge(dest_ready, 1)
            pool.wait_ge(r_in, 64)
            pool.wait_ge(zeroed, 16)
            for n in range(2):
                for t in range(TT):
                    nc.gpsimd.indirect_dma_start(
                        out=k.table_dram, out_offset=bass.IndirectOffsetOnAxis(ap=k.dest[:, n, t:t + 1], axis=0),
                        in_=tokid[:, t:t + 1], in_offset=None).then_inc(scattered, 16)


def experts_stage(k):
    nc, ins = k.nc, k.ins
    gain, shift = k.gain[:, KC:2 * KC], k.mod[:, 3 * KC:4 * KC]
    FC = FFN // P
    least = 2 * S // P // 2
    with ExitStack() as ctx:
        sb = lambda n, s, d=F32: k.sb(f"m_{n}", s, d, ctx=ctx)
        wg, wu = sb("wg", [P, 2, KC, FFN]), sb("wu", [P, 2, KC, FFN])
        wd = sb("wd", [P, 2, FC, D])
        idx = sb("idx", [P, 2], U32)
        xg, xT = sb("xg", [P, 2, D]), sb("xT", [P, 2, KC, P])
        sg, hid, hidT, y = sb("sg", [P, FFN]), sb("hid", [P, FFN]), sb("hidT", [P, FC, P]), sb("y", [P, 2, D])
        xt_ps = [k.ps(f"m_xt{i}", [P, HALF], ctx=ctx) for i in range(2)]
        g_ps, u_ps, ht_ps = (k.ps(f"m_{n}_ps", [P, FFN], ctx=ctx) for n in ("g", "u", "ht"))
        y_ps = k.ps("m_y_ps", [P, D], ctx=ctx)
        two = lambda n: [k.sem(f"m_{n}{b}") for b in range(2)]
        g_in, u_in, d_in, x_in, y_stored = (two(n) for n in ("g_in", "u_in", "d_in", "x_in", "y_stored"))
        turn = k.sem("m_turn")
        idx_ready, xt_done, xt_sb, g_done, u_done, sg_done, hid_done, ht_done, ht_sb, y_done, y_act, y_dve = (
            k.sem(f"m_{n}") for n in ("idx_ready", "xt_done", "xt_sb", "g_done", "u_done", "sg_done",
                                      "hid_done", "ht_done", "ht_sb", "y_done", "y_act", "y_dve"))
        block = ctx.enter_context(nc.Block())

        def count(eng):
            return eng.value_load(k.pairs[0:1, 0:1], min_val=least - 3, max_val=SLOT_BLOCKS // 2 - 3) + 3

        @block.sync
        def _(sp):
            pairs = count(sp)

            def load(v, b, first):
                e = sp.value_load(k.block_expert[0:1, v:v + 1] if first else k.block_expert[0:1, bass.ds(v, 1)],
                                  min_val=0, max_val=EXPERTS - 1)
                if not first:
                    sp.wait_ge(g_done, v - 1)
                sp.dma_start(wg[:, b], ins["moe_w_gate"][bass.ds(e, 1)].rearrange("e (c p) n -> p (e c) n", p=P)) \
                    .then_inc(g_in[b], 16)
                if not first:
                    sp.wait_ge(u_done, v - 1)
                sp.dma_start(wu[:, b], ins["moe_w_up"][bass.ds(e, 1)].rearrange("e (c p) n -> p (e c) n", p=P)) \
                    .then_inc(u_in[b], 16)
                if not first:
                    sp.wait_ge(y_done, v - 1)
                sp.dma_start(wd[:, b], ins["moe_w_down"][bass.ds(e, 1)].rearrange("e (c p) n -> p (e c) n", p=P)) \
                    .then_inc(d_in[b], 16)

            for b in range(2):
                load(b, b, True)
            with sp.Fori(1, pairs) as i:
                for b in range(2):
                    load(2 * i + b, b, False)

        @block.gpsimd
        def _(pool):
            pairs = count(pool)

            def gather(column, b):
                nc.gpsimd.tensor_copy(idx[:, b:b + 1], column).then_inc(idx_ready, 1)

            def fetch(b):
                nc.gpsimd.indirect_dma_start(
                    out=xg[:, b, :], out_offset=None, in_=k.normed_dram,
                    in_offset=bass.IndirectOffsetOnAxis(ap=idx[:, b:b + 1], axis=0)).then_inc(x_in[b], 16)

            for b in range(2):
                gather(k.slot_token[:, b:b + 1], b)
                pool.wait_ge(idx_ready, b + 1)
                fetch(b)
            with pool.Fori(1, pairs) as i:
                for b in range(2):
                    pool.wait_ge(xt_done, 2 * i + b - 1)
                    gather(k.slot_token[:, bass.ds(2 * i + b, 1)], b)
                    pool.wait_ge(idx_ready, 2 * i + b + 1)
                    pool.sem_inc(turn, 1)
                    fetch(b)


        @block.tensor
        def _(pe):
            pairs = count(pe)

            def X(b, r):
                pe.wait_ge(x_in[b], 16 * r + 16)
                for c in range(KC):
                    last = nc.tensor.transpose(xt_ps[c // 4][:, (c % 4) * P:(c % 4 + 1) * P],
                                               xg[:, b, c * P:(c + 1) * P], k.const("ident"))
                last.then_inc(xt_done, 1)

            def G(n, b, r, first=False):
                pe.wait_ge(xt_sb, n + 1)
                pe.wait_ge(g_in[b], 16 * r + 16)
                if not first:
                    pe.wait_ge(sg_done, n)
                for c in range(KC):
                    last = nc.tensor.matmul(g_ps[:, :], lhsT=xT[:, b, c, :], rhs=wg[:, b, c, :],
                                            start=c == 0, stop=c == KC - 1)
                last.then_inc(g_done, 1)

            def U(b, r):
                pe.wait_ge(u_in[b], 16 * r + 16)
                for c in range(KC):
                    last = nc.tensor.matmul(u_ps[:, :], lhsT=xT[:, b, c, :], rhs=wu[:, b, c, :],
                                            start=c == 0, stop=c == KC - 1)
                last.then_inc(u_done, 1)

            def H(n):
                pe.wait_ge(hid_done, n + 1)
                for c in range(FC):
                    last = nc.tensor.transpose(ht_ps[:, c * P:(c + 1) * P], hid[:, c * P:(c + 1) * P],
                                               k.const("ident"))
                last.then_inc(ht_done, 1)

            def Y(n, b, r, first=False):
                pe.wait_ge(ht_sb, n + 1)
                pe.wait_ge(d_in[b], 16 * r + 16)
                if not first:
                    pe.wait_ge(y_act, n)
                    pe.wait_ge(y_dve, n)
                for h in range(2):
                    for c in range(FC):
                        last = nc.tensor.matmul(y_ps[:, h * HALF:(h + 1) * HALF], lhsT=hidT[:, c, :],
                                                rhs=wd[:, b, c, h * HALF:(h + 1) * HALF],
                                                start=c == 0, stop=c == FC - 1)
                last.then_inc(y_done, 1)

            X(0, 0)
            G(0, 0, 0, first=True)
            X(1, 0)
            U(0, 0)
            G(1, 1, 0)
            H(0)
            X(0, 1)
            U(1, 0)
            Y(0, 0, 0, first=True)
            with pe.Fori(1, pairs - 1) as i:
                for b in range(2):
                    n = 2 * i + b
                    G(n, b, i)
                    H(n - 1)
                    X(1 - b, i + b)
                    U(b, i)
                    Y(n - 1, 1 - b, i - 1 + b)
            n, i = 2 * (pairs - 1), pairs - 1
            G(n, 0, i)
            H(n - 1)
            X(1, i)
            U(0, i)
            Y(n - 1, 1, i - 1)
            G(n + 1, 1, i)
            H(n)
            U(1, i)
            Y(n, 0, i)
            H(n + 1)
            Y(n + 1, 1, i)

        @block.scalar
        def _(act):
            pairs = count(act)

            def silu(n, first=False):
                act.wait_ge(g_done, n + 1)
                if not first:
                    act.wait_ge(hid_done, n)
                nc.scalar.activation(sg[:, :], g_ps[:, :], ACT.Silu).then_inc(sg_done, 1)

            def hidden(n):
                act.wait_ge(ht_done, n + 1)
                nc.scalar.copy(hidT[:, :, :], ht_ps[:, :].rearrange("p (c q) -> p c q", q=P)).then_inc(ht_sb, 1)

            def out(n, b, r, first=False):
                act.wait_ge(y_done, n + 1)
                if not first:
                    act.wait_ge(y_stored[b], 32 * r)
                nc.scalar.copy(y[:, b, 0:HALF], y_ps[:, 0:HALF]).then_inc(y_act, 1)
                rows = slice(n * P, (n + 1) * P) if first else bass.ds(n * P, P)
                act.wait_ge(y_act, n + 1)
                act.dma_start(k.slot_out[rows, 0:HALF], y[:, b, 0:HALF]).then_inc(y_stored[b], 16)
                act.wait_ge(y_dve, n + 1)
                act.dma_start(k.slot_out[rows, HALF:D], y[:, b, HALF:D]).then_inc(y_stored[b], 16)

            silu(0, first=True)
            silu(1)
            hidden(0)
            out(0, 0, 0, first=True)
            silu(2)
            hidden(1)
            out(1, 1, 0, first=True)
            silu(3)
            hidden(2)
            out(2, 0, 1)
            with act.Fori(2, pairs) as i:
                for b in range(2):
                    n = 2 * i + b
                    silu(n)
                    hidden(n - 1)
                    out(n - 1, 1 - b, i - 1 + b)
            n = 2 * pairs - 1
            hidden(n)
            out(n, 1, pairs - 1)
            for b in range(2):
                act.wait_ge(y_stored[b], 32 * pairs)
            act.sem_inc(turn, 1)

        @block.vector
        def _(dve):
            pairs = count(dve)

            def turned(n, b):
                dve.wait_ge(xt_done, n + 1)
                for c in range(KC):
                    last = nc.vector.tensor_scalar(xT[:, b, c, :], xt_ps[c // 4][:, (c % 4) * P:(c % 4 + 1) * P],
                                                   gain[:, c:c + 1], shift[:, c:c + 1], ALU.mult, ALU.add)
                last.then_inc(xt_sb, 1)

            def hidden(n):
                dve.wait_ge(sg_done, n + 1)
                dve.wait_ge(u_done, n + 1)
                nc.vector.tensor_tensor(hid[:, :], sg[:, :], u_ps[:, :], ALU.mult).then_inc(hid_done, 1)

            def out(n, b, r, first=False):
                dve.wait_ge(y_done, n + 1)
                if not first:
                    dve.wait_ge(y_stored[b], 32 * r)
                nc.vector.tensor_copy(y[:, b, HALF:D], y_ps[:, HALF:D]).then_inc(y_dve, 1)

            turned(0, 0)
            turned(1, 1)
            hidden(0)
            turned(2, 0)
            hidden(1)
            out(0, 0, 0, first=True)
            turned(3, 1)
            hidden(2)
            out(1, 1, 0, first=True)
            turned(4, 0)
            hidden(3)
            out(2, 0, 1)
            with dve.Fori(2, pairs - 1) as i:
                for b in range(2):
                    n = 2 * i + b
                    turned(n + 1, 1 - b)
                    hidden(n)
                    out(n - 1, 1 - b, i - 1 + b)
            n, i = 2 * (pairs - 1), pairs - 1
            turned(n + 1, 1)
            hidden(n)
            out(n - 1, 1, i - 1)
            hidden(n + 1)
            out(n, 0, i)
            out(n + 1, 1, i)


def combine_stage(k):
    nc, ins = k.nc, k.ins
    with ExitStack() as ctx:
        sb = lambda n, s, d=F32: k.sb(f"b_{n}", s, d, ctx=ctx)
        rows = sb("rows", [P, 2, 2, D])
        part = sb("part", [P, 2, D])
        gate, final = sb("gate", [P, D]), sb("final", [P, D])
        sq, ss = sb("sq", [P, 2, D]), sb("ss", [P, TT])
        gate_ps = k.ps("b_gate_ps", [P, D], ctx=ctx)
        gate_mm, gate_sb, f_in, summed, added, squared, var, std, dve_step = (k.sem(f"b_{n}") for n in (
            "gate_mm", "gate_sb", "f_in", "summed", "added", "squared", "var", "std", "dve_step"))
        row_in = [k.sem(f"b_row_in{b}") for b in range(2)]
        rows_used = k.sem("b_rows_used")
        block = ctx.enter_context(nc.Block())

        @block.sync
        def _(sp):
            sp.dma_start(final[:, :], ins["final_g"].partition_broadcast(P)).then_inc(f_in, 16)

        @block.gpsimd
        def _(pool):
            def gather(t):
                if t >= 2:
                    pool.wait_ge(rows_used, t - 1)
                for n in range(2):
                    nc.gpsimd.indirect_dma_start(
                        out=rows[:, t % 2, n, :], out_offset=None, in_=k.slot_out,
                        in_offset=bass.IndirectOffsetOnAxis(ap=k.dest[:, n, t:t + 1], axis=0)).then_inc(row_in[t % 2], 16)
            gather(0)
            for t in range(TT):
                if t + 1 < TT:
                    gather(t + 1)
                pool.wait_ge(summed, t + 1)
                nc.gpsimd.tensor_tensor(k.x_tok[:, t, :], k.x_tok[:, t, :], part[:, t % 2], ALU.add).then_inc(added, 1)

        @block.tensor
        def _(pe):
            for c in range(KC):
                last = nc.tensor.matmul(gate_ps[:, c * P:(c + 1) * P],
                                        lhsT=k.mod[:, 5 * KC + c:5 * KC + c + 1].to_broadcast([P, P]),
                                        rhs=k.const("ident"), start=True, stop=True)
            last.then_inc(gate_mm, 1)

        @block.scalar
        def _(act):
            act.wait_ge(gate_mm, 1)
            nc.scalar.copy(gate[:, :], gate_ps[:, :]).then_inc(gate_sb, 1)
            for t in range(TT):
                act.wait_ge(added, t + 1)
                if t >= 2:
                    act.wait_ge(squared, t - 1)
                nc.scalar.activation(sq[:, t % 2], k.x_tok[:, t, :], ACT.Square,
                                     accum_out=ss[:, t:t + 1]).then_inc(squared, 1)
            act.wait_ge(var, 1)
            nc.scalar.activation(ss[:, :], ss[:, :], ACT.Sqrt).then_inc(std, 1)

        @block.vector
        def _(dve):
            step = chain(dve, dve_step)
            dve.wait_ge(gate_sb, 1)
            for t in range(TT):
                dve.wait_ge(row_in[t % 2], 32 * (t // 2 + 1))
                if t >= 2:
                    dve.wait_ge(added, t - 1)
                r = rows[:, t % 2]
                step(nc.vector.tensor_scalar(r[:, 0, :], r[:, 0, :], k.gates[:, 0, t:t + 1], None, ALU.mult))
                step(nc.vector.scalar_tensor_tensor(r[:, 0, :], in0=r[:, 1, :], scalar=k.gates[:, 1, t:t + 1],
                                                    in1=r[:, 0, :], op0=ALU.mult, op1=ALU.add))
                last = nc.vector.tensor_tensor(part[:, t % 2], r[:, 0, :], gate[:, :], ALU.mult)
                last.then_inc(summed, 1)
                dve.wait_ge(summed, t + 1)
                dve.sem_inc(rows_used, 1)
            dve.wait_ge(squared, TT)
            nc.vector.tensor_scalar(ss[:, :], ss[:, :], 1.0 / D, EPS, ALU.mult, ALU.add).then_inc(var, 1)
            dve.wait_ge(std, 1)
            step(nc.vector.reciprocal(ss[:, :], ss[:, :]))
            dve.wait_ge(f_in, 16)
            for t in range(TT):
                nc.vector.scalar_tensor_tensor(k.x_tok[:, t, :], in0=k.x_tok[:, t, :], scalar=ss[:, t:t + 1],
                                               in1=final[:, :], op0=ALU.mult, op1=ALU.mult)


def alloc_routing(k, ctx):
    k.dest = k.sb("dest", [P, 2, TT], U32, ctx=ctx)
    k.gates = k.sb("gates", [P, 2, TT], ctx=ctx)
    k.slot_token = k.sb("slot_token", [P, SLOT_BLOCKS], U32, ctx=ctx)
    k.block_expert = k.sb("block_expert", [P, SLOT_BLOCKS], I32, ctx=ctx)
    k.pairs = k.sb("pairs", [P, 1], I32, ctx=ctx)
    k.normed_dram = k.nc.dram_tensor("normed_tokens", (S, D), F32, kind="Internal").ap()
    k.table_dram = k.nc.dram_tensor("slot_table", (SLOT_BLOCKS * P, 1), F32, kind="Internal").ap()
    k.slot_out = k.nc.dram_tensor("slot_out", (SLOT_BLOCKS * P, D), F32, kind="Internal").ap()


QK_HEADS = HEADS + KV_HEADS
TOKEN_COLS = 1536 + 356
ROPE_A, ROPE_I = HD // 4 // 2, IDX_DIM // 4 // 2


def qkv_stage(k):
    nc, ins = k.nc, k.ins
    with ExitStack() as ctx:
        sb = lambda n, s, d=F32: k.sb(f"q_{n}", s, d, ctx=ctx)
        w_q, w_rest = (x[:, :, :].bitcast(F16).rearrange("p c (s n) -> p s c n", s=2) for x in (k.g_att, k.z_att))
        raw = sb("raw", [P, 2, TOKEN_COLS])
        sq = sb("sq", [P, QK_HEADS * HD])
        gq = sb("gq", [P, 2, HD])
        lnr = sb("lnr", [P, 2, IDX_DIM])
        pos_i, pos = sb("pos_i", [P, TT], I32), sb("pos", [P, TT])
        nf = ROPE_A + ROPE_I
        freq, ang, turns = sb("freq", [P, nf]), sb("ang", [P, TT, nf]), sb("turns", [P, TT, nf])
        sin, cos = sb("sin", [P, TT, nf]), sb("cos", [P, TT, nf])
        ss, mu = sb("ss", [P, 2, QK_HEADS + 1]), sb("mu", [P, 2])
        kc_, kd, ksq = sb("kc", [P, 2, IDX_DIM]), sb("kd", [P, 2, 2, IDX_DIM]), sb("ksq", [P, IDX_DIM])
        ra, rb, rc, rd = (sb(f"rot{n}", [P, QK_HEADS, ROPE_A]) for n in range(4))
        mm = [k.ps(f"q_mm{i}", [P, HALF], ctx=ctx) for i in range(4)]
        tp = [k.ps(f"q_tp{i}", [P, HALF], ctx=ctx) for i in range(4)]
        w_in, high, low = [k.sem(f"q_w_in{n}") for n in range(2)], k.sem("q_high"), k.sem("q_low")
        rest = TOKEN_COLS - S
        small_in, mm_done, raw_done, tr_done, tr_out = (k.sem(f"q_{n}") for n in (
            "small_in", "mm_done", "raw_done", "tr_done", "tr_out"))
        sq_done, var, std, scaled, gained, ready, ang_ready, trig, dve_step, pool_step = (k.sem(f"q_{n}") for n in (
            "sq_done", "var", "std", "scaled", "gained", "ready", "ang_ready", "trig", "dve_step", "pool_step"))
        spans = [(0, 512), (512, 1024), (1024, 1536), (1536, TOKEN_COLS)]
        evac = (1, 2, 4, 5)
        block = ctx.enter_context(nc.Block())

        @block.sync
        def _(sp):
            sp.dma_start(pos_i[:, :], ins["positions"]).then_inc(small_in, 16)
            sp.dma_start(freq[:, :], ins["freq"].partition_broadcast(P)).then_inc(small_in, 16)
            sp.dma_start(gq[:, 0, :], ins["q_norm_g"].partition_broadcast(P)).then_inc(small_in, 16)
            sp.dma_start(gq[:, 1, :], ins["k_norm_g"].partition_broadcast(P)).then_inc(small_in, 16)
            sp.dma_start(lnr[:, 0, :], ins["idx_ln_g"].partition_broadcast(P)).then_inc(small_in, 16)
            sp.dma_start(lnr[:, 1, :], ins["idx_ln_b"].partition_broadcast(P)).then_inc(small_in, 16)
            for c in range(KC):
                if c >= 2:
                    sp.wait_ge(high, c - 1)
                    sp.wait_ge(low, c - 1)
                sp.dma_start(raw[:, c % 2, :], ins["w_tok"][c * P:(c + 1) * P, :]).then_inc(w_in[c % 2], 16)

        @block.tensor
        def _(pe):
            def transposes(t):
                pe.wait_ge(ready, t + 1)
                if t:
                    pe.wait_ge(tr_out, 4 * t)
                s = t % 2
                for n in range(13):
                    src = raw[:, s, n * HD:(n + 1) * HD] if n < 10 else \
                        raw[:, s, 1536 + (n - 10) * P:1536 + (n - 9) * P] if n < 12 else \
                        kd[:, s].rearrange("p a d -> p (a d)")
                    last = nc.tensor.transpose(tp[n // 4][:, (n % 4) * P:(n % 4 + 1) * P], src, k.const("ident"))
                    if n % 4 == 3 or n == 12:
                        last.then_inc(tr_done, 1)

            for t in range(TT):
                for n, (a, b) in enumerate(spans):
                    w_n = w_q[:, :, :, a:b] if n < 2 else w_rest[:, :, :, a - S:b - S]
                    if t:
                        pe.wait_ge(raw_done, 5 * (t - 1) + evac[n])
                    for c in range(KC):
                        if t == 0 and n == 0:
                            pe.wait_ge(high, c + 1)
                            pe.wait_ge(low, c + 1)
                        last = product(nc, mm[n][:, 0:b - a], part(k.hT, c, slice(t * P, (t + 1) * P)),
                                       part(w_n, c), c == 0, c == KC - 1)
                    last.then_inc(mm_done, 1)
                if t:
                    transposes(t - 1)
            transposes(TT - 1)

        @block.scalar
        def _(act):
            for c in range(KC):
                act.wait_ge(w_in[c % 2], 16 * (c // 2 + 1))
                high_part(nc, w_q[:, 0, c, :], raw[:, c % 2, 0:S])
                high_part(nc, w_rest[:, 0, c, 0:rest], raw[:, c % 2, S:TOKEN_COLS]).then_inc(high, 1)
            act.wait_ge(ang_ready, 1)
            nc.scalar.activation(sin[:, :, :], sin[:, :, :], ACT.Sin)
            nc.scalar.activation(cos[:, :, :], cos[:, :, :], ACT.Sin).then_inc(trig, 1)

            def out(t):
                span = slice(t * P, (t + 1) * P)
                for n, (dst, width) in enumerate((
                        (k.qT[:, 0:4, span], 4), (k.qT[:, 4:8, span], 4), (None, 4), (k.kidxT[:, span], 1))):
                    act.wait_ge(tr_done, 4 * t + n + 1)
                    src = tp[n][:, 0:width * P]
                    if n == 2:
                        r = src.rearrange("p (a q) -> p a q", q=P)
                        nc.scalar.copy(k.kT[:, :, span], r[:, 0:2, :])
                        last = nc.scalar.copy(k.qidxT[:, :, span], r[:, 2:4, :])
                    elif n == 3:
                        last = nc.scalar.copy(dst, src)
                    else:
                        last = nc.scalar.copy(dst, src.rearrange("p (a q) -> p a q", q=P))
                    last.then_inc(tr_out, 1)

            act.wait_ge(low, KC)
            for t in range(TT):
                if t >= 2:
                    act.wait_ge(tr_done, 4 * (t - 1))
                for n, (a, b) in enumerate(spans):
                    act.wait_ge(mm_done, 4 * t + n + 1)
                    if n == 2:
                        nc.scalar.activation(raw[:, t % 2, a:a + 256], mm[n][:, 0:256], ACT.Copy,
                                             scale=1.0 / W_UP).then_inc(raw_done, 1)
                        nc.scalar.activation(k.v_tok[:, t, :], mm[n][:, 256:512], ACT.Copy,
                                             scale=1.0 / W_UP).then_inc(raw_done, 1)
                    else:
                        nc.scalar.activation(raw[:, t % 2, a:b], mm[n][:, 0:b - a], ACT.Copy,
                                             scale=1.0 / W_UP).then_inc(raw_done, 1)
                act.wait_ge(var, t + 1)
                nc.scalar.activation(ss[:, t % 2], ss[:, t % 2], ACT.Sqrt).then_inc(std, 1)
                if t:
                    out(t - 1)
            out(TT - 1)

        @block.gpsimd
        def _(pool):
            pool.wait_ge(small_in, 96)
            for t in range(TT):
                qk = raw[:, t % 2, 0:QK_HEADS * HD]
                pool.wait_ge(raw_done, 5 * t + 3)
                if t:
                    pool.wait_ge(var, t)
                nc.gpsimd.tensor_tensor(sq[:, :], qk, qk, ALU.mult).then_inc(sq_done, 1)
                pool.wait_ge(scaled, t + 1)
                heads = qk.rearrange("p (h d) -> p h d", d=HD)
                for n, (a, b) in enumerate(((0, HEADS), (HEADS, QK_HEADS))):
                    nc.gpsimd.tensor_tensor(heads[:, a:b, :], heads[:, a:b, :],
                                            gq[:, n, :].unsqueeze(1).to_broadcast([P, b - a, HD]), ALU.mult) \
                        .then_inc(gained, 1)

        @block.vector
        def _(dve):
            step = chain(dve, dve_step)
            v = nc.vector
            for c in range(KC):
                dve.wait_ge(high, c + 1)
                low_part(nc, w_q[:, 1, c, :], raw[:, c % 2, 0:S], w_q[:, 0, c, :])
                low_part(nc, w_rest[:, 1, c, 0:rest], raw[:, c % 2, S:TOKEN_COLS],
                         w_rest[:, 0, c, 0:rest]).then_inc(low, 1)
            dve.wait_ge(small_in, 96)
            step(v.tensor_copy(pos[:, :], pos_i[:, :]))
            step(v.tensor_tensor(ang[:, :, :], pos[:, :].unsqueeze(2).to_broadcast([P, TT, nf]),
                                 freq[:, :].unsqueeze(1).to_broadcast([P, TT, nf]), ALU.mult))
            step(v.tensor_scalar(turns[:, :, :], ang[:, :, :], float(1 / (2 * np.pi)), None, ALU.mult))
            step(v.tensor_scalar(turns[:, :, :], turns[:, :, :], 12582912.0, None, ALU.add))
            step(v.tensor_scalar(turns[:, :, :], turns[:, :, :], -12582912.0, None, ALU.add))
            c1 = 6.28125
            c2 = float(np.float32(np.round((2 * np.pi - c1) * 2 ** 21) / 2 ** 21))
            for part in (c1, c2, 2 * np.pi - c1 - c2):
                step(v.scalar_tensor_tensor(ang[:, :, :].rearrange("p t f -> p (t f)"),
                                            in0=turns[:, :, :].rearrange("p t f -> p (t f)"), scalar=float(-part),
                                            in1=ang[:, :, :].rearrange("p t f -> p (t f)"),
                                            op0=ALU.mult, op1=ALU.add))
            step(v.tensor_scalar(sin[:, :, :], ang[:, :, :], 3.1415925, -3.1415925, ALU.min, ALU.max))
            step(v.scalar_tensor_tensor(cos[:, :, :].rearrange("p t f -> p (t f)"),
                                        in0=sin[:, :, :].rearrange("p t f -> p (t f)"), scalar=-1.0,
                                        in1=sin[:, :, :].rearrange("p t f -> p (t f)"), op0=ALU.mult, op1=ALU.max))
            v.tensor_scalar(cos[:, :, :], cos[:, :, :], -1.0, float(np.pi / 2), ALU.mult, ALU.add).then_inc(ang_ready, 1)
            dve.wait_ge(trig, 1)

            def rope(x, heads, half, at, t):
                cs = cos[:, t, at:at + half].unsqueeze(1).to_broadcast([P, heads, half])
                sn = sin[:, t, at:at + half].unsqueeze(1).to_broadcast([P, heads, half])
                x1, x2 = x[:, :, 0:half], x[:, :, half:2 * half]
                a, b, c, d = (r[:, 0:heads, 0:half] for r in (ra, rb, rc, rd))
                v.tensor_tensor(a, x1, cs, ALU.mult)
                v.tensor_tensor(b, x2, sn, ALU.mult)
                v.tensor_tensor(c, x2, cs, ALU.mult)
                step(v.tensor_tensor(d, x1, sn, ALU.mult))
                v.tensor_tensor(x1, a, b, ALU.subtract)
                step(v.tensor_tensor(x2, c, d, ALU.add))

            for t in range(TT):
                s = t % 2
                r = raw[:, s, :]
                heads = r[:, 0:QK_HEADS * HD].rearrange("p (h d) -> p h d", d=HD)
                qi = r[:, 1536:1792].rearrange("p (h d) -> p h d", d=IDX_DIM)
                ki = r[:, 1792:1856]
                dve.wait_ge(raw_done, 5 * t + 5)
                step(v.tensor_scalar(k.widx[:, t, :], r[:, 1856:1860], float(IDX_HEADS ** -0.5 * IDX_DIM ** -0.5),
                                     None, ALU.mult))
                v.tensor_copy(k.dt_raw[:, t, :], r[:, 1860:1892])
                step(v.tensor_reduce(mu[:, s:s + 1], ki, AX.X, ALU.add))
                step(v.tensor_scalar(mu[:, s:s + 1], mu[:, s:s + 1], -1.0 / IDX_DIM, None, ALU.mult))
                step(v.tensor_scalar(kc_[:, s], ki, mu[:, s:s + 1], None, ALU.add))
                step(v.tensor_tensor(ksq[:, :], kc_[:, s], kc_[:, s], ALU.mult))
                step(v.tensor_reduce(ss[:, s, 10:11], ksq[:, :], AX.X, ALU.add))
                step(v.tensor_scalar(ss[:, s, 10:11], ss[:, s, 10:11], 1.0 / IDX_DIM, EPS, ALU.mult, ALU.add))
                dve.wait_ge(sq_done, t + 1)
                step(v.tensor_reduce(ss[:, s, 0:10], sq[:, :].rearrange("p (h d) -> p h d", d=HD), AX.X, ALU.add))
                v.tensor_scalar(ss[:, s, 0:10], ss[:, s, 0:10], 1.0 / HD, EPS, ALU.mult, ALU.add).then_inc(var, 1)
                dve.wait_ge(std, t + 1)
                step(v.reciprocal(ss[:, s], ss[:, s]))
                v.tensor_tensor(heads, heads, ss[:, s, 0:10].unsqueeze(2).to_broadcast([P, QK_HEADS, HD]),
                                ALU.mult).then_inc(scaled, 1)
                step(v.scalar_tensor_tensor(kc_[:, s], in0=kc_[:, s], scalar=ss[:, s, 10:11], in1=lnr[:, 0, :],
                                            op0=ALU.mult, op1=ALU.mult))
                step(v.tensor_tensor(kc_[:, s], kc_[:, s], lnr[:, 1, :], ALU.add))
                rope(kc_[:, s].unsqueeze(1), 1, ROPE_I, ROPE_A, t)
                rope(qi, IDX_HEADS, ROPE_I, ROPE_A, t)
                if t >= 2:
                    dve.wait_ge(tr_done, 4 * (t - 1))
                step(v.tensor_copy(kd[:, s], kc_[:, s].unsqueeze(1).to_broadcast([P, 2, IDX_DIM])))
                dve.wait_ge(gained, 2 * t + 2)
                rope(heads, QK_HEADS, ROPE_A, 0, t)
                dve.sem_inc(ready, 1)


def causal(b):
    n = (b + 1) * P
    return n, b * (b + 1) // 2 * P


def select_stage(k):
    nc, ins = k.nc, k.ins
    first = TOPK // P
    NEVER = -3.0e38
    with ExitStack() as ctx:
        sb = lambda n, s, d=F32: k.sb(f"s_{n}", s, d, ctx=ctx)
        w, scaled = sb("w", [P, 2, KC, P]), k.sem("s_scaled")
        ws = sb("ws", [P, 2, 2, KC, P], F16)
        high, low = k.sem("s_high"), k.sem("s_low")
        rl, work, best = sb("rl", [P, 2, S]), sb("work", [P, 2, S]), sb("best", [P, 2, 8])
        future = sb("future", [P, P])
        sc_ps = [k.ps(f"s_sc{i}", [P, S], ctx=ctx) for i in range(2)]
        pj_ps = [k.ps(f"s_pj{i}", [P, S], ctx=ctx) for i in range(2)]
        w_in = [k.sem(f"s_w_in{i}") for i in range(2)]
        pj_done, pj_out, sc_done, relu, used, scored, picked, fut, dve_step, pool_step = (k.sem(f"s_{n}") for n in (
            "pj_done", "pj_out", "sc_done", "relu", "used", "scored", "picked", "fut", "dve_step", "pool_step"))
        blocks = list(range(first, TT))
        jobs = [(dst, func, n) for dst, func in ((k.z_att, ACT.Silu), (k.g_att, ACT.Sigmoid)) for n in range(KC)]
        share = [range(16 * i // len(blocks), 16 * (i + 1) // len(blocks)) for i in range(len(blocks))]
        block = ctx.enter_context(nc.Block())

        @block.sync
        def _(sp):
            for j in range(len(jobs)):
                if j >= 2:
                    sp.wait_ge(low, j - 1)
                sp.dma_start(w[:, j % 2], ins["w_gates"][j]).then_inc(w_in[j % 2], 16)

        @block.tensor
        def _(pe):
            for i, b in enumerate(blocks):
                n, _ = causal(b)
                for h in range(IDX_HEADS):
                    m = i * IDX_HEADS + h
                    if m >= 2:
                        pe.wait_ge(relu, m - 1)
                    rows = slice(IDX_DIM * (h % 2), IDX_DIM * (h % 2 + 1))
                    for a in range(0, n, HALF):
                        e = min(n, a + HALF)
                        last = nc.tensor.matmul(sc_ps[m % 2][:, a:e], lhsT=k.qidxT[rows, h // 2, b * P:(b + 1) * P],
                                                rhs=k.kidxT[rows, a:e], start=True, stop=True)
                    last.then_inc(sc_done, 1)
                for j in share[i]:
                    pe.wait_ge(high, j + 1)
                    pe.wait_ge(low, j + 1)
                    if j >= 2:
                        pe.wait_ge(pj_out, j - 1)
                    for a in range(0, S, HALF):
                        for c in range(KC):
                            last = product(nc, pj_ps[j % 2][:, a:a + HALF], part(ws, j % 2, c),
                                           part(k.hT, c, slice(a, a + HALF)), c == 0, c == KC - 1)
                    last.then_inc(pj_done, 1)

        @block.scalar
        def _(act):
            def split(j):
                act.wait_ge(w_in[j % 2], 16 * (j // 2 + 1))
                high_part(nc, w[:, j % 2], w[:, j % 2]).then_inc(scaled, 1)
                if j >= 2:
                    act.wait_ge(pj_done, j - 1)
                act.wait_ge(scaled, j + 1)
                nc.scalar.copy(ws[:, 0, j % 2], w[:, j % 2]).then_inc(high, 1)

            split(0)
            for i, b in enumerate(blocks):
                n, _ = causal(b)
                for h in range(IDX_HEADS):
                    m = i * IDX_HEADS + h
                    act.wait_ge(sc_done, m + 1)
                    if m >= 2:
                        act.wait_ge(used, m - 1)
                    nc.scalar.activation(rl[:, m % 2, 0:n], sc_ps[m % 2][:, 0:n], ACT.Relu).then_inc(relu, 1)
                for j in share[i]:
                    dst, func, n_ = jobs[j]
                    if j + 1 < len(jobs):
                        split(j + 1)
                    act.wait_ge(pj_done, j + 1)
                    nc.scalar.activation(dst[:, n_, :], pj_ps[j % 2][:, :], func, scale=1.0 / W_UP).then_inc(pj_out, 1)

        @block.gpsimd
        def _(pool):
            step = chain(pool, pool_step)
            nc.gpsimd.tensor_scalar(future[:, :], k.const("before"), -BIG, None, ALU.mult).then_inc(fut, 1)
            pool.wait_ge(fut, 1)

            def split(j):
                pool.wait_ge(high, j + 1)
                nc.gpsimd.tensor_tensor(ws[:, 1, j % 2], w[:, j % 2], ws[:, 0, j % 2], ALU.subtract) \
                    .then_inc(low, 1)

            split(0)
            for i, b in enumerate(blocks):
                n, _ = causal(b)
                wk = work[:, i % 2, 0:n]
                if i >= 2:
                    pool.wait_ge(picked, i - 1)
                for h in range(IDX_HEADS):
                    m = i * IDX_HEADS + h
                    pool.wait_ge(relu, m + 1)
                    r = rl[:, m % 2, 0:n]
                    if h == 0:
                        nc.gpsimd.tensor_scalar(wk, r, k.widx[:, b, h:h + 1], None, ALU.mult).then_inc(used, 1)
                    else:
                        step(nc.gpsimd.tensor_scalar(r, r, k.widx[:, b, h:h + 1], None, ALU.mult))
                        nc.gpsimd.tensor_tensor(wk, wk, r, ALU.add).then_inc(used, 1)
                    pool.wait_ge(used, m + 1)
                nc.gpsimd.tensor_tensor(work[:, i % 2, b * P:n], work[:, i % 2, b * P:n], future[:, :],
                                        ALU.add).then_inc(scored, 1)
                for j in share[i]:
                    if j + 1 < len(jobs):
                        split(j + 1)

        @block.vector
        def _(dve):
            step = chain(dve, dve_step)
            v = nc.vector
            dve.wait_ge(fut, 1)
            for b in range(first):
                n, at = causal(b)
                if b:
                    v.memset(k.bias[:, at:at + b * P], 0.0)
                v.tensor_copy(k.bias[:, at + b * P:at + n], future[:, :])
            for i, b in enumerate(blocks):
                n, at = causal(b)
                wk = work[:, i % 2, 0:n]
                dve.wait_ge(scored, i + 1)
                for r in range(TOPK // 8):
                    step(v.max(best[:, r % 2], wk))
                    step(v.match_replace(wk, best[:, r % 2], wk, NEVER))
                v.tensor_scalar(k.bias[:, at:at + n], wk, NEVER / 2, -BIG, ALU.is_gt, ALU.mult).then_inc(picked, 1)
            dve.wait_ge(picked, len(blocks))


def attention_stage(k):
    nc = k.nc
    scale = float(HD ** -0.5)
    with ExitStack() as ctx:
        sb = lambda n, s, d=F32: k.sb(f"a_{n}", s, d, ctx=ctx)
        sm, pT = sb("sm", [P, 2, S]), sb("pT", [P, 2, S])
        mx, nb, rs = sb("mx", [P, 2]), sb("nb", [P, 2]), sb("rs", [P, 2])
        s_ps = [k.ps(f"a_s{i}", [P, S], ctx=ctx) for i in range(2)]
        t_ps = k.ps("a_t", [P, S], ctx=ctx)
        o_ps = [k.ps(f"a_o{i}", [P, P], ctx=ctx) for i in range(2)]
        s_done, masked, neg, exped, scaled, t_done, t_out, o_done, o_out, dve_step = (k.sem(f"a_{n}") for n in (
            "s_done", "masked", "neg", "exped", "scaled", "t_done", "t_out", "o_done", "o_out", "dve_step"))
        jobs = [(b, h) for b in range(TT) for h in range(HEADS)]
        block = ctx.enter_context(nc.Block())

        @block.tensor
        def _(pe):
            def scores(m):
                b, h = jobs[m]
                n, _ = causal(b)
                if m >= 2:
                    pe.wait_ge(masked, m - 1)
                for a in range(0, n, HALF):
                    e = min(n, a + HALF)
                    last = nc.tensor.matmul(s_ps[m % 2][:, a:e], lhsT=k.qT[:, h, b * P:(b + 1) * P],
                                            rhs=k.kT[:, h // (HEADS // KV_HEADS), a:e], start=True, stop=True)
                last.then_inc(s_done, 1)

            def transposes(m):
                b, h = jobs[m]
                pe.wait_ge(scaled, m + 1)
                if m:
                    pe.wait_ge(t_out, m)
                for j in range(b + 1):
                    last = nc.tensor.transpose(t_ps[:, j * P:(j + 1) * P], sm[:, m % 2, j * P:(j + 1) * P],
                                               k.const("ident"))
                last.then_inc(t_done, 1)

            def values(m):
                b, h = jobs[m]
                pe.wait_ge(t_out, m + 1)
                if m >= 2:
                    pe.wait_ge(o_out, m - 1)
                kv = h // (HEADS // KV_HEADS)
                for j in range(b + 1):
                    last = nc.tensor.matmul(o_ps[m % 2][:, :], lhsT=k.v_tok[:, j, kv * HD:(kv + 1) * HD],
                                            rhs=pT[:, m % 2, j * P:(j + 1) * P], start=j == 0, stop=j == b)
                last.then_inc(o_done, 1)

            for m in range(-2, len(jobs)):
                if m + 2 < len(jobs):
                    scores(m + 2)
                if 0 <= m + 1 < len(jobs):
                    transposes(m + 1)
                if m >= 0:
                    values(m)

        @block.scalar
        def _(act):
            def exps(m):
                n, _ = causal(jobs[m][0])
                act.wait_ge(neg, m + 1)
                nc.scalar.activation(sm[:, m % 2, 0:n], sm[:, m % 2, 0:n], ACT.Exp, bias=nb[:, m % 2:m % 2 + 1],
                                     scale=scale, accum_out=rs[:, m % 2:m % 2 + 1]).then_inc(exped, 1)

            for m in range(-2, len(jobs)):
                if 0 <= m + 1 < len(jobs):
                    n, _ = causal(jobs[m + 1][0])
                    act.wait_ge(t_done, m + 2)
                    if m + 1 >= 2:
                        act.wait_ge(o_done, m)
                    nc.scalar.copy(pT[:, (m + 1) % 2, 0:n], t_ps[:, 0:n]).then_inc(t_out, 1)
                if m + 2 < len(jobs):
                    exps(m + 2)

        @block.vector
        def _(dve):
            step = chain(dve, dve_step)
            v = nc.vector

            def out(m):
                b, h = jobs[m]
                dve.wait_ge(o_done, m + 1)
                z = k.z_att[:, h, b * P:(b + 1) * P]
                nc.vector.tensor_tensor(z, o_ps[m % 2][:, :], z, ALU.mult).then_inc(o_out, 1)

            def mask(m):
                n, at = causal(jobs[m][0])
                s = m % 2
                dve.wait_ge(s_done, m + 1)
                if m >= 2:
                    dve.wait_ge(t_done, m - 1)
                v.tensor_tensor_reduce(out=sm[:, s, 0:n], in0=s_ps[s][:, 0:n], in1=k.bias[:, at:at + n], scale=1.0,
                                       scalar=-3.0e38, op0=ALU.add, op1=ALU.max,
                                       accum_out=mx[:, s:s + 1]).then_inc(masked, 1)
                dve.wait_ge(masked, m + 1)
                v.tensor_scalar(nb[:, s:s + 1], mx[:, s:s + 1], -scale, None, ALU.mult).then_inc(neg, 1)

            def normalise(m):
                n, _ = causal(jobs[m][0])
                s = m % 2
                dve.wait_ge(exped, m + 1)
                step(v.reciprocal(rs[:, s:s + 1], rs[:, s:s + 1]))
                v.tensor_scalar(sm[:, s, 0:n], sm[:, s, 0:n], rs[:, s:s + 1], None, ALU.mult).then_inc(scaled, 1)

            for m in range(-2, len(jobs)):
                if 0 <= m + 1 < len(jobs):
                    normalise(m + 1)
                if m + 2 < len(jobs):
                    mask(m + 2)
                if m >= 0:
                    out(m)


def branch_att_stage(k):
    nc, ins = k.nc, k.ins
    with ExitStack() as ctx:
        w = k.sb("ba_w", [P, 2, KC, P], ctx=ctx)
        ws = k.sb("ba_ws", [P, 2, 2, KC, P], F16, ctx=ctx)
        oT = k.sb("ba_o", [P, 2, KC, S], F16, ctx=ctx)
        acc = [k.ps(f"ba_ps{i}", [P, S], ctx=ctx) for i in range(2)]
        w_in = [k.sem(f"ba_w_in{i}") for i in range(2)]
        done, out, high, low, o_high, o_low = (k.sem(f"ba_{n}") for n in ("done", "out", "high", "low", "o_high", "o_low"))
        stored = k.sem("ba_stored")
        block = ctx.enter_context(nc.Block())

        @block.sync
        def _(sp):
            for j in range(KC):
                if j >= 2:
                    sp.wait_ge(high, j - 1)
                    sp.wait_ge(low, j - 1)
                sp.dma_start(w[:, j % 2], ins["w_branch_att"][j]).then_inc(w_in[j % 2], 16)
            for j in range(KC):
                sp.wait_ge(out, j + 1)
                sp.dma_start(k.att_dram[j], k.g_att[:, j, :]).then_inc(stored, 16)
            sp.wait_ge(stored, 16 * KC)

        @block.tensor
        def _(pe):
            for j in range(KC):
                pe.wait_ge(high, j + 1)
                pe.wait_ge(low, j + 1)
                if j >= 2:
                    pe.wait_ge(out, j - 1)
                for c in range(KC):
                    if j == 0:
                        pe.wait_ge(o_high, c + 1)
                        pe.wait_ge(o_low, c + 1)
                    for a in range(0, S, HALF):
                        last = product(nc, acc[j % 2][:, a:a + HALF], part(ws, j % 2, c),
                                       part(oT, c, slice(a, a + HALF)), c == 0, c == KC - 1)
                last.then_inc(done, 1)

        @block.scalar
        def _(act):
            def split(j):
                act.wait_ge(w_in[j % 2], 16 * (j // 2 + 1))
                if j >= 2:
                    act.wait_ge(done, j - 1)
                high_part(nc, ws[:, 0, j % 2], w[:, j % 2]).then_inc(high, 1)

            nc.scalar.copy(oT[:, 0, 0, :], k.z_att[:, 0, :]).then_inc(o_high, 1)
            split(0)
            for c in range(1, KC):
                nc.scalar.copy(oT[:, 0, c, :], k.z_att[:, c, :]).then_inc(o_high, 1)
            for j in range(1, KC):
                split(j)

        @block.vector
        def _(dve):
            def split(j):
                dve.wait_ge(high, j + 1)
                low_part(nc, ws[:, 1, j % 2].rearrange("p c q -> p (c q)"), w[:, j % 2].rearrange("p c q -> p (c q)"),
                         ws[:, 0, j % 2].rearrange("p c q -> p (c q)")).then_inc(low, 1)

            for c in range(KC):
                dve.wait_ge(o_high, c + 1)
                nc.vector.tensor_tensor(oT[:, 1, c, :], k.z_att[:, c, :], oT[:, 0, c, :], ALU.subtract).then_inc(o_low, 1)
                if c == 0:
                    split(0)
            for j in range(KC):
                if j + 1 < KC:
                    split(j + 1)
                dve.wait_ge(done, j + 1)
                nc.vector.scalar_tensor_tensor(k.g_att[:, j, :], in0=acc[j % 2][:, :], scalar=1.0 / W_UP,
                                               in1=k.g_att[:, j, :], op0=ALU.mult, op1=ALU.mult).then_inc(out, 1)


def step_sizes_stage(k):
    nc, ins = k.nc, k.ins
    with ExitStack() as ctx:
        sb = lambda n, s=(P, TT, SSM_HEADS), d=F32: k.sb(f"d_{n}", list(s), d, ctx=ctx)
        rows = sb("rows", (P, 2, SSM_HEADS))
        x, u, w1, lnw, eq = sb("x"), sb("u"), sb("w1"), sb("lnw"), sb("eq")
        sums = [k.ps(f"d_ps{i}", [P, TT, SSM_HEADS], ctx=ctx) for i in range(3)]
        r_in, a_done, absx, exped, plus, logged, adt_ready, summed, expsum, dve_step = (k.sem(f"d_{n}") for n in (
            "r_in", "a_done", "absx", "exped", "plus", "logged", "adt_ready", "summed", "expsum", "dve_step"))
        block = ctx.enter_context(nc.Block())

        @block.sync
        def _(sp):
            sp.dma_start(rows[:, 0, :], ins["dt_bias"].partition_broadcast(P)).then_inc(r_in, 16)
            sp.dma_start(rows[:, 1, :], ins["a_log"].partition_broadcast(P)).then_inc(r_in, 16)
            sp.dma_start(k.d_skip[:, :], ins["d_skip"].partition_broadcast(P)).then_inc(r_in, 16)

        @block.scalar
        def _(act):
            act.wait_ge(r_in, 48)
            nc.scalar.activation(rows[:, 1, :], rows[:, 1, :], ACT.Exp).then_inc(a_done, 1)
            act.wait_ge(absx, 1)
            nc.scalar.activation(u[:, :, :], u[:, :, :], ACT.Exp).then_inc(exped, 1)
            act.wait_ge(plus, 1)
            nc.scalar.activation(lnw[:, :, :], w1[:, :, :], ACT.Ln).then_inc(logged, 1)
            act.wait_ge(summed, 1)
            for src, dst in zip(sums, (k.e_cum, k.e_after, k.e_all)):
                last = nc.scalar.activation(dst[:, :, :], src[:, :, :], ACT.Exp)
            last.then_inc(expsum, 1)

        @block.tensor
        def _(pe):
            pe.wait_ge(adt_ready, 1)
            for n, tri in enumerate(("upto", "after", "ones")):
                last = nc.tensor.matmul(sums[n][:, :, :].rearrange("p t h -> p (t h)"), lhsT=k.const(tri),
                                        rhs=k.adt[:, :, :].rearrange("p t h -> p (t h)"), start=True, stop=True)
            last.then_inc(summed, 1)

        @block.vector
        def _(dve):
            step = chain(dve, dve_step)
            v = nc.vector
            row = lambda n: rows[:, n, :].unsqueeze(1).to_broadcast([P, TT, SSM_HEADS])
            dve.wait_ge(r_in, 48)
            step(v.tensor_tensor(x[:, :, :], k.dt_raw[:, :, :], row(0), ALU.add))
            step(v.tensor_scalar(u[:, :, :], x[:, :, :], -1.0, None, ALU.mult))
            v.tensor_tensor(u[:, :, :], u[:, :, :], x[:, :, :], ALU.min).then_inc(absx, 1)
            dve.wait_ge(exped, 1)
            v.tensor_scalar(w1[:, :, :], u[:, :, :], 1.0, None, ALU.add).then_inc(plus, 1)
            dve.wait_ge(logged, 1)
            dve.wait_ge(plus, 1)
            step(v.tensor_scalar(w1[:, :, :], w1[:, :, :], -1.0, None, ALU.add))
            step(v.tensor_scalar(eq[:, :, :], w1[:, :, :], 0.0, None, ALU.is_equal))
            step(v.tensor_tensor(w1[:, :, :], w1[:, :, :], eq[:, :, :], ALU.add))
            step(v.tensor_tensor(lnw[:, :, :], lnw[:, :, :], eq[:, :, :], ALU.add))
            step(v.reciprocal(w1[:, :, :], w1[:, :, :]))
            step(v.tensor_tensor(lnw[:, :, :], lnw[:, :, :], w1[:, :, :], ALU.mult))
            step(v.tensor_tensor(lnw[:, :, :], lnw[:, :, :], u[:, :, :], ALU.mult))
            step(v.tensor_scalar(x[:, :, :], x[:, :, :], 0.0, None, ALU.max))
            step(v.tensor_tensor(k.dt[:, :, :], x[:, :, :], lnw[:, :, :], ALU.add))
            dve.wait_ge(a_done, 1)
            step(v.tensor_tensor(k.adt[:, :, :], k.dt[:, :, :], row(1), ALU.mult))
            step(v.tensor_scalar(k.adt[:, :, :], k.adt[:, :, :], -1.0, None, ALU.mult))
            dve.sem_inc(adt_ready, 1)
            dve.wait_ge(expsum, 1)
            step(v.tensor_tensor(k.e_after[:, :, :], k.e_after[:, :, :], k.dt[:, :, :], ALU.mult))


def ssm_inputs_stage(k, g):
    nc, ins = k.nc, k.ins
    pad = SSM_CONV - 1
    tiles = [4 * g + n for n in range(4)] + [16 + g, 20 + g]
    with ExitStack() as ctx:
        sb = lambda n, s, d=F32: k.sb(f"i{g}_{n}", s, d, ctx=ctx)
        w = sb("w", [P, 2, KC, P])
        ws = sb("ws", [P, 2, 2, KC, P], F16)
        u, xf = sb("u", [P, 2, pad + S]), sb("xf", [P, 2, S])
        pj = [k.ps(f"i{g}_pj{i}", [P, S], ctx=ctx) for i in range(2)]
        tr = [k.ps(f"i{g}_tr{i}", [P, HALF], ctx=ctx) for i in range(2)]
        w_in = [k.sem(f"i{g}_w_in{i}") for i in range(2)]
        pads, pj_done, u_done, conv, act_done, tr_done, tr_out, dve_step, high, low = (
            k.sem(f"i{g}_{n}") for n in ("pads", "pj_done", "u_done", "conv", "act_done", "tr_done",
                                        "tr_out", "dve_step", "high", "low"))
        wz_in, z_high = k.sem(f"i{g}_wz_in"), k.sem(f"i{g}_z_high")
        dsts = [xf[:, 0], xf[:, 1], xf[:, 0], xf[:, 1], k.BT[:, :], k.CT[:, :]]
        block = ctx.enter_context(nc.Block())

        @block.sync
        def _(sp):
            for j, tile in enumerate(tiles):
                if j >= 2:
                    sp.wait_ge(high, j - 1)
                    sp.wait_ge(low, j - 1)
                sp.dma_start(w[:, j % 2], ins["w_xbc"][tile]).then_inc(w_in[j % 2], 16)
                if j == 2:
                    sp.dma_start(k.w_group[:, :, :],
                                 ins["w_z"][:, g * GW:(g + 1) * GW].rearrange("(c p) n -> p c n", p=P)) \
                        .then_inc(wz_in, 16)

        @block.tensor
        def _(pe):
            def transposes(j):
                pe.wait_ge(act_done, j + 1)
                for h in range(2):
                    if 2 * j + h >= 2:
                        pe.wait_ge(tr_out, 2 * j + h - 1)
                    for t in range(4):
                        last = nc.tensor.transpose(tr[h][:, t * P:(t + 1) * P],
                                                   dsts[j][:, (4 * h + t) * P:(4 * h + t + 1) * P], k.const("ident"))
                    last.then_inc(tr_done, 1)

            for j in range(6):
                pe.wait_ge(high, j + 1)
                pe.wait_ge(low, j + 1)
                if j >= 2:
                    pe.wait_ge(u_done, j - 1)
                for a in range(0, S, HALF):
                    for c in range(KC):
                        last = product(nc, pj[j % 2][:, a:a + HALF], part(ws, j % 2, c),
                                       part(k.hT, c, slice(a, a + HALF)), c == 0, c == KC - 1)
                last.then_inc(pj_done, 1)
                if j:
                    transposes(j - 1)

        @block.vector
        def _(dve):
            step = chain(dve, dve_step)
            v = nc.vector
            for i in range(2):
                v.memset(u[:, i, 0:pad], 0.0).then_inc(pads, 1)
            dve.wait_ge(pads, 2)

            def split(j):
                dve.wait_ge(high, j + 1)
                low_part(nc, ws[:, 1, j % 2].rearrange("p c q -> p (c q)"), w[:, j % 2].rearrange("p c q -> p (c q)"),
                         ws[:, 0, j % 2].rearrange("p c q -> p (c q)")).then_inc(low, 1)

            split(0)
            for j, tile in enumerate(tiles):
                if j + 1 < len(tiles):
                    split(j + 1)
                if j == 5:
                    dve.wait_ge(z_high, 1)
                    low_part(nc, k.ws_group[:, 1], k.w_group[:, :, :], k.ws_group[:, 0])
                dve.wait_ge(u_done, j + 1)
                if j >= 2 and j < 4:
                    dve.wait_ge(tr_done, 2 * (j - 1))
                tap = lambda i: k.pv("conv_w_2", tile * SSM_CONV + i)
                step(v.tensor_scalar(dsts[j], u[:, j % 2, 0:S], tap(0), None, ALU.mult))
                for i in range(1, SSM_CONV):
                    last = v.scalar_tensor_tensor(dsts[j], in0=u[:, j % 2, i:i + S], scalar=tap(i), in1=dsts[j],
                                                  op0=ALU.mult, op1=ALU.add)
                    if i < SSM_CONV - 1:
                        step(last)
                last.then_inc(conv, 1)

        @block.scalar
        def _(act):
            def split(j):
                act.wait_ge(w_in[j % 2], 16 * (j // 2 + 1))
                if j >= 2:
                    act.wait_ge(pj_done, j - 1)
                high_part(nc, ws[:, 0, j % 2], w[:, j % 2]).then_inc(high, 1)

            def activate(j):
                act.wait_ge(conv, j + 1)
                nc.scalar.activation(dsts[j], dsts[j], ACT.Silu, bias=k.pv("conv_b_2", tiles[j])).then_inc(act_done, 1)

            def out(j):
                for h in range(2):
                    act.wait_ge(tr_done, 2 * j + h + 1)
                    dst = k.x_ssm[:, 4 * h:4 * h + 4, j * P:(j + 1) * P] if j < 4 else k.B_tok[:, 4 * h:4 * h + 4, :]
                    nc.scalar.copy(dst, tr[h][:, :].rearrange("p (t q) -> p t q", q=P)).then_inc(tr_out, 1)

            split(0)
            for j in range(6):
                if j + 1 < 6:
                    split(j + 1)
                if j == 4:
                    act.wait_ge(wz_in, 16)
                    high_part(nc, k.ws_group[:, 0], k.w_group[:, :, :]).then_inc(z_high, 1)
                act.wait_ge(pj_done, j + 1)
                if j >= 2:
                    act.wait_ge(conv, j - 1)
                nc.scalar.activation(u[:, j % 2, pad:pad + S], pj[j % 2][:, :], ACT.Copy,
                                     scale=1.0 / W_UP).then_inc(u_done, 1)
                if j:
                    activate(j - 1)
                if j >= 2:
                    out(j - 2)
            activate(5)
            out(4)


def ssm_scan_stage(k, g):
    nc, ins = k.nc, k.ins
    heads = slice(g * HPG, (g + 1) * HPG)
    with ExitStack() as ctx:
        sb = lambda n, s, d=F32: k.sb(f"y{g}_{n}", s, d, ctx=ctx)
        xdt, xds = sb("xdt", [P, 2, HPG, SSM_HD]), sb("xds", [P, 2, HPG, SSM_HD])
        A, E = sb("A", [P, 2, HPG, P]), sb("E", [P, 2, HPG * P])
        M = E[:, :, :].rearrange("p s (h l) -> p s h l", l=P)
        cbm, state, xd = sb("cbm", [P, 2, P]), sb("state", [P, GW]), sb("xd", [P, 2, HPG, SSM_HD])
        ss = sb("ss", [P, TT])
        w_z = k.ws_group
        w = k.w_group[:, :, :].rearrange("p (c a) n -> p c (a n)", c=4)
        ws = w_z[:, :, :, :].rearrange("p s (c a) n -> p s c (a n)", c=4)
        yT = k.x_ssm[:, :, :].rearrange("p t n -> p (t n)").bitcast(F16).rearrange(
            "p (s c n) -> p s c n", s=2, c=4)
        cb = k.ps(f"y{g}_cb", [P, P], ctx=ctx)
        seg = k.ps(f"y{g}_seg", [P, HPG * P], ctx=ctx)
        yd_ps, yo_ps, st_ps = (k.ps(f"y{g}_{n}", [P, GW], ctx=ctx) for n in ("yd_ps", "yo_ps", "st_ps"))
        br = k.ps(f"y{g}_br", [P, S], ctx=ctx)
        names = ("w_in", "pool_in", "A_done", "seg_done", "cb_done", "E_done", "cbm_done", "M_done", "yd_done",
                 "yo_done", "st_done", "state_done", "yo_read", "y_done", "var", "std", "normed", "tr_done",
                 "tr_out", "br_done", "br_out", "dve_step", "xd_done", "gated", "squared", "z_done", "z_out",
                 "z_act", "w_high", "w_low", "tr_low")
        q = {n: k.sem(f"y{g}_{n}") for n in names}
        block = ctx.enter_context(nc.Block())

        def per_head(x, t, n=SSM_HD):
            return x[:, t, heads].unsqueeze(2).to_broadcast([P, HPG, n])

        @block.sync
        def _(sp):
            sp.dma_start(w, ins["w_branch_ssm"][g * GW:(g + 1) * GW, :].rearrange("(c p) n -> p c n", p=P)) \
                .then_inc(q["w_in"], 16)

        @block.gpsimd
        def _(pool):
            for t in range(TT):
                s = t % 2
                xs = k.x_ssm[:, t, :].rearrange("p (h d) -> p h d", d=SSM_HD)
                if t >= 2:
                    pool.wait_ge(q["seg_done"], t - 1)
                nc.gpsimd.tensor_tensor(A[:, s], per_head(k.adt, t, P),
                                        k.const("after").unsqueeze(1).to_broadcast([P, HPG, P]), ALU.mult) \
                    .then_inc(q["A_done"], 1)
                if t >= 2:
                    pool.wait_ge(q["yd_done"], t - 1)
                    pool.wait_ge(q["st_done"], t - 1)
                    pool.wait_ge(q["y_done"], t - 1)
                nc.gpsimd.tensor_tensor(xdt[:, s], xs, per_head(k.dt, t), ALU.mult)
                nc.gpsimd.tensor_tensor(xds[:, s], xs, per_head(k.e_after, t), ALU.mult).then_inc(q["pool_in"], 1)
                nc.gpsimd.tensor_tensor(xd[:, s], xs,
                                        k.d_skip[:, heads].unsqueeze(2).to_broadcast([P, HPG, SSM_HD]),
                                        ALU.mult).then_inc(q["xd_done"], 1)

        @block.tensor
        def _(pe):
            def segments(t):
                span = slice(t * P, (t + 1) * P)
                pe.wait_ge(q["A_done"], t + 1)
                if t:
                    pe.wait_ge(q["E_done"], t)
                for h in range(HPG):
                    last = nc.tensor.matmul(seg[:, h * P:(h + 1) * P], lhsT=A[:, t % 2, h, :], rhs=k.const("upto"),
                                            start=True, stop=True)
                last.then_inc(q["seg_done"], 1)
                if t:
                    pe.wait_ge(q["cbm_done"], t)
                nc.tensor.matmul(cb[:, :], lhsT=k.BT[:, span], rhs=k.CT[:, span], start=True, stop=True) \
                    .then_inc(q["cb_done"], 1)

            def z(t):
                if t >= 2:
                    pe.wait_ge(q["z_out"], t - 1)
                for c in range(KC):
                    last = product(nc, br[:, t % 2 * GW:(t % 2 + 1) * GW], part(k.hT, c, slice(t * P, (t + 1) * P)),
                                   part(w_z, c), c == 0, c == KC - 1)
                last.then_inc(q["z_done"], 1)

            segments(0)
            for t in range(TT):
                s = t % 2
                span = slice(t * P, (t + 1) * P)
                if t + 1 < TT:
                    segments(t + 1)
                z(t)
                pe.wait_ge(q["pool_in"], t + 1)
                if t:
                    pe.wait_ge(q["state_done"], t)
                    pe.wait_ge(q["yo_read"], t)
                    nc.tensor.matmul(yo_ps[:, :], lhsT=k.CT[:, span], rhs=state[:, :], start=True, stop=True) \
                        .then_inc(q["yo_done"], 1)
                nc.tensor.matmul(st_ps[:, :], lhsT=k.B_tok[:, t, :], rhs=xds[:, s].rearrange("p h d -> p (h d)"),
                                 start=True, stop=True).then_inc(q["st_done"], 1)
                pe.wait_ge(q["M_done"], t + 1)
                if t:
                    pe.wait_ge(q["y_done"], t)
                for h in range(HPG):
                    last = nc.tensor.matmul(yd_ps[:, h * SSM_HD:(h + 1) * SSM_HD], lhsT=M[:, s, h, :],
                                            rhs=xdt[:, s, h, :], start=True, stop=True)
                last.then_inc(q["yd_done"], 1)
            for t in range(TT):
                pe.wait_ge(q["normed"], t + 1)
                if t >= 2:
                    pe.wait_ge(q["tr_out"], 4 * (t - 1))
                    pe.wait_ge(q["tr_low"], 4 * (t - 1))
                bank = (yd_ps, yo_ps)[t % 2]
                for c in range(4):
                    last = nc.tensor.transpose(bank[:, c * P:(c + 1) * P], k.z_ssm[:, t, c * P:(c + 1) * P],
                                               k.const("ident"))
                last.then_inc(q["tr_done"], 1)
            pe.wait_ge(q["tr_out"], 4 * TT)
            pe.wait_ge(q["tr_low"], 4 * TT)
            pe.wait_ge(q["w_high"], 1)
            pe.wait_ge(q["w_low"], 1)
            for m in range(KC):
                bank = (br, seg)[m % 2]
                if m >= 2:
                    pe.wait_ge(q["br_out"], m - 1)
                for a in range(0, S, HALF):
                    for c in range(4):
                        last = product(nc, bank[:, a:a + HALF], part(ws, c, slice(m * P, (m + 1) * P)),
                                       part(yT, c, slice(a, a + HALF)), c == 0, c == 3)
                last.then_inc(q["br_done"], 1)

        @block.scalar
        def _(act):
            for t in range(TT):
                act.wait_ge(q["seg_done"], t + 1)
                if t >= 2:
                    act.wait_ge(q["yd_done"], t - 1)
                nc.scalar.activation(E[:, t % 2], seg[:, :], ACT.Exp).then_inc(q["E_done"], 1)
                act.wait_ge(q["z_done"], t + 1)
                nc.scalar.activation(k.z_ssm[:, t, :], br[:, t % 2 * GW:(t % 2 + 1) * GW], ACT.Copy,
                                     scale=1.0 / W_UP).then_inc(q["z_out"], 1)
            for t in range(TT):
                act.wait_ge(q["z_out"], t + 1)
                nc.scalar.activation(k.z_ssm[:, t, :], k.z_ssm[:, t, :], ACT.Silu).then_inc(q["z_act"], 1)
            act.wait_ge(q["w_in"], 16)
            high_part(nc, ws[:, 0], w).then_inc(q["w_high"], 1)
            act.wait_ge(q["var"], 1)
            nc.scalar.activation(ss[:, :], ss[:, :], ACT.Sqrt).then_inc(q["std"], 1)
            for t in range(TT):
                act.wait_ge(q["tr_done"], t + 1)
                bank = (yd_ps, yo_ps)[t % 2]
                for c in range(4):
                    nc.scalar.activation(yT[:, 0, c, t * P:(t + 1) * P], bank[:, c * P:(c + 1) * P], ACT.Copy,
                                         scale=k.pv("ssm_norm_g_2", 4 * g + c)).then_inc(q["tr_out"], 1)

        @block.vector
        def _(dve):
            step = chain(dve, q["dve_step"])
            v = nc.vector
            for t in range(TT):
                s = t % 2
                dve.wait_ge(q["cb_done"], t + 1)
                v.tensor_tensor(cbm[:, s], cb[:, :], k.const("upto"), ALU.mult).then_inc(q["cbm_done"], 1)
                dve.wait_ge(q["cbm_done"], t + 1)
                dve.wait_ge(q["E_done"], t + 1)
                v.tensor_tensor(M[:, s], E[:, s].rearrange("p (h l) -> p h l", l=P),
                                cbm[:, s].unsqueeze(1).to_broadcast([P, HPG, P]), ALU.mult).then_inc(q["M_done"], 1)
                dve.wait_ge(q["st_done"], t + 1)
                if t == 0:
                    v.tensor_copy(state[:, :], st_ps[:, :]).then_inc(q["state_done"], 1)
                else:
                    sh = state[:, :].rearrange("p (h d) -> p h d", d=SSM_HD)
                    dve.wait_ge(q["yo_done"], t)
                    step(v.tensor_tensor(sh, sh, per_head(k.e_all, t), ALU.mult))
                    v.tensor_tensor(state[:, :], state[:, :], st_ps[:, :], ALU.add).then_inc(q["state_done"], 1)
                y = k.x_ssm[:, t, :]
                yh = y.rearrange("p (h d) -> p h d", d=SSM_HD)
                xdf = xd[:, s].rearrange("p h d -> p (h d)")
                dve.wait_ge(q["xd_done"], t + 1)
                if t:
                    step(v.tensor_tensor(yh, yo_ps[:, :].rearrange("p (h d) -> p h d", d=SSM_HD),
                                         per_head(k.e_cum, t), ALU.mult))
                    step(v.tensor_tensor(y, y, xdf, ALU.add))
                    xdf = y
                dve.sem_inc(q["yo_read"], 1)
                dve.wait_ge(q["yd_done"], t + 1)
                v.tensor_tensor(y, yd_ps[:, :], xdf, ALU.add).then_inc(q["y_done"], 1)
            for t in range(TT):
                dve.wait_ge(q["z_act"], t + 1)
                dve.wait_ge(q["y_done"], t + 1)
                z = k.z_ssm[:, t, :]
                v.tensor_tensor(z, z, k.x_ssm[:, t, :], ALU.mult).then_inc(q["gated"], 1)
                dve.wait_ge(q["gated"], t + 1)
                v.tensor_tensor_reduce(out=k.x_ssm[:, t, :], in0=z, in1=z, scale=1.0, scalar=0.0,
                                       op0=ALU.mult, op1=ALU.add, accum_out=ss[:, t:t + 1]).then_inc(q["squared"], 1)
            dve.wait_ge(q["squared"], TT)
            step(v.tensor_scalar(ss[:, :], ss[:, :], 1.0 / GW, EPS, ALU.mult, ALU.add))
            dve.sem_inc(q["var"], 1)
            dve.wait_ge(q["std"], 1)
            step(v.reciprocal(ss[:, :], ss[:, :]))
            for t in range(TT):
                v.tensor_scalar(k.z_ssm[:, t, :], k.z_ssm[:, t, :], ss[:, t:t + 1], None, ALU.mult) \
                    .then_inc(q["normed"], 1)
            dve.wait_ge(q["w_high"], 1)
            low_part(nc, ws[:, 1], w, ws[:, 0]).then_inc(q["w_low"], 1)
            for t in range(TT):
                dve.wait_ge(q["tr_out"], 4 * (t + 1))
                for c in range(4):
                    v.scalar_tensor_tensor(yT[:, 1, c, t * P:(t + 1) * P], in0=(yd_ps, yo_ps)[t % 2][:, c * P:(c + 1) * P],
                                           scalar=k.pv("ssm_norm_g_2", 4 * g + c), in1=yT[:, 0, c, t * P:(t + 1) * P],
                                           op0=ALU.mult, op1=ALU.subtract).then_inc(q["tr_low"], 1)
            for m in range(KC):
                bank = (br, seg)[m % 2]
                dve.wait_ge(q["br_done"], m + 1)
                if g == 0:
                    v.tensor_scalar(k.y_ssm[:, m, :], bank[:, :], 1.0 / W_UP, None, ALU.mult).then_inc(q["br_out"], 1)
                else:
                    v.scalar_tensor_tensor(k.y_ssm[:, m, :], in0=bank[:, :], scalar=1.0 / W_UP, in1=k.y_ssm[:, m, :],
                                           op0=ALU.mult, op1=ALU.add).then_inc(q["br_out"], 1)


def merge_stage(k):
    nc, ins = k.nc, k.ins
    with ExitStack() as ctx:
        w = k.sb("mg_w", [P, 2, KC, P], ctx=ctx)
        ws = k.sb("mg_ws", [P, 2, 2, KC, P], F16, ctx=ctx)
        sig, att = k.sb("mg_sig", [P, 2, S], ctx=ctx), k.sb("mg_att", [P, KC, S], ctx=ctx)
        att_in = [k.sem(f"mg_att_in{j}") for j in range(KC)]
        acc = [k.ps(f"mg_ps{i}", [P, S], ctx=ctx) for i in range(2)]
        w_in = [k.sem(f"mg_w_in{i}") for i in range(2)]
        done, out, mul, added, high, low, m_high, m_low = (k.sem(f"mg_{n}") for n in (
            "done", "out", "mul", "added", "high", "low", "m_high", "m_low"))
        block = ctx.enter_context(nc.Block())

        @block.sync
        def _(sp):
            for j in range(KC):
                if j >= 2:
                    sp.wait_ge(high, j - 1)
                    sp.wait_ge(low, j - 1)
                sp.dma_start(w[:, j % 2], ins["w_gates"][2 * KC + j]).then_inc(w_in[j % 2], 16)
                sp.dma_start(att[:, j, :], k.att_dram[j]).then_inc(att_in[j], 16)
            for j in range(KC):
                sp.dma_start(k.next_w[:, j, :], ins["w_out_2"][j * P:(j + 1) * P, :]).then_inc(k.next_w_in, 16)

        @block.tensor
        def _(pe):
            for j in range(KC):
                pe.wait_ge(high, j + 1)
                pe.wait_ge(low, j + 1)
                if j >= 2:
                    pe.wait_ge(out, j - 1)
                for a in range(0, S, HALF):
                    for c in range(KC):
                        last = product(nc, acc[j % 2][:, a:a + HALF], part(ws, j % 2, c),
                                       part(k.hT, c, slice(a, a + HALF)), c == 0, c == KC - 1)
                last.then_inc(done, 1)

        @block.scalar
        def _(act):
            def split(j):
                act.wait_ge(w_in[j % 2], 16 * (j // 2 + 1))
                if j >= 2:
                    act.wait_ge(done, j - 1)
                high_part(nc, ws[:, 0, j % 2], w[:, j % 2]).then_inc(high, 1)

            split(0)
            for j in range(KC):
                if j + 1 < KC:
                    split(j + 1)
                act.wait_ge(done, j + 1)
                if j >= 2:
                    act.wait_ge(added, j - 1)
                nc.scalar.activation(sig[:, j % 2], acc[j % 2][:, :], ACT.Sigmoid, scale=1.0 / W_UP).then_inc(out, 1)
                act.wait_ge(added, j + 1)
                nc.scalar.copy(k.merged[:, 0, j, :], att[:, j, :]).then_inc(m_high, 1)

        @block.vector
        def _(dve):
            def split(j):
                dve.wait_ge(high, j + 1)
                low_part(nc, ws[:, 1, j % 2].rearrange("p c q -> p (c q)"), w[:, j % 2].rearrange("p c q -> p (c q)"),
                         ws[:, 0, j % 2].rearrange("p c q -> p (c q)")).then_inc(low, 1)

            split(0)
            for j in range(KC):
                if j + 1 < KC:
                    split(j + 1)
                dve.wait_ge(out, j + 1)
                nc.vector.tensor_tensor(sig[:, j % 2], sig[:, j % 2], k.y_ssm[:, j, :], ALU.mult).then_inc(mul, 1)
                dve.wait_ge(mul, j + 1)
                dve.wait_ge(att_in[j], 16)
                nc.vector.tensor_tensor(att[:, j, :], att[:, j, :], sig[:, j % 2], ALU.add).then_inc(added, 1)
                dve.wait_ge(m_high, j + 1)
                nc.vector.tensor_tensor(k.merged[:, 1, j, :], att[:, j, :], k.merged[:, 0, j, :], ALU.subtract)


def mixer_program(nc, ins, out):
    with ExitStack() as ctx:
        k = Core(nc, ctx, ins)
        k.params, k.consts = k.sb("params", [P, PV_N]), k.sb("consts", [P, len(CONSTS), P])
        k.mod, k.gain = k.sb("mod", [P, 9 * KC]), k.sb("gain", [P, 3 * KC])
        k.x_dram = nc.dram_tensor("x_second", (S, D), F32, kind="Internal").ap()
        k.att_dram = nc.dram_tensor("gated_att", (KC, P, S), F32, kind="Internal").ap()
        k.hT = k.sb("hT", [P, 2, KC, S], F16)
        with ExitStack() as first:
            k.x_tok = k.sb("x_tok", [P, TT, D], ctx=first)
            alloc_routing(k, first)
            modulation_stage(k)
            with ExitStack() as c:
                k.y = k.sb("conv_y", [P, KC, S], ctx=c)
                norm_transpose_stage(k, "mix", k.x_tok, k.gain[:, 0:KC], k.mod[:, 0:KC])
                conv_stage(k)
                k.next_w, k.next_w_in = k.sb("conv_out_w", [P, KC, D], ctx=c), k.sem("conv_out_w_in")
                conv_norm_stage(k)
                token_projection_stage(k, "co", k.hT, k.mod[:, 2 * KC:3 * KC])
            norm_transpose_stage(k, "ffn", k.x_tok, k.gain[:, KC:2 * KC], k.mod[:, 3 * KC:4 * KC],
                                 normed_dram=k.normed_dram)
            k.clear_semaphores()
            router_stage(k)
            experts_stage(k)
            combine_stage(k)
            norm_transpose_stage(k, "two", k.x_tok, k.gain[:, 2 * KC:3 * KC], k.mod[:, 6 * KC:7 * KC],
                                 raw_dram=k.x_dram)
        k.clear_semaphores()
        second_block(k, out)


def second_block(k, out):
    ctx = k.ctx
    k.dt_raw, k.widx = k.sb("dt_raw", [P, TT, SSM_HEADS]), k.sb("widx", [P, TT, IDX_HEADS])
    with ExitStack() as att:
        k.g_att = k.sb("g_att", [P, KC, S], ctx=att)
        k.z_att = k.sb("z_att", [P, KC, S], ctx=att)
        k.qT, k.kT = k.sb("qT", [P, HEADS, S], ctx=att), k.sb("kT", [P, KV_HEADS, S], ctx=att)
        k.v_tok = k.sb("v_tok", [P, TT, KV_HEADS * HD], ctx=att)
        k.bias = k.sb("bias", [P, TT * (TT + 1) // 2 * P], BF16, ctx=att)
        with ExitStack() as idx:
            k.qidxT, k.kidxT = k.sb("qidxT", [P, 2, S], ctx=idx), k.sb("kidxT", [P, S], ctx=idx)
            qkv_stage(k)
            select_stage(k)
        attention_stage(k)
        branch_att_stage(k)
    k.clear_semaphores()
    with ExitStack() as s:
        k.y_ssm = k.sb("y_ssm", [P, KC, S], ctx=s)
        with ExitStack() as grp:
            k.dt, k.adt, k.e_cum, k.e_after, k.e_all = (
                k.sb(n, [P, TT, SSM_HEADS], ctx=grp) for n in ("dt", "adt", "e_cum", "e_after", "e_all"))
            k.d_skip = k.sb("d_skip", [P, SSM_HEADS], ctx=grp)
            step_sizes_stage(k)
            k.x_ssm, k.z_ssm = k.sb("x_ssm", [P, TT, GW], ctx=grp), k.sb("z_ssm", [P, TT, GW], ctx=grp)
            k.B_tok = k.sb("B_tok", [P, TT, SSM_N], ctx=grp)
            k.BT, k.CT = k.sb("BT", [P, S], ctx=grp), k.sb("CT", [P, S], ctx=grp)
            k.w_group, k.ws_group = k.sb("w_group", [P, KC, GW], ctx=grp), k.sb("ws_group", [P, 2, KC, GW], F16, ctx=grp)
            for g in range(SSM_GROUPS):
                ssm_inputs_stage(k, g)
                ssm_scan_stage(k, g)
                k.clear_semaphores()
        k.merged = k.sb("merged", [P, 2, KC, S], F16, ctx=s)
        k.next_w, k.next_w_in = k.sb("out_w", [P, KC, D], ctx=s), k.sem("out_w_in")
        merge_stage(k)
        k.x_tok = k.y_ssm
        token_projection_stage(k, "fin", k.merged, k.mod[:, 8 * KC:9 * KC], out_dram=out, x_from=k.x_dram)


def layout(inputs):
    f = np.ascontiguousarray
    d = {n: np.asarray(v) for n, v in inputs.items()}

    def columns(name, n):
        v = d[name]
        if name == "conv_w_dw":
            return v[0].reshape(CONV, KC, P).transpose(2, 1, 0).reshape(P, n)
        if name == "conv_w_2":
            return v[0].reshape(SSM_CONV, 24, P).transpose(2, 1, 0).reshape(P, n)
        return v.reshape(-1, P).T

    def tiles(w):
        return f(w.reshape(KC, P, w.shape[1] // P, P).transpose(2, 1, 0, 3))

    q0, z0, i0, zs0, x0, dt0, g0 = 0, 1536, 2560, 2884, 4932, 8004, 8036
    w = d["w_in_2"][0]
    consts, freq = constant_tables()
    return {
        "x": d["x"][0], "params": f(np.concatenate([columns(n, m) for n, m in PV_FIELDS], axis=1)),
        "consts": consts, "freq": freq, "rows": row_constants(),
        "token_ids": f(np.arange(S, dtype=np.float32).reshape(TT, P).T),
        "ada_w": d["ada_w"][0], "ada_w_2": d["ada_w_2"][0],
        "conv_w_in": tiles(d["conv_w_in"][0]), "conv_w_out": d["conv_w_out"][0],
        "router_w": f(np.concatenate([d["moe_w_rg"][0], d["moe_w_re"][0]], axis=1)),
        "router_b": f(np.concatenate([d["moe_b_rg"][0], d["moe_b_re"][0]])),
        "moe_w_gate": d["moe_w_gate"][0], "moe_w_up": d["moe_w_up"][0], "moe_w_down": d["moe_w_down"][0],
        "final_g": d["final_g"], "positions": f(d["positions_2"][0].reshape(TT, P).T),
        "q_norm_g": d["q_norm_g_2"][0], "k_norm_g": d["k_norm_g_2"][0],
        "idx_ln_g": d["idx_k_ln_g_2"][0], "idx_ln_b": d["idx_k_ln_b_2"][0],
        "w_tok": f(np.concatenate([w[:, q0:z0], w[:, i0:zs0], w[:, dt0:g0]], axis=1)),
        "w_gates": tiles(np.concatenate([w[:, z0:i0], w[:, g0:]], axis=1)),
        "w_xbc": tiles(w[:, x0:dt0]), "w_z": f(w[:, zs0:x0]),
        "dt_bias": d["dt_bias_2"][0], "a_log": d["a_log_2"][0], "d_skip": d["d_skip_2"][0],
        "w_branch_att": tiles(d["w_branch_att_2"][0]), "w_branch_ssm": d["w_branch_ssm_2"][0],
        "w_out_2": d["w_out_2"][0],
    }


def kernel(**inputs):
    import concourse.bacc as bacc
    from concourse.bass_utils import run_bass_kernel_spmd

    nc = bacc.Bacc("TRN2", target_bir_lowering=False, num_devices=1)
    arrays, ins = {}, {}
    for name, a in layout(inputs).items():
        arrays[f"in_{name}"] = a
        ins[name] = nc.dram_tensor(f"in_{name}", a.shape, mybir.dt.from_np(a.dtype), kind="ExternalInput").ap()
    out = nc.dram_tensor("out_x", (S, D), F32, kind="ExternalOutput").ap()
    mixer_program(nc, ins, out)
    r = run_bass_kernel_spmd(nc, [arrays], core_ids=[0])
    return r.results[0]["out_x"].reshape(1, S, D)
```

```python
import numpy as np
from contextlib import ExitStack

import concourse.bass as bass
from concourse import mybir

F32 = mybir.dt.float32
I32 = mybir.dt.int32
U32 = mybir.dt.uint32
BF16 = mybir.dt.bfloat16
F16 = mybir.dt.float16
ALU = mybir.AluOpType
ACT = mybir.ActivationFunctionType
AX = mybir.AxisListType

P = 128
D = 1024
S = 1024
KC = D // P
TT = S // P
HALF = 512
EPS = 1e-6
CONV = 31
GROUPS, PER_GROUP = 4, 8
EXPERTS = GROUPS * PER_GROUP
FFN = D // 2
SLOT_BLOCKS = 2 * S // P + EXPERTS
HEADS, KV_HEADS, HD = 8, 2, 128
IDX_HEADS, IDX_DIM = 4, 64
TOPK = 256
SSM_INNER, SSM_HEADS, SSM_HD, SSM_GROUPS, SSM_N, SSM_CONV = 2048, 32, 64, 4, 128, 4
HPG = SSM_HEADS // SSM_GROUPS
GW = HPG * SSM_HD
BIG = 1.0e30
PE_TAPS = 8
EARLY_GATES = 6
EARLY_Z = 4
W_UP = 256.0

PV_FIELDS = [
    ("ada_b", 48), ("norm_mix_g", 8), ("norm_ffn_g", 8), ("conv_b_in", 16), ("conv_w_dw", 8 * CONV),
    ("conv_b_dw", 8), ("conv_ln_g", 8), ("conv_ln_b", 8), ("ada_b_2", 24), ("norm_g_2", 8),
    ("conv_w_2", 24 * SSM_CONV), ("conv_b_2", 24), ("ssm_norm_g_2", 16), ("c", 8), ("c_2", 8),
]
PV_AT, PV_N = {}, 0
for _name, _n in PV_FIELDS:
    PV_AT[_name] = PV_N
    PV_N += _n

CONSTS = ["ident", "upto", "before", "after", "ones", "mean_d"]


def constant_tables():
    k, m = np.arange(P)[:, None], np.arange(P)[None, :]
    c = {
        "ident": k == m, "upto": k <= m, "before": k < m, "after": k > m,
        "ones": np.ones((P, P)), "mean_d": np.full((P, P), 1.0 / D),
    }
    table = np.stack([np.asarray(c[n], np.float32) for n in CONSTS], axis=1)
    freq = [np.power(500000.0, -(2.0 * np.arange(n // 2) / n)) for n in (HD // 4, IDX_DIM // 4)]
    return np.ascontiguousarray(table), np.concatenate(freq).astype(np.float32)


def row_constants():
    return np.concatenate([np.arange(GROUPS, 0, -1), np.arange(EXPERTS, 0, -1), np.arange(SLOT_BLOCKS)]) \
        .astype(np.float32)


def zero_fill(k, eng, zeros, done):
    first, parts = 2 * S // P, 4
    n = (SLOT_BLOCKS - first) // parts
    for i in range(parts):
        a = (first + i * n) * P
        eng.dma_start(k.slot_out[a:a + n * P, :].rearrange("(b p) d -> p b d", p=P),
                      zeros.unsqueeze(1).to_broadcast([P, n, D])).then_inc(done, 16)
    return 16 * parts


class Core:

    def __init__(self, nc, ctx, ins):
        self.nc, self.ctx, self.ins, self.sems = nc, ctx, ins, []

    def sb(self, name, shape, dtype=F32, ctx=None):
        return (ctx or self.ctx).enter_context(self.nc.sbuf_tensor(name, shape, dtype))

    def ps(self, name, shape, dtype=F32, ctx=None):
        return (ctx or self.ctx).enter_context(self.nc.psum_tensor(name, shape, dtype))

    def sem(self, name):
        self.sems.append(self.nc.alloc_semaphore(name))
        return self.sems[-1]

    def clear_semaphores(self):
        self.nc.clear_and_free_semaphores(self.sems)
        self.nc.all_engine_barrier()
        self.sems = []

    def const(self, name):
        return self.consts[:, CONSTS.index(name), :]

    def pv(self, name, i=0, n=1):
        at = PV_AT[name] + i
        return self.params[:, at:at + n]


def chain(eng, sem):
    count = [0]

    def step(ins):
        count[0] += 1
        ins.then_inc(sem, 1)
        eng.wait_ge(sem, count[0])

    return step



def product(nc, out, lhsT, rhs, start, stop):
    (lh, ll), (rh, rl) = lhsT, rhs
    nc.tensor.matmul(out, lhsT=lh, rhs=rh, start=start, stop=False)
    nc.tensor.matmul(out, lhsT=lh, rhs=rl, start=False, stop=False)
    return nc.tensor.matmul(out, lhsT=ll, rhs=rh, start=False, stop=stop)


def part(pair, *index):
    return tuple(pair[(slice(None), n, *index)] for n in range(2))


MOD_PIECES, FIRST_PIECES = 9 * D // HALF, 3 * D // HALF


def modulation_source(k, j):
    n1 = 6 * D // HALF
    w, j = (k.ins["ada_w"], j) if j < n1 else (k.ins["ada_w_2"], j - n1)
    return w[:, j * HALF:(j + 1) * HALF].rearrange("(c p) n -> p c n", p=P)


def modulation_products(k, step, w, sums, j):
    for c in range(KC):
        scale = k.csilu[:, int(j >= 6 * D // HALF), c:c + 1]
        if c == 0:
            last = k.nc.vector.tensor_scalar(sums, w[:, c, :], scale, None, ALU.mult)
        else:
            last = k.nc.vector.scalar_tensor_tensor(sums, in0=w[:, c, :], scalar=scale, in1=sums,
                                                    op0=ALU.mult, op1=ALU.add)
        if c < KC - 1:
            step(last)
    return last


def modulation_sums(k, out, sums, j):
    for m in range(HALF // P):
        col = j * (HALF // P) + m
        last = k.nc.tensor.matmul(out[:, col:col + 1], lhsT=sums[:, m * P:(m + 1) * P],
                                  rhs=k.const("ones")[:, 0:1], start=True, stop=True)
    return last


def modulated_gain(k, n):
    scale_at, gain = ((8, "norm_mix_g"), (32, "norm_ffn_g"), (56, "norm_g_2"))[n]
    return k.nc.vector.scalar_tensor_tensor(
        k.gain[:, n * KC:(n + 1) * KC], in0=k.mod[:, scale_at:scale_at + KC], scalar=1.0,
        in1=k.pv(gain, 0, KC), op0=ALU.add, op1=ALU.mult)


def modulation_stage(k):
    nc, ins = k.nc, k.ins
    slots = 4
    with ExitStack() as ctx:
        ring = k.sb("ada_ring", [P, slots, KC, HALF], ctx=ctx)
        parts, mod_mm = k.sb("mod_parts", [P, 2, HALF], ctx=ctx), k.sem("mod_mm")
        mod_ps = k.ps("mod_ps", [P, 72], ctx=ctx)
        tables_in, x_in = k.sem("tables_in"), k.sem("x_in")
        ada_in = [k.sem(f"ada_in{i}") for i in range(slots)]
        ada_used, c_ready, mod_done = k.sem("ada_used"), k.sem("c_ready"), k.sem("mod_done")
        dve_step = k.sem("mod_dve_step")
        block = ctx.enter_context(nc.Block())

        @block.sync
        def _(sp):
            for j in range(FIRST_PIECES):
                if j >= slots:
                    sp.wait_ge(ada_used, j - slots + 1)
                sp.dma_start(ring[:, j % slots], modulation_source(k, j)).then_inc(ada_in[j % slots], 16)

        @block.scalar
        def _(act):
            act.dma_start(k.params[:, :], ins["params"]).then_inc(tables_in, 16)
            act.dma_start(k.consts[:, :, :], ins["consts"]).then_inc(tables_in, 16)
            act.dma_start(k.x_tok[:, :, :], ins["x"].rearrange("(t p) d -> p t d", p=P)).then_inc(x_in, 16)
            act.wait_ge(tables_in, 32)
            nc.scalar.activation(k.csilu[:, 0, :], k.pv("c", 0, KC), ACT.Silu)
            nc.scalar.activation(k.csilu[:, 1, :], k.pv("c_2", 0, KC), ACT.Silu).then_inc(c_ready, 1)

        @block.vector
        def _(dve):
            step = chain(dve, dve_step)
            dve.wait_ge(c_ready, 1)
            for j in range(FIRST_PIECES):
                dve.wait_ge(ada_in[j % slots], 16 * (j // slots + 1))
                if j >= 2:
                    dve.wait_ge(mod_mm, j - 1)
                modulation_products(k, step, ring[:, j % slots], parts[:, j % 2, :], j).then_inc(ada_used, 1)
            dve.wait_ge(tables_in, 32)
            dve.wait_ge(x_in, 16)
            dve.wait_ge(mod_mm, FIRST_PIECES)
            step(nc.vector.tensor_tensor(k.mod[:, 0:3 * KC], mod_ps[:, 0:3 * KC], k.pv("ada_b", 0, 3 * KC), ALU.add))
            modulated_gain(k, 0).then_inc(mod_done, 1)
            dve.wait_ge(mod_done, 1)

        @block.tensor
        def _(pe):
            pe.wait_ge(tables_in, 32)
            for j in range(FIRST_PIECES):
                pe.wait_ge(ada_used, j + 1)
                modulation_sums(k, mod_ps, parts[:, j % 2, :], j).then_inc(mod_mm, 1)


def norm_transpose_stage(k, name, src, gain, shift, normed_dram=None, raw_dram=None):
    nc = k.nc
    with ExitStack() as ctx:
        normed = k.sb(f"{name}_normed", [P, TT, D], ctx=ctx)
        full = k.sb(f"{name}_full", [P, 4, HALF], ctx=ctx)
        ss = k.sb(f"{name}_ss", [P, TT], ctx=ctx)
        banks = [k.ps(f"{name}_t{i}", [P, HALF], ctx=ctx) for i in range(4)]
        squared, var_ready, std_ready = k.sem(f"{name}_squared"), k.sem(f"{name}_var"), k.sem(f"{name}_std")
        normed_ready, transposed = k.sem(f"{name}_normed_ready"), k.sem(f"{name}_transposed")
        high_out, full_out, low_out = k.sem(f"{name}_high"), k.sem(f"{name}_full_out"), k.sem(f"{name}_low")
        dve_step, stored = k.sem(f"{name}_dve_step"), k.sem(f"{name}_stored")
        block = ctx.enter_context(nc.Block())
        groups = KC * 2

        def at(g):
            return g // 2, slice(g % 2 * HALF, (g % 2 + 1) * HALF)

        @block.scalar
        def _(act):
            for t in range(TT):
                nc.scalar.activation(normed[:, t, :], src[:, t, :], ACT.Square,
                                     accum_out=ss[:, t:t + 1]).then_inc(squared, 1)
            act.wait_ge(var_ready, 1)
            nc.scalar.activation(ss[:, :], ss[:, :], ACT.Sqrt).then_inc(std_ready, 1)
            for g in range(groups):
                act.wait_ge(full_out, g + 1)
                c, span = at(g)
                nc.scalar.copy(k.hT[:, 0, c, span], full[:, g % 4]).then_inc(high_out, 1)

        @block.vector
        def _(dve):
            step = chain(dve, dve_step)
            dve.wait_ge(squared, TT)
            nc.vector.tensor_scalar(ss[:, :], ss[:, :], 1.0 / D, EPS, ALU.mult, ALU.add).then_inc(var_ready, 1)
            dve.wait_ge(std_ready, 1)
            step(nc.vector.reciprocal(ss[:, :], ss[:, :]))
            for t in range(TT):
                nc.vector.tensor_scalar(normed[:, t, :], src[:, t, :], ss[:, t:t + 1], None,
                                        ALU.mult).then_inc(normed_ready, 1)
            for g in range(groups):
                dve.wait_ge(transposed, g + 1)
                c, span = at(g)
                if g >= 4:
                    dve.wait_ge(low_out, g - 3)
                nc.vector.tensor_scalar(full[:, g % 4], banks[g % 4][:, :],
                                        gain[:, c:c + 1], shift[:, c:c + 1], ALU.mult, ALU.add) \
                    .then_inc(full_out, 1)

        @block.gpsimd
        def _(pool):
            for g in range(groups):
                c, span = at(g)
                pool.wait_ge(full_out, g + 1)
                pool.wait_ge(high_out, g + 1)
                nc.gpsimd.tensor_tensor(k.hT[:, 1, c, span], full[:, g % 4], k.hT[:, 0, c, span],
                                        ALU.subtract).then_inc(low_out, 1)

        @block.tensor
        def _(pe):
            for g in range(groups):
                c, h = g // 2, g % 2
                if g >= 4:
                    pe.wait_ge(full_out, g - 3)
                for t in range(4):
                    if g < 2:
                        pe.wait_ge(normed_ready, 4 * h + t + 1)
                    last = nc.tensor.transpose(banks[g % 4][:, t * P:(t + 1) * P],
                                               normed[:, 4 * h + t, c * P:(c + 1) * P], k.const("ident"))
                last.then_inc(transposed, 1)

        if normed_dram is not None:
            @block.sync
            def _(sp):
                for t in range(TT):
                    sp.wait_ge(normed_ready, t + 1)
                    sp.dma_start(normed_dram[t * P:(t + 1) * P, :], normed[:, t, :]).then_inc(stored, 16)
                sp.wait_ge(stored, 16 * TT)

        if raw_dram is not None:
            @block.sync
            def _(sp):
                sp.dma_start(raw_dram.rearrange("(t p) d -> p t d", p=P), src[:, :, :]).then_inc(stored, 16)
                sp.wait_ge(stored, 16)


def high_part(nc, out, w):
    return nc.scalar.activation(out, w, ACT.Copy, scale=W_UP)


def low_part(nc, out, w, high):
    return nc.vector.scalar_tensor_tensor(out, in0=w, scalar=W_UP, in1=high, op0=ALU.mult, op1=ALU.subtract)


def conv_stage(k):
    nc, ins = k.nc, k.ins
    pad = CONV - 1
    with ExitStack() as ctx:
        w = k.sb("cw", [P, 2, 2, KC, P], ctx=ctx)
        ws = k.sb("cws", [P, 2, 2, 2, KC, P], F16, ctx=ctx)
        b_up, w_down = k.sb("cb_up", [P, KC], ctx=ctx), k.sb("cw_down", [P, KC * CONV], ctx=ctx)
        u = k.sb("cu", [P, 2, pad + S], ctx=ctx)
        sig = k.sb("csig", [P, 2, S], ctx=ctx)
        pool_sum = k.sb("cpool_sum", [P, S], ctx=ctx)
        tap = k.sb("ctap", [P, 3, S], ctx=ctx)
        acc = [[k.ps(f"ca{i}", [P, S], ctx=ctx) for i in range(2)], [k.ps("cg", [P, S], ctx=ctx)] * 2]
        conv_ps = k.ps("c_taps", [P, S], ctx=ctx)
        u_parts = k.sb("cu_parts", [P, 2, 2, pad + S], F16, ctx=ctx)
        diag = k.sb("cdiag", [P, 2, 2, PE_TAPS, P], F16, ctx=ctx)
        w_up = k.sb("cw_up", [P, KC * CONV], ctx=ctx)
        w_in = [k.sem(f"cw_in{i}") for i in range(2)]
        mm_done, sig_done, u_done, conv_done = k.sem("c_mm"), k.sem("c_sig"), k.sem("c_u"), k.sem("c_conv")
        pads, tap_done, tap_added, dve_step = k.sem("c_pads"), k.sem("c_tap"), k.sem("c_tap_added"), k.sem("c_dve")
        zeros, zero_sb, zeroed = k.sb("c_zeros", [P, D], ctx=ctx), k.sem("c_zero_sb"), k.sem("c_zeroed")
        high, low, params_up = k.sem("c_high"), k.sem("c_low"), k.sem("c_params_up")
        u_high, u_low, taps_done, taps_read = (k.sem(f"c_{n}") for n in ("u_high", "u_low", "taps_done", "taps_read"))
        diag_high, diag_low = k.sem("c_diag_high"), k.sem("c_diag_low")
        pool_taps = 8
        block = ctx.enter_context(nc.Block())

        @block.sync
        def _(sp):
            for i in range(KC):
                if i >= 2:
                    sp.wait_ge(low, i - 1)
                    sp.wait_ge(high, i - 1)
                for n in range(2):
                    sp.dma_start(w[:, i % 2, n], ins["conv_w_in"][n * KC + i]).then_inc(w_in[i % 2], 16)
            sp.wait_ge(zero_sb, 1)
            sp.wait_ge(zeroed, zero_fill(k, sp, zeros[:, :], zeroed))

        @block.tensor
        def _(pe):
            def taps(i):
                for sem in (u_high, u_low, diag_high, diag_low):
                    pe.wait_ge(sem, i + 1)
                if i:
                    pe.wait_ge(taps_read, i)
                for h in range(2):
                    for j in range(PE_TAPS):
                        at = pool_taps + j + h * HALF
                        last = product(nc, conv_ps[:, h * HALF:(h + 1) * HALF], part(diag, i % 2, j),
                                       part(u_parts, i % 2, slice(at, at + HALF)), j == 0, j == PE_TAPS - 1)
                last.then_inc(taps_done, 1)

            for i in range(KC):
                pe.wait_ge(high, i + 1)
                pe.wait_ge(low, i + 1)
                if i >= 2:
                    pe.wait_ge(u_done, i - 1)
                for n in (0, 1):
                    if n == 1 and i:
                        pe.wait_ge(sig_done, i)
                        taps(i - 1)
                    for h in range(2):
                        for c in range(KC):
                            last = product(nc, acc[n][i % 2][:, h * HALF:(h + 1) * HALF],
                                           part(ws, i % 2, n, c), part(k.hT, c, slice(h * HALF, (h + 1) * HALF)),
                                           c == 0, c == KC - 1)
                last.then_inc(mm_done, 1)
            taps(KC - 1)

        @block.scalar
        def _(act):
            def diagonals(i):
                if i >= 2:
                    act.wait_ge(taps_done, i - 1)
                for j in range(PE_TAPS):
                    at = i * CONV + pool_taps + j
                    last = nc.scalar.activation(diag[:, 0, i % 2, j, :], k.const("ident"), ACT.Copy,
                                                scale=w_up[:, at:at + 1])
                last.then_inc(diag_high, 1)

            def split(i):
                act.wait_ge(w_in[i % 2], 32 * (i // 2 + 1))
                if i >= 2:
                    act.wait_ge(mm_done, i - 1)
                high_part(nc, ws[:, 0, i % 2], w[:, i % 2]).then_inc(high, 1)

            split(0)
            for i in range(KC):
                if i + 1 < KC:
                    split(i + 1)
                act.wait_ge(pads, 5)
                diagonals(i)
                act.wait_ge(mm_done, i + 1)
                if i >= 2:
                    act.wait_ge(u_done, i - 1)
                nc.scalar.activation(sig[:, i % 2], acc[1][i % 2][:, :], ACT.Sigmoid, scale=1.0 / W_UP,
                                     bias=k.pv("conv_b_in", KC + i)).then_inc(sig_done, 1)
                act.wait_ge(u_done, i + 1)
                nc.scalar.activation(u_parts[:, 0, i % 2, :], u[:, i % 2, :], ACT.Copy, scale=1.0 / W_UP) \
                    .then_inc(u_high, 1)
                for j in range(pool_taps):
                    n = i * pool_taps + j
                    if n >= 3:
                        act.wait_ge(tap_added, n - 2)
                    nc.scalar.activation(tap[:, n % 3], u[:, i % 2, j:j + S], ACT.Copy,
                                         scale=w_down[:, i * CONV + j:i * CONV + j + 1]).then_inc(tap_done, 1)

        @block.gpsimd
        def _(pool):
            nc.gpsimd.memset(zeros[:, :], 0.0).then_inc(zero_sb, 1)
            for i in range(KC):
                for j in range(pool_taps):
                    n = i * pool_taps + j
                    pool.wait_ge(tap_done, n + 1)
                    if j == 0:
                        if i:
                            pool.wait_ge(conv_done, i)
                        nc.gpsimd.tensor_copy(pool_sum[:, :], tap[:, n % 3]).then_inc(tap_added, 1)
                    else:
                        pool.wait_ge(tap_added, n)
                        nc.gpsimd.tensor_tensor(pool_sum[:, :], pool_sum[:, :], tap[:, n % 3], ALU.add) \
                            .then_inc(tap_added, 1)

        @block.vector
        def _(dve):
            step = chain(dve, dve_step)
            for i in range(2):
                nc.vector.memset(u[:, i, 0:pad], 0.0).then_inc(pads, 1)
            nc.vector.tensor_scalar(b_up[:, :], k.pv("conv_b_in", 0, KC), W_UP, None, ALU.mult).then_inc(pads, 1)
            nc.vector.tensor_scalar(w_down[:, :], k.pv("conv_w_dw", 0, KC * CONV), 1.0 / W_UP, None,
                                    ALU.mult).then_inc(pads, 1)
            nc.vector.tensor_scalar(w_up[:, :], k.pv("conv_w_dw", 0, KC * CONV), W_UP, None, ALU.mult).then_inc(pads, 1)
            dve.wait_ge(pads, 5)

            def split(i):
                dve.wait_ge(high, i + 1)
                low_part(nc, ws[:, 1, i % 2].rearrange("p a c q -> p (a c q)"),
                         w[:, i % 2].rearrange("p a c q -> p (a c q)"),
                         ws[:, 0, i % 2].rearrange("p a c q -> p (a c q)")).then_inc(low, 1)

            split(0)
            for i in range(KC):
                if i + 1 < KC:
                    split(i + 1)
                dve.wait_ge(diag_high, i + 1)
                for j in range(PE_TAPS):
                    at = i * CONV + pool_taps + j
                    last = nc.vector.scalar_tensor_tensor(diag[:, 1, i % 2, j, :], in0=k.const("ident"),
                                                          scalar=w_up[:, at:at + 1], in1=diag[:, 0, i % 2, j, :],
                                                          op0=ALU.mult, op1=ALU.subtract)
                last.then_inc(diag_low, 1)
                dve.wait_ge(sig_done, i + 1)
                if i >= 2:
                    dve.wait_ge(tap_done, (i - 1) * pool_taps)
                nc.vector.scalar_tensor_tensor(
                    u[:, i % 2, pad:pad + S], in0=acc[0][i % 2][:, :], scalar=b_up[:, i:i + 1],
                    in1=sig[:, i % 2], op0=ALU.add, op1=ALU.mult).then_inc(u_done, 1)
                dve.wait_ge(u_done, i + 1)
                dve.wait_ge(u_high, i + 1)
                nc.vector.scalar_tensor_tensor(u_parts[:, 1, i % 2, :], in0=u[:, i % 2, :], scalar=1.0 / W_UP,
                                               in1=u_parts[:, 0, i % 2, :], op0=ALU.mult,
                                               op1=ALU.subtract).then_inc(u_low, 1)
                y = k.y[:, i, :]
                j = pool_taps + PE_TAPS
                step(nc.vector.tensor_scalar(y, u[:, i % 2, j:j + S], w_down[:, i * CONV + j:i * CONV + j + 1],
                                             k.pv("conv_b_dw", i), ALU.mult, ALU.add))
                for j in range(pool_taps + PE_TAPS + 1, CONV):
                    step(nc.vector.scalar_tensor_tensor(
                        y, in0=u[:, i % 2, j:j + S], scalar=w_down[:, i * CONV + j:i * CONV + j + 1], in1=y,
                        op0=ALU.mult, op1=ALU.add))
                dve.wait_ge(tap_added, (i + 1) * pool_taps)
                step(nc.vector.tensor_tensor(y, y, pool_sum[:, :], ALU.add))
                dve.sem_inc(conv_done, 1)
                dve.wait_ge(taps_done, i + 1)
                nc.vector.scalar_tensor_tensor(y, in0=conv_ps[:, :], scalar=1.0 / W_UP, in1=y, op0=ALU.mult,
                                               op1=ALU.add).then_inc(taps_read, 1)


def conv_norm_stage(k):
    nc, ins = k.nc, k.ins
    with ExitStack() as ctx:
        sq = k.sb("ln_sq", [P, 4, HALF], ctx=ctx)
        rstd = k.sb("ln_rstd", [P, 2, HALF], ctx=ctx)
        mean_ps, var_ps = k.ps("ln_mean", [P, 2, HALF], ctx=ctx), k.ps("ln_var", [P, 2, HALF], ctx=ctx)
        mean_done, centred, squared, sq_used = (k.sem(n) for n in ("ln_mean_done", "ln_centred", "ln_squared", "ln_sq_used"))
        var_sb, std_done, scaled, activated, high, dve_step = (
            k.sem(n) for n in ("ln_var_sb", "ln_std", "ln_scaled", "ln_activated", "ln_high", "ln_dve"))
        high_pool = k.sem("ln_high_pool")
        block = ctx.enter_context(nc.Block())
        pieces = [(h, c) for h in range(2) for c in range(KC)]
        y = lambda h, c: k.y[:, c, h * HALF:(h + 1) * HALF]

        @block.sync
        def _(sp):
            for c in range(KC):
                sp.dma_start(k.next_w[:, c, :], ins["conv_w_out"][c * P:(c + 1) * P, :]).then_inc(k.next_w_in, 16)

        @block.tensor
        def _(pe):
            for h, c in pieces:
                last = nc.tensor.matmul(mean_ps[:, h, :], lhsT=k.const("mean_d"), rhs=y(h, c),
                                        start=c == 0, stop=c == KC - 1)
                if c == KC - 1:
                    last.then_inc(mean_done, 1)
            for n, (h, c) in enumerate(pieces):
                pe.wait_ge(squared, n + 1)
                nc.tensor.matmul(var_ps[:, h, :], lhsT=k.const("mean_d"), rhs=sq[:, n % 4], start=c == 0,
                                 stop=c == KC - 1).then_inc(sq_used, 1)

        @block.vector
        def _(dve):
            step = chain(dve, dve_step)
            for n, (h, c) in enumerate(pieces):
                dve.wait_ge(mean_done, h + 1)
                nc.vector.tensor_tensor(y(h, c), y(h, c), mean_ps[:, h, :], ALU.subtract).then_inc(centred, 1)
            for h in range(2):
                dve.wait_ge(sq_used, KC * (h + 1))
                nc.vector.tensor_scalar(rstd[:, h], var_ps[:, h, :], EPS, None, ALU.add).then_inc(var_sb, 1)
                dve.wait_ge(std_done, h + 1)
                step(nc.vector.reciprocal(rstd[:, h], rstd[:, h]))
                for c in range(KC):
                    dve.wait_ge(centred, KC * h + c + 1)
                    nc.vector.tensor_tensor(y(h, c), y(h, c), rstd[:, h], ALU.mult).then_inc(scaled, 1)
            for n, (h, c) in enumerate(pieces):
                dve.wait_ge((high, high_pool)[n % 2], n // 2 + 1)
                nc.vector.tensor_tensor(k.hT[:, 1, c, h * HALF:(h + 1) * HALF], y(h, c),
                                        k.hT[:, 0, c, h * HALF:(h + 1) * HALF], ALU.subtract)

        @block.scalar
        def _(act):
            for n, (h, c) in enumerate(pieces):
                act.wait_ge(centred, n + 1)
                if n >= 4:
                    act.wait_ge(sq_used, n - 3)
                nc.scalar.activation(sq[:, n % 4], y(h, c), ACT.Square).then_inc(squared, 1)
            for h in range(2):
                act.wait_ge(var_sb, h + 1)
                nc.scalar.activation(rstd[:, h], rstd[:, h], ACT.Sqrt).then_inc(std_done, 1)
            for n, (h, c) in enumerate(pieces):
                act.wait_ge(scaled, n + 1)
                nc.scalar.activation(y(h, c), y(h, c), ACT.Silu, bias=k.pv("conv_ln_b", c),
                                     scale=k.pv("conv_ln_g", c)).then_inc(activated, 1)
                if n % 2:
                    act.wait_ge(activated, n)
                    h, c = pieces[n - 1]
                    nc.scalar.copy(k.hT[:, 0, c, h * HALF:(h + 1) * HALF], y(h, c)).then_inc(high, 1)

        @block.gpsimd
        def _(pool):
            for n, (h, c) in enumerate(pieces):
                if n % 2:
                    pool.wait_ge(activated, n + 1)
                    nc.gpsimd.tensor_copy(k.hT[:, 0, c, h * HALF:(h + 1) * HALF], y(h, c)).then_inc(high_pool, 1)


def token_projection_stage(k, name, actT, gate_cols, out_dram=None, x_from=None, pieces=()):
    nc, w = k.nc, k.next_w
    with ExitStack() as ctx:
        ws = k.sb(f"{name}_ws", [P, 2, KC, D], F16, ctx=ctx)
        gate = k.sb(f"{name}_gate", [P, D], ctx=ctx)
        gated = k.sb(f"{name}_gated", [P, 2, D], ctx=ctx)
        gate_ps = k.ps(f"{name}_gate_ps", [P, D], ctx=ctx)
        acc = [k.ps(f"{name}_ps{i}", [P, D], ctx=ctx) for i in range(3)]
        gate_mm, gate_sb, high, low = (k.sem(f"{name}_{n}") for n in ("gate_mm", "gate_sb", "high", "low"))
        mm_done, gated_done, added, stored = (k.sem(f"{name}_{n}") for n in ("mm", "gated_done", "added", "stored"))
        x_in = k.sem(f"{name}_x_in")
        early = 4
        if pieces:
            sums = k.sb("mod_sums", [P, 4, HALF], ctx=ctx)
            ring = k.y[:, :, :].rearrange("p c s -> p (c s)").rearrange("p (r c n) -> p r c n", r=2, c=KC)
            ada_in = [k.sem(f"late_ada_in{i}") for i in range(2)]
            ada_used, mod_mm, dve_step = k.sem("late_ada_used"), k.sem("late_mod_mm"), k.sem("late_dve_step")
        block = ctx.enter_context(nc.Block())

        @block.sync
        def _(sp):
            if x_from is not None:
                sp.dma_start(k.x_tok[:, :, :], x_from.rearrange("(t p) d -> p t d", p=P)).then_inc(x_in, 16)
            for n, j in enumerate(pieces):
                if n >= 2:
                    sp.wait_ge(ada_used, n - 1)
                sp.dma_start(ring[:, n % 2], modulation_source(k, j)).then_inc(ada_in[n % 2], 16)
            if out_dram is not None:
                for t in range(TT):
                    sp.wait_ge(added, t + 1)
                    sp.dma_start(out_dram[t * P:(t + 1) * P, :], k.x_tok[:, t, :]).then_inc(stored, 16)
                sp.wait_ge(stored, 16 * TT)

        @block.tensor
        def _(pe):
            for c in range(KC):
                last = nc.tensor.matmul(gate_ps[:, c * P:(c + 1) * P],
                                        lhsT=gate_cols[:, c:c + 1].to_broadcast([P, P]),
                                        rhs=k.const("ident"), start=True, stop=True)
            last.then_inc(gate_mm, 1)

            def products(t, c):
                for h in range(2):
                    last = product(nc, acc[t % 3][:, h * HALF:(h + 1) * HALF],
                                   part(actT, c, slice(t * P, (t + 1) * P)),
                                   part(ws, c, slice(h * HALF, (h + 1) * HALF)), c == 0, c == KC - 1)
                return last

            def piece(n):
                if n == 0:
                    pe.wait_ge(gate_sb, 1)
                pe.wait_ge(ada_used, n + 1)
                modulation_sums(k, gate_ps, sums[:, n % 4, :], pieces[n]).then_inc(mod_mm, 1)

            for c in range(KC):
                pe.wait_ge(high, c + 1)
                pe.wait_ge(low, c + 1)
                for t in range(3):
                    last = products(t, c)
                    if c == KC - 1:
                        last.then_inc(mm_done, 1)
            for n in range(early if pieces else 0):
                piece(n)
            for t in range(3, TT):
                pe.wait_ge(gated_done, t - 2)
                for c in range(KC):
                    last = products(t, c)
                last.then_inc(mm_done, 1)
                if pieces:
                    piece(early + t - 3)
            for n in range(early + TT - 3, len(pieces)):
                piece(n)

        @block.scalar
        def _(act):
            act.wait_ge(k.next_w_in, 16 * KC)
            for c in range(KC):
                high_part(nc, ws[:, 0, c, :], w[:, c, :]).then_inc(high, 1)
            act.wait_ge(gate_mm, 1)
            nc.scalar.activation(gate[:, :], gate_ps[:, :], ACT.Copy, scale=1.0 / W_UP).then_inc(gate_sb, 1)

        @block.vector
        def _(dve):
            for c in range(KC):
                dve.wait_ge(high, c + 1)
                low_part(nc, ws[:, 1, c, :], w[:, c, :], ws[:, 0, c, :]).then_inc(low, 1)

            def piece(n):
                dve.wait_ge(ada_in[n % 2], 16 * (n // 2 + 1))
                if n >= 4:
                    dve.wait_ge(mod_mm, n - 3)
                modulation_products(k, chain_step, ring[:, n % 2], sums[:, n % 4, :], pieces[n]).then_inc(ada_used, 1)

            if pieces:
                chain_step = chain(dve, dve_step)
                for n in range(early):
                    piece(n)
            dve.wait_ge(gate_sb, 1)
            for t in range(TT):
                dve.wait_ge(mm_done, t + 1)
                if t >= 2:
                    dve.wait_ge(added, t - 1)
                nc.vector.tensor_tensor(gated[:, t % 2], acc[t % 3][:, :], gate[:, :], ALU.mult) \
                    .then_inc(gated_done, 1)
                if pieces:
                    piece(early + t)
            if pieces:
                dve.wait_ge(mod_mm, len(pieces))
                nc.vector.tensor_tensor(k.mod[:, 24:48], gate_ps[:, 24:48], k.pv("ada_b", 24, 24), ALU.add)
                chain_step(nc.vector.tensor_tensor(k.mod[:, 48:72], gate_ps[:, 48:72], k.pv("ada_b_2", 0, 24), ALU.add))
                modulated_gain(k, 1)
                chain_step(modulated_gain(k, 2))

        @block.gpsimd
        def _(pool):
            if x_from is not None:
                pool.wait_ge(x_in, 16)
            for t in range(TT):
                pool.wait_ge(gated_done, t + 1)
                nc.gpsimd.tensor_tensor(k.x_tok[:, t, :], k.x_tok[:, t, :], gated[:, t % 2], ALU.add) \
                    .then_inc(added, 1)


def router_stage(k):
    nc, ins = k.nc, k.ins
    NL = GROUPS + EXPERTS
    with ExitStack() as ctx:
        sb = lambda n, s, d=F32: k.sb(f"r_{n}", s, d, ctx=ctx)
        ws = sb("ws", [P, 2, KC, NL], F16)
        wr, br, rows = sb("w", [P, KC, NL]), sb("b", [P, NL]), sb("rows", [P, NL + SLOT_BLOCKS])
        tokid, zeros = sb("tokid", [P, TT]), sb("zeros", [SLOT_BLOCKS, P])
        lg, el, tmp = sb("lg", [P, TT, NL]), sb("el", [P, TT, EXPERTS]), sb("tmp", [P, TT, EXPERTS])
        oh1, oh2, mask = sb("oh1", [P, TT, EXPERTS]), sb("oh2", [P, TT, EXPERTS]), sb("mask", [P, TT, EXPERTS])
        goh, gex = sb("goh", [P, TT, GROUPS]), sb("gex", [P, TT, GROUPS])
        c1, m1, m2, e2, gp = (sb(n, [P, TT]) for n in ("c1", "m1", "m2", "e2", "gp"))
        cnt, nb, cum, start, one = (sb(n, [P, EXPERTS]) for n in ("cnt", "nb", "cum", "start", "one"))
        dfull = sb("dfull", [P, TT, EXPERTS])
        dest_f = sb("dest_f", [P, 2, TT])
        le = sb("le", [P, SLOT_BLOCKS, EXPERTS])
        bef, pr = sb("bef", [P, SLOT_BLOCKS]), sb("pr", [P, SLOT_BLOCKS // 2])
        prs = sb("prs", [P, 1])
        table = sb("table", [SLOT_BLOCKS, P])
        lg_ps = k.ps("r_lg_ps", [P, TT, 64], ctx=ctx)
        pos_ps = k.ps("r_pos_ps", [P, TT, EXPERTS], ctx=ctx)
        cnt_ps = k.ps("r_cnt_ps", [P, EXPERTS], ctx=ctx)
        tab_ps = k.ps("r_tab_ps", [P, SLOT_BLOCKS], ctx=ctx)
        r_in, lg_done, ex_in, ex_done, e2_in, e2_done = (k.sem(f"r_{n}") for n in (
            "in", "lg_done", "ex_in", "ex_done", "e2_in", "e2_done"))
        mask_ready, pos_done, dest_ready, zero_sb, zeroed, scattered, tab_in, tab_done, dve_step = (
            k.sem(f"r_{n}") for n in ("mask_ready", "pos_done", "dest_ready", "zero_sb", "zeroed", "scattered",
                                      "tab_in", "tab_done", "dve_step"))
        split = k.sem("r_split")
        desc_g, desc_e = rows[:, 0:GROUPS], rows[:, GROUPS:NL]
        viota = rows[:, NL:NL + SLOT_BLOCKS]
        block = ctx.enter_context(nc.Block())

        @block.sync
        def _(sp):
            sp.dma_start(wr[:, :, :], ins["router_w"].rearrange("(c p) n -> p c n", p=P)).then_inc(r_in, 16)
            sp.dma_start(br[:, :], ins["router_b"].partition_broadcast(P)).then_inc(r_in, 16)
            sp.dma_start(rows[:, :], ins["rows"].partition_broadcast(P)).then_inc(r_in, 16)
            sp.dma_start(tokid[:, :], ins["token_ids"]).then_inc(r_in, 16)
            sp.wait_ge(zero_sb, 1)
            sp.dma_start(k.table_dram.rearrange("(b p) o -> b (p o)", p=P), zeros[:, :]).then_inc(zeroed, 16)
            sp.wait_ge(scattered, 16 * 2 * TT)
            sp.dma_start(table[:, :], k.table_dram.rearrange("(b p) o -> b (p o)", p=P)).then_inc(tab_in, 16)

        @block.tensor
        def _(pe):
            pe.wait_ge(r_in, 64)
            pe.wait_ge(split, 2)
            for t in range(TT):
                for c in range(KC):
                    last = product(nc, lg_ps[:, t, 0:NL], part(k.hT, c, slice(t * P, (t + 1) * P)),
                                   part(ws, c), c == 0, c == KC - 1)
            last.then_inc(lg_done, 1)
            pe.wait_ge(mask_ready, 1)
            for t in range(TT):
                for j in range(t):
                    nc.tensor.matmul(pos_ps[:, t, :], lhsT=k.const("ones"), rhs=mask[:, j, :],
                                     start=j == 0, stop=False)
                nc.tensor.matmul(pos_ps[:, t, :], lhsT=k.const("before"), rhs=mask[:, t, :],
                                 start=t == 0, stop=True)
            for j in range(TT):
                last = nc.tensor.matmul(cnt_ps[:, :], lhsT=k.const("ones"), rhs=mask[:, j, :],
                                        start=j == 0, stop=j == TT - 1)
            last.then_inc(pos_done, 1)
            pe.wait_ge(tab_in, 16)
            nc.tensor.transpose(tab_ps[:, :], table[:, :], k.const("ident")[0:SLOT_BLOCKS, 0:SLOT_BLOCKS]) \
                .then_inc(tab_done, 1)

        @block.scalar
        def _(act):
            act.wait_ge(r_in, 64)
            high_part(nc, ws[:, 0], wr[:, :, :]).then_inc(split, 1)
            act.wait_ge(ex_in, 1)
            nc.scalar.activation(gex[:, :, :], gex[:, :, :], ACT.Exp).then_inc(ex_done, 1)
            act.wait_ge(e2_in, 1)
            nc.scalar.activation(e2[:, :], e2[:, :], ACT.Exp).then_inc(e2_done, 1)

        @block.vector
        def _(dve):
            step = chain(dve, dve_step)
            v = nc.vector

            def bc(x, n):
                return x.unsqueeze(len(x.shape)).to_broadcast([*x.shape, n])

            def first_max(scores, desc, n, top, onehot):
                step(v.tensor_reduce(top[:, :], scores, AX.X, ALU.max))
                step(v.tensor_tensor(onehot, scores, bc(top[:, :], n), ALU.is_equal))
                step(v.tensor_tensor(onehot, onehot, desc.unsqueeze(1).to_broadcast([P, TT, n]), ALU.mult))
                step(v.tensor_reduce(c1[:, :], onehot, AX.X, ALU.max))
                step(v.tensor_tensor(onehot, onehot, bc(c1[:, :], n), ALU.is_equal))

            step(v.memset(one[:, :], 1.0))
            v.memset(zeros[:, :], 0.0).then_inc(zero_sb, 1)
            dve.wait_ge(r_in, 64)
            dve.wait_ge(split, 1)
            low_part(nc, ws[:, 1].rearrange("p c n -> p (c n)"), wr[:, :, :].rearrange("p c n -> p (c n)"),
                     ws[:, 0].rearrange("p c n -> p (c n)")).then_inc(split, 1)
            dve.wait_ge(lg_done, 1)
            step(v.tensor_scalar(lg[:, :, :], lg_ps[:, :, 0:NL], 1.0 / W_UP, None, ALU.mult))
            step(v.tensor_tensor(lg[:, :, :], lg[:, :, :], br[:, :].unsqueeze(1).to_broadcast([P, TT, NL]), ALU.add))
            gl = lg[:, :, 0:GROUPS]
            first_max(gl, desc_g, GROUPS, m1, goh[:, :, :])
            v.tensor_tensor(gex[:, :, :], gl, bc(m1[:, :], GROUPS), ALU.subtract).then_inc(ex_in, 1)
            step(v.tensor_scalar(goh[:, :, :], goh[:, :, :], BIG, -BIG, ALU.mult, ALU.add))
            step(v.tensor_tensor(el[:, :, :].rearrange("p t (g e) -> p t g e", g=GROUPS),
                                 lg[:, :, GROUPS:NL].rearrange("p t (g e) -> p t g e", g=GROUPS),
                                 bc(goh[:, :, :], PER_GROUP), ALU.add))
            dve.wait_ge(ex_done, 1)
            step(v.tensor_reduce(gp[:, :], gex[:, :, :], AX.X, ALU.add))
            step(v.reciprocal(gp[:, :], gp[:, :]))
            first_max(el[:, :, :], desc_e, EXPERTS, m1, oh1[:, :, :])
            step(v.scalar_tensor_tensor(el[:, :, :], in0=oh1[:, :, :], scalar=-2 * BIG, in1=el[:, :, :],
                                        op0=ALU.mult, op1=ALU.add))
            first_max(el[:, :, :], desc_e, EXPERTS, m2, oh2[:, :, :])
            v.tensor_tensor(e2[:, :], m2[:, :], m1[:, :], ALU.subtract).then_inc(e2_in, 1)
            v.tensor_tensor(mask[:, :, :], oh1[:, :, :], oh2[:, :, :], ALU.add).then_inc(mask_ready, 1)
            dve.wait_ge(e2_done, 1)
            step(v.tensor_scalar(m1[:, :], e2[:, :], 1.0, None, ALU.add))
            step(v.reciprocal(m1[:, :], m1[:, :]))
            step(v.tensor_tensor(k.gates[:, 0, :], gp[:, :], m1[:, :], ALU.mult))
            step(v.tensor_tensor(k.gates[:, 1, :], k.gates[:, 0, :], e2[:, :], ALU.mult))
            dve.wait_ge(pos_done, 1)
            step(v.tensor_copy(cnt[:, :], cnt_ps[:, :]))
            step(v.tensor_scalar(nb[:, :], cnt[:, :], 0.0, None, ALU.is_gt))
            for m in range(1, S // P):
                step(v.scalar_tensor_tensor(nb[:, :], in0=cnt[:, :], scalar=float(m * P), in1=nb[:, :],
                                            op0=ALU.is_gt, op1=ALU.add))
            step(v.tensor_tensor_scan(cum[:, :], one[:, :], nb[:, :], 0.0, ALU.mult, ALU.add))
            step(v.tensor_tensor(start[:, :], cum[:, :], nb[:, :], ALU.subtract))
            step(v.tensor_scalar(start[:, :], start[:, :], float(P), None, ALU.mult))
            step(v.tensor_tensor(dfull[:, :, :], pos_ps[:, :, :],
                                 start[:, :].unsqueeze(1).to_broadcast([P, TT, EXPERTS]), ALU.add))
            for n, oh in enumerate((oh1, oh2)):
                step(v.tensor_tensor(tmp[:, :, :], oh[:, :, :], dfull[:, :, :], ALU.mult))
                step(v.tensor_reduce(dest_f[:, n, :], tmp[:, :, :], AX.X, ALU.add))
            v.tensor_copy(k.dest[:, :, :], dest_f[:, :, :]).then_inc(dest_ready, 1)
            step(v.tensor_tensor(le[:, :, :], cum[:, :].unsqueeze(1).to_broadcast([P, SLOT_BLOCKS, EXPERTS]),
                                 bc(viota, EXPERTS), ALU.is_le))
            step(v.tensor_reduce(bef[:, :], le[:, :, :], AX.X, ALU.add))
            step(v.tensor_scalar(bef[:, :], bef[:, :], float(EXPERTS - 1), None, ALU.min))
            step(v.tensor_copy(k.block_expert[:, :], bef[:, :]))
            step(v.tensor_scalar(pr[:, :], viota[:, 0:SLOT_BLOCKS // 2], 2.0, cum[:, EXPERTS - 1:EXPERTS],
                                 ALU.mult, ALU.is_lt))
            step(v.tensor_reduce(prs[:, :], pr[:, :], AX.X, ALU.add))
            step(v.tensor_scalar(prs[:, :], prs[:, :], -3.0, None, ALU.add))
            step(v.tensor_copy(k.pairs[:, :], prs[:, :]))
            dve.wait_ge(tab_done, 1)
            step(v.tensor_copy(k.slot_token[:, :], tab_ps[:, :]))

        @block.gpsimd
        def _(pool):
            pool.wait_ge(dest_ready, 1)
            pool.wait_ge(r_in, 64)
            pool.wait_ge(zeroed, 16)
            for n in range(2):
                for t in range(TT):
                    nc.gpsimd.indirect_dma_start(
                        out=k.table_dram, out_offset=bass.IndirectOffsetOnAxis(ap=k.dest[:, n, t:t + 1], axis=0),
                        in_=tokid[:, t:t + 1], in_offset=None).then_inc(scattered, 16)


def experts_stage(k):
    nc, ins = k.nc, k.ins
    gain, shift = k.gain[:, KC:2 * KC], k.mod[:, 3 * KC:4 * KC]
    FC = FFN // P
    least = 2 * S // P // 2
    with ExitStack() as ctx:
        sb = lambda n, s, d=F32: k.sb(f"m_{n}", s, d, ctx=ctx)
        wg, wu = sb("wg", [P, 2, KC, FFN]), sb("wu", [P, 2, KC, FFN])
        wd = sb("wd", [P, 2, FC, D])
        idx = sb("idx", [P, 2], U32)
        xg, xT = sb("xg", [P, 2, D]), sb("xT", [P, 2, KC, P])
        sg, hid, hidT, y = sb("sg", [P, FFN]), sb("hid", [P, FFN]), sb("hidT", [P, FC, P]), sb("y", [P, 2, D])
        xt_ps = [k.ps(f"m_xt{i}", [P, HALF], ctx=ctx) for i in range(2)]
        g_ps, u_ps, ht_ps = (k.ps(f"m_{n}_ps", [P, FFN], ctx=ctx) for n in ("g", "u", "ht"))
        y_ps = k.ps("m_y_ps", [P, D], ctx=ctx)
        two = lambda n: [k.sem(f"m_{n}{b}") for b in range(2)]
        g_in, u_in, d_in, x_in, y_stored = (two(n) for n in ("g_in", "u_in", "d_in", "x_in", "y_stored"))
        turn = k.sem("m_turn")
        idx_ready, xt_done, xt_sb, g_done, u_done, sg_done, hid_done, ht_done, ht_sb, y_done, y_act, y_dve = (
            k.sem(f"m_{n}") for n in ("idx_ready", "xt_done", "xt_sb", "g_done", "u_done", "sg_done",
                                      "hid_done", "ht_done", "ht_sb", "y_done", "y_act", "y_dve"))
        block = ctx.enter_context(nc.Block())

        def count(eng):
            return eng.value_load(k.pairs[0:1, 0:1], min_val=least - 3, max_val=SLOT_BLOCKS // 2 - 3) + 3

        @block.sync
        def _(sp):
            pairs = count(sp)

            def load(v, b, first):
                e = sp.value_load(k.block_expert[0:1, v:v + 1] if first else k.block_expert[0:1, bass.ds(v, 1)],
                                  min_val=0, max_val=EXPERTS - 1)
                if not first:
                    sp.wait_ge(g_done, v - 1)
                sp.dma_start(wg[:, b], ins["moe_w_gate"][bass.ds(e, 1)].rearrange("e (c p) n -> p (e c) n", p=P)) \
                    .then_inc(g_in[b], 16)
                if not first:
                    sp.wait_ge(u_done, v - 1)
                sp.dma_start(wu[:, b], ins["moe_w_up"][bass.ds(e, 1)].rearrange("e (c p) n -> p (e c) n", p=P)) \
                    .then_inc(u_in[b], 16)
                if not first:
                    sp.wait_ge(y_done, v - 1)
                sp.dma_start(wd[:, b], ins["moe_w_down"][bass.ds(e, 1)].rearrange("e (c p) n -> p (e c) n", p=P)) \
                    .then_inc(d_in[b], 16)

            for b in range(2):
                load(b, b, True)
            with sp.Fori(1, pairs) as i:
                for b in range(2):
                    load(2 * i + b, b, False)

        @block.gpsimd
        def _(pool):
            pairs = count(pool)

            def gather(column, b):
                nc.gpsimd.tensor_copy(idx[:, b:b + 1], column).then_inc(idx_ready, 1)

            def fetch(b):
                nc.gpsimd.indirect_dma_start(
                    out=xg[:, b, :], out_offset=None, in_=k.normed_dram,
                    in_offset=bass.IndirectOffsetOnAxis(ap=idx[:, b:b + 1], axis=0)).then_inc(x_in[b], 16)

            for b in range(2):
                gather(k.slot_token[:, b:b + 1], b)
                pool.wait_ge(idx_ready, b + 1)
                fetch(b)
            with pool.Fori(1, pairs) as i:
                for b in range(2):
                    pool.wait_ge(xt_done, 2 * i + b - 1)
                    gather(k.slot_token[:, bass.ds(2 * i + b, 1)], b)
                    pool.wait_ge(idx_ready, 2 * i + b + 1)
                    pool.sem_inc(turn, 1)
                    fetch(b)


        @block.tensor
        def _(pe):
            pairs = count(pe)

            def X(b, r):
                pe.wait_ge(x_in[b], 16 * r + 16)
                for c in range(KC):
                    last = nc.tensor.transpose(xt_ps[c // 4][:, (c % 4) * P:(c % 4 + 1) * P],
                                               xg[:, b, c * P:(c + 1) * P], k.const("ident"))
                last.then_inc(xt_done, 1)

            def G(n, b, r, first=False):
                pe.wait_ge(xt_sb, n + 1)
                pe.wait_ge(g_in[b], 16 * r + 16)
                if not first:
                    pe.wait_ge(sg_done, n)
                for c in range(KC):
                    last = nc.tensor.matmul(g_ps[:, :], lhsT=xT[:, b, c, :], rhs=wg[:, b, c, :],
                                            start=c == 0, stop=c == KC - 1)
                last.then_inc(g_done, 1)

            def U(b, r):
                pe.wait_ge(u_in[b], 16 * r + 16)
                for c in range(KC):
                    last = nc.tensor.matmul(u_ps[:, :], lhsT=xT[:, b, c, :], rhs=wu[:, b, c, :],
                                            start=c == 0, stop=c == KC - 1)
                last.then_inc(u_done, 1)

            def H(n):
                pe.wait_ge(hid_done, n + 1)
                for c in range(FC):
                    last = nc.tensor.transpose(ht_ps[:, c * P:(c + 1) * P], hid[:, c * P:(c + 1) * P],
                                               k.const("ident"))
                last.then_inc(ht_done, 1)

            def Y(n, b, r, first=False):
                pe.wait_ge(ht_sb, n + 1)
                pe.wait_ge(d_in[b], 16 * r + 16)
                if not first:
                    pe.wait_ge(y_act, n)
                    pe.wait_ge(y_dve, n)
                for h in range(2):
                    for c in range(FC):
                        last = nc.tensor.matmul(y_ps[:, h * HALF:(h + 1) * HALF], lhsT=hidT[:, c, :],
                                                rhs=wd[:, b, c, h * HALF:(h + 1) * HALF],
                                                start=c == 0, stop=c == FC - 1)
                last.then_inc(y_done, 1)

            X(0, 0)
            G(0, 0, 0, first=True)
            X(1, 0)
            U(0, 0)
            G(1, 1, 0)
            H(0)
            X(0, 1)
            U(1, 0)
            Y(0, 0, 0, first=True)
            with pe.Fori(1, pairs - 1) as i:
                for b in range(2):
                    n = 2 * i + b
                    G(n, b, i)
                    H(n - 1)
                    X(1 - b, i + b)
                    U(b, i)
                    Y(n - 1, 1 - b, i - 1 + b)
            n, i = 2 * (pairs - 1), pairs - 1
            G(n, 0, i)
            H(n - 1)
            X(1, i)
            U(0, i)
            Y(n - 1, 1, i - 1)
            G(n + 1, 1, i)
            H(n)
            U(1, i)
            Y(n, 0, i)
            H(n + 1)
            Y(n + 1, 1, i)

        @block.scalar
        def _(act):
            pairs = count(act)

            def silu(n, first=False):
                act.wait_ge(g_done, n + 1)
                if not first:
                    act.wait_ge(hid_done, n)
                nc.scalar.activation(sg[:, :], g_ps[:, :], ACT.Silu).then_inc(sg_done, 1)

            def hidden(n):
                act.wait_ge(ht_done, n + 1)
                nc.scalar.copy(hidT[:, :, :], ht_ps[:, :].rearrange("p (c q) -> p c q", q=P)).then_inc(ht_sb, 1)

            def out(n, b, r, first=False):
                act.wait_ge(y_done, n + 1)
                if not first:
                    act.wait_ge(y_stored[b], 32 * r)
                nc.scalar.copy(y[:, b, 0:HALF], y_ps[:, 0:HALF]).then_inc(y_act, 1)
                rows = slice(n * P, (n + 1) * P) if first else bass.ds(n * P, P)
                act.wait_ge(y_act, n + 1)
                act.dma_start(k.slot_out[rows, 0:HALF], y[:, b, 0:HALF]).then_inc(y_stored[b], 16)
                act.wait_ge(y_dve, n + 1)
                act.dma_start(k.slot_out[rows, HALF:D], y[:, b, HALF:D]).then_inc(y_stored[b], 16)

            silu(0, first=True)
            silu(1)
            hidden(0)
            out(0, 0, 0, first=True)
            silu(2)
            hidden(1)
            out(1, 1, 0, first=True)
            silu(3)
            hidden(2)
            out(2, 0, 1)
            with act.Fori(2, pairs) as i:
                for b in range(2):
                    n = 2 * i + b
                    silu(n)
                    hidden(n - 1)
                    out(n - 1, 1 - b, i - 1 + b)
            n = 2 * pairs - 1
            hidden(n)
            out(n, 1, pairs - 1)
            for b in range(2):
                act.wait_ge(y_stored[b], 32 * pairs)
            act.sem_inc(turn, 1)

        @block.vector
        def _(dve):
            pairs = count(dve)

            def turned(n, b):
                dve.wait_ge(xt_done, n + 1)
                for c in range(KC):
                    last = nc.vector.tensor_scalar(xT[:, b, c, :], xt_ps[c // 4][:, (c % 4) * P:(c % 4 + 1) * P],
                                                   gain[:, c:c + 1], shift[:, c:c + 1], ALU.mult, ALU.add)
                last.then_inc(xt_sb, 1)

            def hidden(n):
                dve.wait_ge(sg_done, n + 1)
                dve.wait_ge(u_done, n + 1)
                nc.vector.tensor_tensor(hid[:, :], sg[:, :], u_ps[:, :], ALU.mult).then_inc(hid_done, 1)

            def out(n, b, r, first=False):
                dve.wait_ge(y_done, n + 1)
                if not first:
                    dve.wait_ge(y_stored[b], 32 * r)
                nc.vector.tensor_copy(y[:, b, HALF:D], y_ps[:, HALF:D]).then_inc(y_dve, 1)

            turned(0, 0)
            turned(1, 1)
            hidden(0)
            turned(2, 0)
            hidden(1)
            out(0, 0, 0, first=True)
            turned(3, 1)
            hidden(2)
            out(1, 1, 0, first=True)
            turned(4, 0)
            hidden(3)
            out(2, 0, 1)
            with dve.Fori(2, pairs - 1) as i:
                for b in range(2):
                    n = 2 * i + b
                    turned(n + 1, 1 - b)
                    hidden(n)
                    out(n - 1, 1 - b, i - 1 + b)
            n, i = 2 * (pairs - 1), pairs - 1
            turned(n + 1, 1)
            hidden(n)
            out(n - 1, 1, i - 1)
            hidden(n + 1)
            out(n, 0, i)
            out(n + 1, 1, i)


def combine_stage(k):
    nc, ins = k.nc, k.ins
    with ExitStack() as ctx:
        sb = lambda n, s, d=F32: k.sb(f"b_{n}", s, d, ctx=ctx)
        rows = sb("rows", [P, 2, 2, D])
        part = sb("part", [P, 2, D])
        gate, final = sb("gate", [P, D]), sb("final", [P, D])
        sq, ss = sb("sq", [P, 2, D]), sb("ss", [P, TT])
        gate_ps = k.ps("b_gate_ps", [P, D], ctx=ctx)
        gate_mm, gate_sb, f_in, summed, added, squared, var, std, dve_step = (k.sem(f"b_{n}") for n in (
            "gate_mm", "gate_sb", "f_in", "summed", "added", "squared", "var", "std", "dve_step"))
        row_in = [k.sem(f"b_row_in{b}") for b in range(2)]
        rows_used = k.sem("b_rows_used")
        block = ctx.enter_context(nc.Block())

        @block.sync
        def _(sp):
            sp.dma_start(final[:, :], ins["final_g"].partition_broadcast(P)).then_inc(f_in, 16)

        @block.gpsimd
        def _(pool):
            def gather(t):
                if t >= 2:
                    pool.wait_ge(rows_used, t - 1)
                for n in range(2):
                    nc.gpsimd.indirect_dma_start(
                        out=rows[:, t % 2, n, :], out_offset=None, in_=k.slot_out,
                        in_offset=bass.IndirectOffsetOnAxis(ap=k.dest[:, n, t:t + 1], axis=0)).then_inc(row_in[t % 2], 16)
            gather(0)
            for t in range(TT):
                if t + 1 < TT:
                    gather(t + 1)
                pool.wait_ge(summed, t + 1)
                nc.gpsimd.tensor_tensor(k.x_tok[:, t, :], k.x_tok[:, t, :], part[:, t % 2], ALU.add).then_inc(added, 1)

        @block.tensor
        def _(pe):
            for c in range(KC):
                last = nc.tensor.matmul(gate_ps[:, c * P:(c + 1) * P],
                                        lhsT=k.mod[:, 5 * KC + c:5 * KC + c + 1].to_broadcast([P, P]),
                                        rhs=k.const("ident"), start=True, stop=True)
            last.then_inc(gate_mm, 1)

        @block.scalar
        def _(act):
            act.wait_ge(gate_mm, 1)
            nc.scalar.copy(gate[:, :], gate_ps[:, :]).then_inc(gate_sb, 1)
            for t in range(TT):
                act.wait_ge(added, t + 1)
                if t >= 2:
                    act.wait_ge(squared, t - 1)
                nc.scalar.activation(sq[:, t % 2], k.x_tok[:, t, :], ACT.Square,
                                     accum_out=ss[:, t:t + 1]).then_inc(squared, 1)
            act.wait_ge(var, 1)
            nc.scalar.activation(ss[:, :], ss[:, :], ACT.Sqrt).then_inc(std, 1)

        @block.vector
        def _(dve):
            step = chain(dve, dve_step)
            dve.wait_ge(gate_sb, 1)
            for t in range(TT):
                dve.wait_ge(row_in[t % 2], 32 * (t // 2 + 1))
                if t >= 2:
                    dve.wait_ge(added, t - 1)
                r = rows[:, t % 2]
                step(nc.vector.tensor_scalar(r[:, 0, :], r[:, 0, :], k.gates[:, 0, t:t + 1], None, ALU.mult))
                step(nc.vector.scalar_tensor_tensor(r[:, 0, :], in0=r[:, 1, :], scalar=k.gates[:, 1, t:t + 1],
                                                    in1=r[:, 0, :], op0=ALU.mult, op1=ALU.add))
                last = nc.vector.tensor_tensor(part[:, t % 2], r[:, 0, :], gate[:, :], ALU.mult)
                last.then_inc(summed, 1)
                dve.wait_ge(summed, t + 1)
                dve.sem_inc(rows_used, 1)
            dve.wait_ge(squared, TT)
            nc.vector.tensor_scalar(ss[:, :], ss[:, :], 1.0 / D, EPS, ALU.mult, ALU.add).then_inc(var, 1)
            dve.wait_ge(std, 1)
            step(nc.vector.reciprocal(ss[:, :], ss[:, :]))
            dve.wait_ge(f_in, 16)
            for t in range(TT):
                nc.vector.scalar_tensor_tensor(k.x_tok[:, t, :], in0=k.x_tok[:, t, :], scalar=ss[:, t:t + 1],
                                               in1=final[:, :], op0=ALU.mult, op1=ALU.mult)


def alloc_routing(k, ctx):
    k.dest = k.sb("dest", [P, 2, TT], U32, ctx=ctx)
    k.gates = k.sb("gates", [P, 2, TT], ctx=ctx)
    k.slot_token = k.sb("slot_token", [P, SLOT_BLOCKS], U32, ctx=ctx)
    k.block_expert = k.sb("block_expert", [P, SLOT_BLOCKS], I32, ctx=ctx)
    k.pairs = k.sb("pairs", [P, 1], I32, ctx=ctx)
    k.normed_dram = k.nc.dram_tensor("normed_tokens", (S, D), F32, kind="Internal").ap()
    k.table_dram = k.nc.dram_tensor("slot_table", (SLOT_BLOCKS * P, 1), F32, kind="Internal").ap()
    k.slot_out = k.nc.dram_tensor("slot_out", (SLOT_BLOCKS * P, D), F32, kind="Internal").ap()


QK_HEADS = HEADS + KV_HEADS
TOKEN_COLS = 1536 + 356
ROPE_A, ROPE_I = HD // 4 // 2, IDX_DIM // 4 // 2


def qkv_stage(k):
    nc, ins = k.nc, k.ins
    with ExitStack() as ctx:
        sb = lambda n, s, d=F32: k.sb(f"q_{n}", s, d, ctx=ctx)
        w_q, w_rest = (x[:, :, :].bitcast(F16).rearrange("p c (s n) -> p s c n", s=2) for x in (k.ws_q, k.z_att))
        raw = sb("raw", [P, 2, TOKEN_COLS])
        sq = sb("sq", [P, QK_HEADS * HD])
        gq = sb("gq", [P, 2, HD])
        lnr = sb("lnr", [P, 2, IDX_DIM])
        pos_i, pos = sb("pos_i", [P, TT], I32), sb("pos", [P, TT])
        nf = ROPE_A + ROPE_I
        freq, ang, turns = sb("freq", [P, nf]), sb("ang", [P, TT, nf]), sb("turns", [P, TT, nf])
        sin, cos = sb("sin", [P, TT, nf]), sb("cos", [P, TT, nf])
        ss, mu = sb("ss", [P, 2, QK_HEADS + 1]), sb("mu", [P, 2])
        kc_, kd, ksq = sb("kc", [P, 2, IDX_DIM]), sb("kd", [P, 2, 2, IDX_DIM]), sb("ksq", [P, IDX_DIM])
        ra, rb, rc, rd = (sb(f"rot{n}", [P, QK_HEADS, ROPE_A]) for n in range(4))
        mm = [k.ps(f"q_mm{i}", [P, HALF], ctx=ctx) for i in range(4)]
        tp = [k.ps(f"q_tp{i}", [P, HALF], ctx=ctx) for i in range(4)]
        w_in, high, low = [k.sem(f"q_w_in{n}") for n in range(2)], k.sem("q_high"), k.sem("q_low")
        rest = TOKEN_COLS - S
        small_in, mm_done, raw_done, tr_done, tr_out = (k.sem(f"q_{n}") for n in (
            "small_in", "mm_done", "raw_done", "tr_done", "tr_out"))
        sq_done, var, std, scaled, gained, ready, ang_ready, trig, dve_step, pool_step = (k.sem(f"q_{n}") for n in (
            "sq_done", "var", "std", "scaled", "gained", "ready", "ang_ready", "trig", "dve_step", "pool_step"))
        spans = [(0, 512), (512, 1024), (1024, 1536), (1536, TOKEN_COLS)]
        evac = (1, 2, 4, 5)
        block = ctx.enter_context(nc.Block())

        @block.sync
        def _(sp):
            sp.dma_start(pos_i[:, :], ins["positions"]).then_inc(small_in, 16)
            sp.dma_start(freq[:, :], ins["freq"].partition_broadcast(P)).then_inc(small_in, 16)
            sp.dma_start(gq[:, 0, :], ins["q_norm_g"].partition_broadcast(P)).then_inc(small_in, 16)
            sp.dma_start(gq[:, 1, :], ins["k_norm_g"].partition_broadcast(P)).then_inc(small_in, 16)
            sp.dma_start(lnr[:, 0, :], ins["idx_ln_g"].partition_broadcast(P)).then_inc(small_in, 16)
            sp.dma_start(lnr[:, 1, :], ins["idx_ln_b"].partition_broadcast(P)).then_inc(small_in, 16)
            for c in range(KC):
                if c >= 2:
                    sp.wait_ge(high, c - 1)
                    sp.wait_ge(low, c - 1)
                sp.dma_start(raw[:, c % 2, :], ins["w_tok"][c * P:(c + 1) * P, :]).then_inc(w_in[c % 2], 16)

        @block.tensor
        def _(pe):
            def transposes(t):
                pe.wait_ge(ready, t + 1)
                if t:
                    pe.wait_ge(tr_out, 4 * t)
                s = t % 2
                for n in range(13):
                    src = raw[:, s, n * HD:(n + 1) * HD] if n < 10 else \
                        raw[:, s, 1536 + (n - 10) * P:1536 + (n - 9) * P] if n < 12 else \
                        kd[:, s].rearrange("p a d -> p (a d)")
                    last = nc.tensor.transpose(tp[n // 4][:, (n % 4) * P:(n % 4 + 1) * P], src, k.const("ident"))
                    if n % 4 == 3 or n == 12:
                        last.then_inc(tr_done, 1)

            def span_product(t, n, c):
                a, b = spans[n]
                w_n = w_q[:, :, :, a:b] if n < 2 else w_rest[:, :, :, a - S:b - S]
                last = product(nc, mm[n][:, 0:b - a], part(k.hT, c, slice(t * P, (t + 1) * P)),
                               part(w_n, c), c == 0, c == KC - 1)
                if c == KC - 1:
                    last.then_inc(mm_done, 1)

            for c in range(KC):
                pe.wait_ge(high, c + 1)
                pe.wait_ge(low, c + 1)
                for n in range(4):
                    span_product(0, n, c)
            for t in range(1, TT):
                for n in range(4):
                    pe.wait_ge(raw_done, 5 * (t - 1) + evac[n])
                    for c in range(KC):
                        span_product(t, n, c)
                transposes(t - 1)
            transposes(TT - 1)

        @block.scalar
        def _(act):
            for c in range(KC):
                act.wait_ge(w_in[c % 2], 16 * (c // 2 + 1))
                high_part(nc, w_q[:, 0, c, :], raw[:, c % 2, 0:S])
                high_part(nc, w_rest[:, 0, c, 0:rest], raw[:, c % 2, S:TOKEN_COLS]).then_inc(high, 1)
            act.wait_ge(ang_ready, 1)
            nc.scalar.activation(sin[:, :, :], sin[:, :, :], ACT.Sin)
            nc.scalar.activation(cos[:, :, :], cos[:, :, :], ACT.Sin).then_inc(trig, 1)

            def out(t):
                span = slice(t * P, (t + 1) * P)
                for n, (dst, width) in enumerate((
                        (k.qT[:, 0:4, span], 4), (k.qT[:, 4:8, span], 4), (None, 4), (k.kidxT[:, span], 1))):
                    act.wait_ge(tr_done, 4 * t + n + 1)
                    src = tp[n][:, 0:width * P]
                    if n == 2:
                        r = src.rearrange("p (a q) -> p a q", q=P)
                        nc.scalar.copy(k.kT[:, :, span], r[:, 0:2, :])
                        last = nc.scalar.copy(k.qidxT[:, :, span], r[:, 2:4, :])
                    elif n == 3:
                        last = nc.scalar.copy(dst, src)
                    else:
                        last = nc.scalar.copy(dst, src.rearrange("p (a q) -> p a q", q=P))
                    last.then_inc(tr_out, 1)

            act.wait_ge(low, KC)
            for t in range(TT):
                if t >= 2:
                    act.wait_ge(tr_done, 4 * (t - 1))
                for n, (a, b) in enumerate(spans):
                    act.wait_ge(mm_done, 4 * t + n + 1)
                    if n == 2:
                        nc.scalar.activation(raw[:, t % 2, a:a + 256], mm[n][:, 0:256], ACT.Copy,
                                             scale=1.0 / W_UP).then_inc(raw_done, 1)
                        nc.scalar.activation(k.v_tok[:, t, :], mm[n][:, 256:512], ACT.Copy,
                                             scale=1.0 / W_UP).then_inc(raw_done, 1)
                    else:
                        nc.scalar.activation(raw[:, t % 2, a:b], mm[n][:, 0:b - a], ACT.Copy,
                                             scale=1.0 / W_UP).then_inc(raw_done, 1)
                act.wait_ge(var, t + 1)
                nc.scalar.activation(ss[:, t % 2], ss[:, t % 2], ACT.Sqrt).then_inc(std, 1)
                if t:
                    out(t - 1)
            out(TT - 1)

        @block.gpsimd
        def _(pool):
            pool.wait_ge(small_in, 96)
            for t in range(TT):
                qk = raw[:, t % 2, 0:QK_HEADS * HD]
                pool.wait_ge(raw_done, 5 * t + 3)
                if t:
                    pool.wait_ge(var, t)
                nc.gpsimd.tensor_tensor(sq[:, :], qk, qk, ALU.mult).then_inc(sq_done, 1)
                pool.wait_ge(scaled, t + 1)
                heads = qk.rearrange("p (h d) -> p h d", d=HD)
                for n, (a, b) in enumerate(((0, HEADS), (HEADS, QK_HEADS))):
                    nc.gpsimd.tensor_tensor(heads[:, a:b, :], heads[:, a:b, :],
                                            gq[:, n, :].unsqueeze(1).to_broadcast([P, b - a, HD]), ALU.mult) \
                        .then_inc(gained, 1)

        @block.vector
        def _(dve):
            step = chain(dve, dve_step)
            v = nc.vector
            for c in range(KC):
                dve.wait_ge(high, c + 1)
                low_part(nc, w_q[:, 1, c, :], raw[:, c % 2, 0:S], w_q[:, 0, c, :])
                low_part(nc, w_rest[:, 1, c, 0:rest], raw[:, c % 2, S:TOKEN_COLS],
                         w_rest[:, 0, c, 0:rest]).then_inc(low, 1)
            dve.wait_ge(small_in, 96)
            step(v.tensor_copy(pos[:, :], pos_i[:, :]))
            step(v.tensor_tensor(ang[:, :, :], pos[:, :].unsqueeze(2).to_broadcast([P, TT, nf]),
                                 freq[:, :].unsqueeze(1).to_broadcast([P, TT, nf]), ALU.mult))
            step(v.tensor_scalar(turns[:, :, :], ang[:, :, :], float(1 / (2 * np.pi)), None, ALU.mult))
            step(v.tensor_scalar(turns[:, :, :], turns[:, :, :], 12582912.0, None, ALU.add))
            step(v.tensor_scalar(turns[:, :, :], turns[:, :, :], -12582912.0, None, ALU.add))
            c1 = 6.28125
            c2 = float(np.float32(np.round((2 * np.pi - c1) * 2 ** 21) / 2 ** 21))
            for part in (c1, c2, 2 * np.pi - c1 - c2):
                step(v.scalar_tensor_tensor(ang[:, :, :].rearrange("p t f -> p (t f)"),
                                            in0=turns[:, :, :].rearrange("p t f -> p (t f)"), scalar=float(-part),
                                            in1=ang[:, :, :].rearrange("p t f -> p (t f)"),
                                            op0=ALU.mult, op1=ALU.add))
            step(v.tensor_scalar(sin[:, :, :], ang[:, :, :], 3.1415925, -3.1415925, ALU.min, ALU.max))
            step(v.scalar_tensor_tensor(cos[:, :, :].rearrange("p t f -> p (t f)"),
                                        in0=sin[:, :, :].rearrange("p t f -> p (t f)"), scalar=-1.0,
                                        in1=sin[:, :, :].rearrange("p t f -> p (t f)"), op0=ALU.mult, op1=ALU.max))
            v.tensor_scalar(cos[:, :, :], cos[:, :, :], -1.0, float(np.pi / 2), ALU.mult, ALU.add).then_inc(ang_ready, 1)
            dve.wait_ge(trig, 1)

            def rope(x, heads, half, at, t):
                cs = cos[:, t, at:at + half].unsqueeze(1).to_broadcast([P, heads, half])
                sn = sin[:, t, at:at + half].unsqueeze(1).to_broadcast([P, heads, half])
                x1, x2 = x[:, :, 0:half], x[:, :, half:2 * half]
                a, b, c, d = (r[:, 0:heads, 0:half] for r in (ra, rb, rc, rd))
                v.tensor_tensor(a, x1, cs, ALU.mult)
                v.tensor_tensor(b, x2, sn, ALU.mult)
                v.tensor_tensor(c, x2, cs, ALU.mult)
                step(v.tensor_tensor(d, x1, sn, ALU.mult))
                v.tensor_tensor(x1, a, b, ALU.subtract)
                step(v.tensor_tensor(x2, c, d, ALU.add))

            for t in range(TT):
                s = t % 2
                r = raw[:, s, :]
                heads = r[:, 0:QK_HEADS * HD].rearrange("p (h d) -> p h d", d=HD)
                qi = r[:, 1536:1792].rearrange("p (h d) -> p h d", d=IDX_DIM)
                ki = r[:, 1792:1856]
                dve.wait_ge(raw_done, 5 * t + 5)
                step(v.tensor_scalar(k.widx[:, t, :], r[:, 1856:1860], float(IDX_HEADS ** -0.5 * IDX_DIM ** -0.5),
                                     None, ALU.mult))
                v.tensor_copy(k.dt_raw[:, t, :], r[:, 1860:1892])
                step(v.tensor_reduce(mu[:, s:s + 1], ki, AX.X, ALU.add))
                step(v.tensor_scalar(mu[:, s:s + 1], mu[:, s:s + 1], -1.0 / IDX_DIM, None, ALU.mult))
                step(v.tensor_scalar(kc_[:, s], ki, mu[:, s:s + 1], None, ALU.add))
                step(v.tensor_tensor(ksq[:, :], kc_[:, s], kc_[:, s], ALU.mult))
                step(v.tensor_reduce(ss[:, s, 10:11], ksq[:, :], AX.X, ALU.add))
                step(v.tensor_scalar(ss[:, s, 10:11], ss[:, s, 10:11], 1.0 / IDX_DIM, EPS, ALU.mult, ALU.add))
                dve.wait_ge(sq_done, t + 1)
                step(v.tensor_reduce(ss[:, s, 0:10], sq[:, :].rearrange("p (h d) -> p h d", d=HD), AX.X, ALU.add))
                v.tensor_scalar(ss[:, s, 0:10], ss[:, s, 0:10], 1.0 / HD, EPS, ALU.mult, ALU.add).then_inc(var, 1)
                dve.wait_ge(std, t + 1)
                step(v.reciprocal(ss[:, s], ss[:, s]))
                v.tensor_tensor(heads, heads, ss[:, s, 0:10].unsqueeze(2).to_broadcast([P, QK_HEADS, HD]),
                                ALU.mult).then_inc(scaled, 1)
                step(v.scalar_tensor_tensor(kc_[:, s], in0=kc_[:, s], scalar=ss[:, s, 10:11], in1=lnr[:, 0, :],
                                            op0=ALU.mult, op1=ALU.mult))
                step(v.tensor_tensor(kc_[:, s], kc_[:, s], lnr[:, 1, :], ALU.add))
                rope(kc_[:, s].unsqueeze(1), 1, ROPE_I, ROPE_A, t)
                rope(qi, IDX_HEADS, ROPE_I, ROPE_A, t)
                if t >= 2:
                    dve.wait_ge(tr_done, 4 * (t - 1))
                step(v.tensor_copy(kd[:, s], kc_[:, s].unsqueeze(1).to_broadcast([P, 2, IDX_DIM])))
                dve.wait_ge(gained, 2 * t + 2)
                rope(heads, QK_HEADS, ROPE_A, 0, t)
                dve.sem_inc(ready, 1)


def causal(b):
    n = (b + 1) * P
    return n, b * (b + 1) // 2 * P


def select_stage(k):
    nc, ins = k.nc, k.ins
    first = TOPK // P
    with ExitStack() as ctx:
        sb = lambda n, s, d=F32: k.sb(f"s_{n}", s, d, ctx=ctx)
        w, scaled = sb("w", [P, 2, KC, P]), k.sem("s_scaled")
        ws = sb("ws", [P, 2, 2, KC, P], F16)
        high, low = k.sem("s_high"), k.sem("s_low")
        blocks = list(range(first, TT))
        work_at = [sum(P * (b + 1) for b in blocks[:i]) for i in range(len(blocks) + 1)]
        rl, work, sig = sb("rl", [P, 2, S]), sb("work", [P, work_at[-1]]), sb("sig", [P, 2, S])
        mask, ties, rank = sb("mask", [P, 4, S], BF16), sb("ties", [P, S]), sb("rank", [P, S])
        found, cand, kept = (sb(n, [P, len(blocks)], I32) for n in ("found", "cand", "kept"))
        count, room = sb("count", [P, len(blocks)]), sb("room", [P, len(blocks)])
        future = sb("future", [P, P])
        sc_ps = [k.ps(f"s_sc{i}", [P, S], ctx=ctx) for i in range(2)]
        pj_ps = [k.ps(f"s_pj{i}", [P, S], ctx=ctx) for i in range(2)]
        w_in = [k.sem(f"s_w_in{i}") for i in range(2)]
        pj_done, pj_out, sc_done, relu, used, scored, counted, fut, dve_step = (k.sem(f"s_{n}") for n in (
            "pj_done", "pj_out", "sc_done", "relu", "used", "scored", "counted", "fut", "dve_step"))
        n_jobs = 2 * KC + EARLY_GATES
        stored, relu_sb = [k.sem(f"s_stored{n}") for n in range(2)], k.sem("s_relu_sb")
        groups = [range(0, 2), range(2, 6)]
        share = [range(i, i + 1) for i in range(len(blocks) - 1)] + [range(len(blocks) - 1, n_jobs)]
        block = ctx.enter_context(nc.Block())

        @block.sync
        def _(sp):
            for j in range(n_jobs):
                if j >= 2:
                    sp.wait_ge(low, j - 1)
                sp.dma_start(w[:, j % 2], ins["w_gates"][j]).then_inc(w_in[j % 2], 16)
                if j >= KC + 2:
                    sp.wait_ge(pj_out, j - 1)
                    sp.dma_start(k.gates_dram[j - KC - 2], sig[:, j % 2]).then_inc(stored[j % 2], 16)
            for j in range(n_jobs, n_jobs + 2):
                sp.wait_ge(pj_out, j - 1)
                sp.dma_start(k.gates_dram[j - KC - 2], sig[:, j % 2]).then_inc(stored[j % 2], 16)
            for n in range(2):
                sp.wait_ge(stored[n], 16 * (n_jobs - KC) // 2)

        @block.tensor
        def _(pe):
            for i, b in enumerate(blocks):
                n, _ = causal(b)
                for h in range(IDX_HEADS):
                    m = i * IDX_HEADS + h
                    if m >= 2:
                        pe.wait_ge(relu, m - 1)
                    rows = slice(IDX_DIM * (h % 2), IDX_DIM * (h % 2 + 1))
                    for a in range(0, n, HALF):
                        e = min(n, a + HALF)
                        last = nc.tensor.matmul(sc_ps[m % 2][:, a:e], lhsT=k.qidxT[rows, h // 2, b * P:(b + 1) * P],
                                                rhs=k.kidxT[rows, a:e], start=True, stop=True)
                    last.then_inc(sc_done, 1)
                for j in share[i]:
                    pe.wait_ge(high, j + 1)
                    pe.wait_ge(low, j + 1)
                    if j >= 2:
                        pe.wait_ge(pj_out, j - 1)
                    for a in range(0, S, HALF):
                        for c in range(KC):
                            last = product(nc, pj_ps[j % 2][:, a:a + HALF], part(ws, j % 2, c),
                                           part(k.hT, c, slice(a, a + HALF)), c == 0, c == KC - 1)
                    last.then_inc(pj_done, 1)

        @block.scalar
        def _(act):
            def split(j):
                act.wait_ge(w_in[j % 2], 16 * (j // 2 + 1))
                high_part(nc, w[:, j % 2], w[:, j % 2]).then_inc(scaled, 1)
                if j >= 2:
                    act.wait_ge(pj_done, j - 1)
                act.wait_ge(scaled, j + 1)
                nc.scalar.copy(ws[:, 0, j % 2], w[:, j % 2]).then_inc(high, 1)

            split(0)
            for i, b in enumerate(blocks):
                n, _ = causal(b)
                for h in range(IDX_HEADS):
                    m = i * IDX_HEADS + h
                    act.wait_ge(sc_done, m + 1)
                    if m >= 2 and (m - 2) % IDX_HEADS:
                        act.wait_ge(used, m - 2 - (m - 2) // IDX_HEADS)
                    nc.scalar.activation(rl[:, m % 2, 0:n], sc_ps[m % 2][:, 0:n], ACT.Relu).then_inc(relu, 1)
                    act.wait_ge(relu, m + 1)
                    dst = work[:, work_at[i]:work_at[i + 1]] if h == 0 else rl[:, m % 2, 0:n]
                    nc.scalar.activation(dst, rl[:, m % 2, 0:n], ACT.Copy,
                                         scale=k.widx[:, b, h:h + 1]).then_inc(relu_sb, 1)
                for j in share[i]:
                    if j + 1 < n_jobs:
                        split(j + 1)
                    act.wait_ge(pj_done, j + 1)
                    if j >= KC + 2:
                        act.wait_ge(stored[j % 2], 16 * ((j - KC) // 2))
                    dst, func = (k.z_att[:, j, :], ACT.Silu) if j < KC else (sig[:, j % 2], ACT.Sigmoid)
                    nc.scalar.activation(dst, pj_ps[j % 2][:, :], func, scale=1.0 / W_UP).then_inc(pj_out, 1)

        @block.gpsimd
        def _(pool):
            nc.gpsimd.tensor_scalar(future[:, :], k.const("before"), -BIG, None, ALU.mult).then_inc(fut, 1)
            pool.wait_ge(fut, 1)

            def split(j):
                pool.wait_ge(high, j + 1)
                nc.gpsimd.tensor_tensor(ws[:, 1, j % 2], w[:, j % 2], ws[:, 0, j % 2], ALU.subtract) \
                    .then_inc(low, 1)

            split(0)
            for i, b in enumerate(blocks):
                n, _ = causal(b)
                wk = work[:, work_at[i]:work_at[i + 1]]
                for h in range(1, IDX_HEADS):
                    m = i * IDX_HEADS + h
                    pool.wait_ge(relu_sb, m + 1)
                    nc.gpsimd.tensor_tensor(wk, wk, rl[:, m % 2, 0:n], ALU.add).then_inc(used, 1)
                    pool.wait_ge(used, m - i)
                nc.gpsimd.tensor_tensor(wk[:, b * P:n], wk[:, b * P:n], future[:, :], ALU.add).then_inc(scored, 1)
                for j in share[i]:
                    if j + 1 < n_jobs:
                        split(j + 1)

        @block.vector
        def _(dve):
            step = chain(dve, dve_step)
            v = nc.vector
            dve.wait_ge(fut, 1)
            for b in range(first):
                n, at = causal(b)
                if b:
                    v.memset(k.bias[:, at:at + b * P], 0.0)
                v.tensor_copy(k.bias[:, at + b * P:at + n], future[:, :])
            scores = lambda i: work[:, work_at[i]:work_at[i + 1]]

            def counts(group, threshold, op):
                for i in group:
                    v.tensor_scalar(mask[:, i % 4, 0:P * (blocks[i] + 1)], scores(i), threshold(i), 0.0, op, ALU.add,
                                    accum_out=count[:, i:i + 1]).then_inc(counted, 1)
                    done[0] += 1
                dve.wait_ge(counted, done[0])

            done = [0]
            for group in groups:
                span = slice(group[0], group[-1] + 1)
                f, c, kp, cnt = found[:, span], cand[:, span], kept[:, span], count[:, span]
                dve.wait_ge(scored, group[-1] + 1)
                counts(group, lambda i: 0.0, ALU.is_ge)
                step(v.tensor_scalar(f, cnt, TOPK - 0.5, -1.0, ALU.is_lt, ALU.mult))
                step(v.tensor_scalar(c, f, 1 << 30, None, ALU.bitwise_xor))
                for bit in range(30, -1, -1):
                    counts(group, lambda i: cand[:, i:i + 1].bitcast(F32), ALU.is_ge)
                    step(v.tensor_scalar(kp, cnt, TOPK - 0.5, float(1 << bit), ALU.is_ge, ALU.mult))
                    if bit:
                        v.scalar_tensor_tensor(c, in0=kp, scalar=1 << (bit - 1), in1=f, op0=ALU.bitwise_xor,
                                               op1=ALU.bitwise_xor)
                    step(v.tensor_tensor(f, f, kp, ALU.bitwise_xor))
                least = lambda i: found[:, i:i + 1].bitcast(F32)
                counts(group, least, ALU.is_gt)
                step(v.tensor_scalar(room[:, span], cnt, -1.0, float(TOPK), ALU.mult, ALU.add))
                for i in group:
                    n, at = causal(blocks[i])
                    e, r = ties[:, 0:n], rank[:, 0:n]
                    step(v.tensor_scalar(e, scores(i), least(i), None, ALU.is_equal))
                    step(v.tensor_tensor_scan(r, e, e, 0.0, ALU.add, ALU.max))
                    step(v.scalar_tensor_tensor(e, in0=r, scalar=room[:, i:i + 1], in1=e, op0=ALU.is_le, op1=ALU.mult))
                    step(v.scalar_tensor_tensor(e, in0=scores(i), scalar=least(i), in1=e, op0=ALU.is_gt, op1=ALU.add))
                    step(v.tensor_scalar(k.bias[:, at:at + n], e, -1.0, BIG, ALU.add, ALU.mult))


def attention_stage(k):
    nc = k.nc
    scale = float(HD ** -0.5)
    with ExitStack() as ctx:
        sb = lambda n, s, d=F32: k.sb(f"a_{n}", s, d, ctx=ctx)
        sm, pT = sb("sm", [P, 4, S]), sb("pT", [P, 2, S])
        mx, nb, rs = sb("mx", [P, 4]), sb("nb", [P, 4]), sb("rs", [P, 4])
        s_ps = [k.ps(f"a_s{i}", [P, S], ctx=ctx) for i in range(2)]
        t_ps = k.ps("a_t", [P, S], ctx=ctx)
        o_ps = [k.ps(f"a_o{i}", [P, P], ctx=ctx) for i in range(2)]
        s_done, masked, neg, exped, scaled, t_done, t_out, o_done, o_out, dve_step = (k.sem(f"a_{n}") for n in (
            "s_done", "masked", "neg", "exped", "scaled", "t_done", "t_out", "o_done", "o_out", "dve_step"))
        jobs = [(b, h) for b in range(TT) for h in range(HEADS)]
        block = ctx.enter_context(nc.Block())

        @block.tensor
        def _(pe):
            def scores(m):
                b, h = jobs[m]
                n, _ = causal(b)
                if m >= 2:
                    pe.wait_ge(masked, m - 1)
                for a in range(0, n, HALF):
                    e = min(n, a + HALF)
                    last = nc.tensor.matmul(s_ps[m % 2][:, a:e], lhsT=k.qT[:, h, b * P:(b + 1) * P],
                                            rhs=k.kT[:, h // (HEADS // KV_HEADS), a:e], start=True, stop=True)
                last.then_inc(s_done, 1)

            def transposes(m):
                b, h = jobs[m]
                pe.wait_ge(scaled, m + 1)
                if m:
                    pe.wait_ge(t_out, m)
                for j in range(b + 1):
                    last = nc.tensor.transpose(t_ps[:, j * P:(j + 1) * P], sm[:, m % 4, j * P:(j + 1) * P],
                                               k.const("ident"))
                last.then_inc(t_done, 1)

            def values(m):
                b, h = jobs[m]
                pe.wait_ge(t_out, m + 1)
                if m >= 2:
                    pe.wait_ge(o_out, m - 1)
                kv = h // (HEADS // KV_HEADS)
                for j in range(b + 1):
                    last = nc.tensor.matmul(o_ps[m % 2][:, :], lhsT=k.v_tok[:, j, kv * HD:(kv + 1) * HD],
                                            rhs=pT[:, m % 2, j * P:(j + 1) * P], start=j == 0, stop=j == b)
                last.then_inc(o_done, 1)

            for m in range(-3, len(jobs)):
                if m + 3 < len(jobs):
                    scores(m + 3)
                if 0 <= m + 1 < len(jobs):
                    transposes(m + 1)
                if m >= 0:
                    values(m)

        @block.scalar
        def _(act):
            def exps(m):
                n, _ = causal(jobs[m][0])
                act.wait_ge(neg, m + 1)
                nc.scalar.activation(sm[:, m % 4, 0:n], sm[:, m % 4, 0:n], ACT.Exp, bias=nb[:, m % 4:m % 4 + 1],
                                     scale=scale, accum_out=rs[:, m % 4:m % 4 + 1]).then_inc(exped, 1)

            for m in range(-3, len(jobs)):
                if 0 <= m + 1 < len(jobs):
                    n, _ = causal(jobs[m + 1][0])
                    act.wait_ge(t_done, m + 2)
                    if m + 1 >= 2:
                        act.wait_ge(o_done, m)
                    nc.scalar.copy(pT[:, (m + 1) % 2, 0:n], t_ps[:, 0:n]).then_inc(t_out, 1)
                if m + 3 < len(jobs):
                    exps(m + 3)

        @block.vector
        def _(dve):
            step = chain(dve, dve_step)
            v = nc.vector

            def out(m):
                b, h = jobs[m]
                dve.wait_ge(o_done, m + 1)
                z = k.z_att[:, h, b * P:(b + 1) * P]
                nc.vector.tensor_tensor(z, o_ps[m % 2][:, :], z, ALU.mult).then_inc(o_out, 1)

            def mask(m):
                n, at = causal(jobs[m][0])
                s = m % 4
                dve.wait_ge(s_done, m + 1)
                if m >= 4:
                    dve.wait_ge(t_done, m - 3)
                v.tensor_tensor_reduce(out=sm[:, s, 0:n], in0=s_ps[m % 2][:, 0:n], in1=k.bias[:, at:at + n], scale=1.0,
                                       scalar=-3.0e38, op0=ALU.add, op1=ALU.max,
                                       accum_out=mx[:, s:s + 1]).then_inc(masked, 1)
                dve.wait_ge(masked, m + 1)
                v.tensor_scalar(nb[:, s:s + 1], mx[:, s:s + 1], -scale, None, ALU.mult).then_inc(neg, 1)

            def normalise(m):
                n, _ = causal(jobs[m][0])
                s = m % 4
                dve.wait_ge(exped, m + 1)
                step(v.reciprocal(rs[:, s:s + 1], rs[:, s:s + 1]))
                v.tensor_scalar(sm[:, s, 0:n], sm[:, s, 0:n], rs[:, s:s + 1], None, ALU.mult).then_inc(scaled, 1)

            for m in range(-3, len(jobs)):
                if 0 <= m + 2 < len(jobs):
                    normalise(m + 2)
                if m + 3 < len(jobs):
                    mask(m + 3)
                if m >= 0:
                    out(m)


def branch_att_stage(k):
    nc, ins = k.nc, k.ins
    with ExitStack() as ctx:
        w = k.sb("ba_w", [P, 2, KC, P], ctx=ctx)
        ws = k.sb("ba_ws", [P, 2, 2, KC, P], F16, ctx=ctx)
        oT = k.sb("ba_o", [P, 2, KC, S], F16, ctx=ctx)
        gated, g_in = k.sb("ba_gated", [P, KC, S], ctx=ctx), k.sem("ba_g_in")
        acc = [k.ps(f"ba_ps{i}", [P, S], ctx=ctx) for i in range(2)]
        w_in = [k.sem(f"ba_w_in{i}") for i in range(2)]
        done, out, high, low, o_high, o_low = (k.sem(f"ba_{n}") for n in ("done", "out", "high", "low", "o_high", "o_low"))
        stored = k.sem("ba_stored")
        block = ctx.enter_context(nc.Block())

        @block.sync
        def _(sp):
            for j in range(KC):
                if j >= 2:
                    sp.wait_ge(high, j - 1)
                    sp.wait_ge(low, j - 1)
                sp.dma_start(w[:, j % 2], ins["w_branch_att"][j]).then_inc(w_in[j % 2], 16)
                if j == 1:
                    sp.dma_start(gated[:, :, :], k.gates_dram[0:KC].rearrange("c p s -> p c s")).then_inc(g_in, 16)
            for j in range(KC):
                sp.wait_ge(out, j + 1)
                sp.dma_start(k.gates_dram[j], gated[:, j, :]).then_inc(stored, 16)
            sp.wait_ge(stored, 16 * KC)

        @block.tensor
        def _(pe):
            for j in range(KC):
                pe.wait_ge(high, j + 1)
                pe.wait_ge(low, j + 1)
                if j >= 2:
                    pe.wait_ge(out, j - 1)
                for c in range(KC):
                    if j == 0:
                        pe.wait_ge(o_high, c + 1)
                        pe.wait_ge(o_low, c + 1)
                    for a in range(0, S, HALF):
                        last = product(nc, acc[j % 2][:, a:a + HALF], part(ws, j % 2, c),
                                       part(oT, c, slice(a, a + HALF)), c == 0, c == KC - 1)
                last.then_inc(done, 1)

        @block.scalar
        def _(act):
            def split(j):
                act.wait_ge(w_in[j % 2], 16 * (j // 2 + 1))
                if j >= 2:
                    act.wait_ge(done, j - 1)
                high_part(nc, ws[:, 0, j % 2], w[:, j % 2]).then_inc(high, 1)

            nc.scalar.copy(oT[:, 0, 0, :], k.z_att[:, 0, :]).then_inc(o_high, 1)
            split(0)
            for c in range(1, KC):
                nc.scalar.copy(oT[:, 0, c, :], k.z_att[:, c, :]).then_inc(o_high, 1)
            for j in range(1, KC):
                split(j)

        @block.vector
        def _(dve):
            def split(j):
                dve.wait_ge(high, j + 1)
                low_part(nc, ws[:, 1, j % 2].rearrange("p c q -> p (c q)"), w[:, j % 2].rearrange("p c q -> p (c q)"),
                         ws[:, 0, j % 2].rearrange("p c q -> p (c q)")).then_inc(low, 1)

            for c in range(KC):
                dve.wait_ge(o_high, c + 1)
                nc.vector.tensor_tensor(oT[:, 1, c, :], k.z_att[:, c, :], oT[:, 0, c, :], ALU.subtract).then_inc(o_low, 1)
                if c == 0:
                    split(0)
            for j in range(KC):
                if j + 1 < KC:
                    split(j + 1)
                dve.wait_ge(done, j + 1)
                dve.wait_ge(g_in, 16)
                nc.vector.scalar_tensor_tensor(gated[:, j, :], in0=acc[j % 2][:, :], scalar=1.0 / W_UP,
                                               in1=gated[:, j, :], op0=ALU.mult, op1=ALU.mult).then_inc(out, 1)


def step_sizes_stage(k):
    nc, ins = k.nc, k.ins
    with ExitStack() as ctx:
        sb = lambda n, s=(P, TT, SSM_HEADS), d=F32: k.sb(f"d_{n}", list(s), d, ctx=ctx)
        rows = sb("rows", (P, 2, SSM_HEADS))
        x, u, w1, lnw, eq = sb("x"), sb("u"), sb("w1"), sb("lnw"), sb("eq")
        sums = [k.ps(f"d_ps{i}", [P, TT, SSM_HEADS], ctx=ctx) for i in range(3)]
        r_in, a_done, absx, exped, plus, logged, adt_ready, summed, expsum, dve_step = (k.sem(f"d_{n}") for n in (
            "r_in", "a_done", "absx", "exped", "plus", "logged", "adt_ready", "summed", "expsum", "dve_step"))
        block = ctx.enter_context(nc.Block())

        @block.sync
        def _(sp):
            sp.dma_start(rows[:, 0, :], ins["dt_bias"].partition_broadcast(P)).then_inc(r_in, 16)
            sp.dma_start(rows[:, 1, :], ins["a_log"].partition_broadcast(P)).then_inc(r_in, 16)
            sp.dma_start(k.d_skip[:, :], ins["d_skip"].partition_broadcast(P)).then_inc(r_in, 16)

        @block.scalar
        def _(act):
            act.wait_ge(r_in, 48)
            nc.scalar.activation(rows[:, 1, :], rows[:, 1, :], ACT.Exp).then_inc(a_done, 1)
            act.wait_ge(absx, 1)
            nc.scalar.activation(u[:, :, :], u[:, :, :], ACT.Exp).then_inc(exped, 1)
            act.wait_ge(plus, 1)
            nc.scalar.activation(lnw[:, :, :], w1[:, :, :], ACT.Ln).then_inc(logged, 1)
            act.wait_ge(summed, 1)
            for src, dst in zip(sums, (k.e_cum, k.e_after, k.e_all)):
                last = nc.scalar.activation(dst[:, :, :], src[:, :, :], ACT.Exp)
            last.then_inc(expsum, 1)

        @block.tensor
        def _(pe):
            pe.wait_ge(adt_ready, 1)
            for n, tri in enumerate(("upto", "after", "ones")):
                last = nc.tensor.matmul(sums[n][:, :, :].rearrange("p t h -> p (t h)"), lhsT=k.const(tri),
                                        rhs=k.adt[:, :, :].rearrange("p t h -> p (t h)"), start=True, stop=True)
            last.then_inc(summed, 1)

        @block.vector
        def _(dve):
            step = chain(dve, dve_step)
            v = nc.vector
            row = lambda n: rows[:, n, :].unsqueeze(1).to_broadcast([P, TT, SSM_HEADS])
            dve.wait_ge(r_in, 48)
            step(v.tensor_tensor(x[:, :, :], k.dt_raw[:, :, :], row(0), ALU.add))
            step(v.tensor_scalar(u[:, :, :], x[:, :, :], -1.0, None, ALU.mult))
            v.tensor_tensor(u[:, :, :], u[:, :, :], x[:, :, :], ALU.min).then_inc(absx, 1)
            dve.wait_ge(exped, 1)
            v.tensor_scalar(w1[:, :, :], u[:, :, :], 1.0, None, ALU.add).then_inc(plus, 1)
            dve.wait_ge(logged, 1)
            dve.wait_ge(plus, 1)
            step(v.tensor_scalar(w1[:, :, :], w1[:, :, :], -1.0, None, ALU.add))
            step(v.tensor_scalar(eq[:, :, :], w1[:, :, :], 0.0, None, ALU.is_equal))
            step(v.tensor_tensor(w1[:, :, :], w1[:, :, :], eq[:, :, :], ALU.add))
            step(v.tensor_tensor(lnw[:, :, :], lnw[:, :, :], eq[:, :, :], ALU.add))
            step(v.reciprocal(w1[:, :, :], w1[:, :, :]))
            step(v.tensor_tensor(lnw[:, :, :], lnw[:, :, :], w1[:, :, :], ALU.mult))
            step(v.tensor_tensor(lnw[:, :, :], lnw[:, :, :], u[:, :, :], ALU.mult))
            step(v.tensor_scalar(x[:, :, :], x[:, :, :], 0.0, None, ALU.max))
            step(v.tensor_tensor(k.dt[:, :, :], x[:, :, :], lnw[:, :, :], ALU.add))
            dve.wait_ge(a_done, 1)
            step(v.tensor_tensor(k.adt[:, :, :], k.dt[:, :, :], row(1), ALU.mult))
            step(v.tensor_scalar(k.adt[:, :, :], k.adt[:, :, :], -1.0, None, ALU.mult))
            dve.sem_inc(adt_ready, 1)
            dve.wait_ge(expsum, 1)
            step(v.tensor_tensor(k.e_after[:, :, :], k.e_after[:, :, :], k.dt[:, :, :], ALU.mult))


def xbc_tiles(g):
    return [4 * g + n for n in range(4)] + [16 + g, 20 + g]


def ssm_inputs_stage(k, g):
    nc, ins = k.nc, k.ins
    pad = SSM_CONV - 1
    tiles = xbc_tiles(g)
    with ExitStack() as ctx:
        sb = lambda n, s, d=F32: k.sb(f"i{g}_{n}", s, d, ctx=ctx)
        w = sb("w", [P, 2, KC, P])
        raw = lambda j: w[:, j % 2] if j else k.w_first[:, :, :]
        first_in = k.sem(f"i{g}_first_in")
        ws = sb("ws", [P, 2, 2, KC, P], F16)
        u, xf = sb("u", [P, 2, pad + S]), sb("xf", [P, 2, S])
        pj = [k.ps(f"i{g}_pj{i}", [P, S], ctx=ctx) for i in range(2)]
        tr = [k.ps(f"i{g}_tr{i}", [P, HALF], ctx=ctx) for i in range(2)]
        w_in = [k.sem(f"i{g}_w_in{i}") for i in range(2)]
        pads, pj_done, u_done, conv, act_done, tr_done, tr_out, dve_step, high, low = (
            k.sem(f"i{g}_{n}") for n in ("pads", "pj_done", "u_done", "conv", "act_done", "tr_done",
                                        "tr_out", "dve_step", "high", "low"))
        wz_in, z_high, z_low, z_done, z_out = (k.sem(f"i{g}_{n}") for n in ("wz_in", "z_high", "z_low", "z_done", "z_out"))
        z_ps = [k.ps(f"i{g}_z{i}", [P, GW], ctx=ctx) for i in range(2)]
        dsts = [xf[:, 0], xf[:, 1], xf[:, 0], xf[:, 1], k.BT[:, :], k.CT[:, :]]
        block = ctx.enter_context(nc.Block())

        @block.sync
        def _(sp):
            for j, tile in enumerate(tiles):
                if j >= 3:
                    sp.wait_ge(high, j - 1)
                    sp.wait_ge(low, j - 1)
                if j or g == 0:
                    sp.dma_start(raw(j), ins["w_xbc"][tile]).then_inc(w_in[j % 2] if j else first_in, 16)
                if j == 1:
                    sp.dma_start(k.w_group[:, :, :],
                                 ins["w_z"][:, g * GW:(g + 1) * GW].rearrange("(c p) n -> p c n", p=P)) \
                        .then_inc(wz_in, 16)
            sp.wait_ge(z_low, 1)
            sp.dma_start(k.w_group[:, :, :].rearrange("p (c a) n -> p c (a n)", c=4),
                         ins["w_branch_ssm"][g * GW:(g + 1) * GW, :].rearrange("(c p) n -> p c n", p=P)) \
                .then_inc(k.w_branch_in, 16)

        @block.tensor
        def _(pe):
            def transposes(j):
                pe.wait_ge(act_done, j + 1)
                for h in range(2):
                    if 2 * j + h >= 2:
                        pe.wait_ge(tr_out, 2 * j + h - 1)
                    for t in range(4):
                        last = nc.tensor.transpose(tr[h][:, t * P:(t + 1) * P],
                                                   dsts[j][:, (4 * h + t) * P:(4 * h + t + 1) * P], k.const("ident"))
                    last.then_inc(tr_done, 1)

            for j in range(6):
                pe.wait_ge(high, j + 1)
                pe.wait_ge(low, j + 1)
                if j >= 2:
                    pe.wait_ge(u_done, j - 1)
                for a in range(0, S, HALF):
                    for c in range(KC):
                        last = product(nc, pj[j % 2][:, a:a + HALF], part(ws, j % 2, c),
                                       part(k.hT, c, slice(a, a + HALF)), c == 0, c == KC - 1)
                last.then_inc(pj_done, 1)
                if j >= 2:
                    transposes(j - 2)
            for t in range(EARLY_Z):
                if t == 1:
                    transposes(4)
                if t == 0:
                    pe.wait_ge(z_low, 1)
                if t >= 2:
                    pe.wait_ge(z_out, t - 1)
                for c in range(KC):
                    last = product(nc, z_ps[t % 2][:, :], part(k.hT, c, slice(t * P, (t + 1) * P)),
                                   part(k.ws_group, c), c == 0, c == KC - 1)
                last.then_inc(z_done, 1)

        @block.vector
        def _(dve):
            step = chain(dve, dve_step)
            v = nc.vector
            for i in range(2):
                v.memset(u[:, i, 0:pad], 0.0).then_inc(pads, 1)
            dve.wait_ge(pads, 2)

            def split(j):
                dve.wait_ge(high, j + 1)
                low_part(nc, ws[:, 1, j % 2].rearrange("p c q -> p (c q)"), raw(j).rearrange("p c q -> p (c q)"),
                         ws[:, 0, j % 2].rearrange("p c q -> p (c q)")).then_inc(low, 1)

            split(0)
            for j, tile in enumerate(tiles):
                if j + 1 < len(tiles):
                    split(j + 1)
                if j == 4:
                    dve.wait_ge(z_high, 1)
                    low_part(nc, k.ws_group[:, 1], k.w_group[:, :, :], k.ws_group[:, 0]).then_inc(z_low, 1)
                dve.wait_ge(u_done, j + 1)
                if j >= 2 and j < 4:
                    dve.wait_ge(tr_done, 2 * (j - 1))
                tap = lambda i: k.pv("conv_w_2", tile * SSM_CONV + i)
                step(v.tensor_scalar(dsts[j], u[:, j % 2, 0:S], tap(0), None, ALU.mult))
                for i in range(1, SSM_CONV):
                    last = v.scalar_tensor_tensor(dsts[j], in0=u[:, j % 2, i:i + S], scalar=tap(i), in1=dsts[j],
                                                  op0=ALU.mult, op1=ALU.add)
                    if i < SSM_CONV - 1:
                        step(last)
                last.then_inc(conv, 1)

        @block.scalar
        def _(act):
            def split(j):
                if j:
                    act.wait_ge(w_in[j % 2], 16 * ((j + 1) // 2))
                elif g == 0:
                    act.wait_ge(first_in, 16)
                if j >= 2:
                    act.wait_ge(pj_done, j - 1)
                high_part(nc, ws[:, 0, j % 2], raw(j)).then_inc(high, 1)

            def activate(j):
                act.wait_ge(conv, j + 1)
                nc.scalar.activation(dsts[j], dsts[j], ACT.Silu, bias=k.pv("conv_b_2", tiles[j])).then_inc(act_done, 1)

            def out(j):
                for h in range(2):
                    act.wait_ge(tr_done, 2 * j + h + 1)
                    dst = k.x_ssm[:, 4 * h:4 * h + 4, j * P:(j + 1) * P] if j < 4 else k.B_tok[:, 4 * h:4 * h + 4, :]
                    nc.scalar.copy(dst, tr[h][:, :].rearrange("p (t q) -> p t q", q=P)).then_inc(tr_out, 1)

            split(0)
            for j in range(6):
                if j + 1 < 6:
                    split(j + 1)
                if j == 3:
                    act.wait_ge(wz_in, 16)
                    high_part(nc, k.ws_group[:, 0], k.w_group[:, :, :]).then_inc(z_high, 1)
                act.wait_ge(pj_done, j + 1)
                if j >= 2:
                    act.wait_ge(conv, j - 1)
                nc.scalar.activation(u[:, j % 2, pad:pad + S], pj[j % 2][:, :], ACT.Copy,
                                     scale=1.0 / W_UP).then_inc(u_done, 1)
                if j:
                    activate(j - 1)
                if j >= 2:
                    out(j - 2)
            activate(5)
            out(4)
            for t in range(EARLY_Z):
                act.wait_ge(z_done, t + 1)
                nc.scalar.activation(k.z_ssm[:, t, :], z_ps[t % 2][:, :], ACT.Silu, scale=1.0 / W_UP).then_inc(z_out, 1)


def ssm_scan_stage(k, g):
    nc, ins = k.nc, k.ins
    heads = slice(g * HPG, (g + 1) * HPG)
    with ExitStack() as ctx:
        sb = lambda n, s, d=F32: k.sb(f"y{g}_{n}", s, d, ctx=ctx)
        xdt, xds = sb("xdt", [P, 2, HPG, SSM_HD]), sb("xds", [P, 2, HPG, SSM_HD])
        A, E = sb("A", [P, 2, HPG, P]), sb("E", [P, 2, HPG * P])
        M = E[:, :, :].rearrange("p s (h l) -> p s h l", l=P)
        cbm, state, xd = sb("cbm", [P, 2, P]), sb("state", [P, GW]), sb("xd", [P, 2, HPG, SSM_HD])
        y, sq = sb("y", [P, GW]), sb("sq", [P, GW])
        ss, eps, gain = sb("ss", [P, TT]), sb("eps", [P, 1]), sb("gain", [P, 4])
        w = k.w_group[:, :, :].rearrange("p (c a) n -> p c (a n)", c=4)
        ws = k.ws_group[:, :, :, :].rearrange("p s (c a) n -> p s c (a n)", c=4)
        yT = k.yT
        cb = k.ps(f"y{g}_cb", [P, P], ctx=ctx)
        seg = k.ps(f"y{g}_seg", [P, HPG * P], ctx=ctx)
        yd_ps, yo_ps, st_ps = (k.ps(f"y{g}_{n}", [P, GW], ctx=ctx) for n in ("yd_ps", "yo_ps", "st_ps"))
        tr, br = k.ps(f"y{g}_tr", [P, HALF], ctx=ctx), k.ps(f"y{g}_br", [P, HALF], ctx=ctx)
        names = ("pool_in", "A_done", "seg_done", "cb_done", "E_done", "cbm_done", "M_done", "yd_done",
                 "yo_done", "st_done", "state_done", "yo_read", "y_done", "gated", "squared", "std", "normed",
                 "tr_done", "tr_high", "tr_low", "br_done", "br_out", "dve_step", "xd_done", "w_high", "w_low",
                 "small", "z_done", "z_out")
        q = {n: k.sem(f"y{g}_{n}") for n in names}
        jobs = [(m, a) for a in (0, HALF) for m in range(KC)]
        middle, end = {6: 0, 7: 2, 8: 4, 9: 6}, {6: 1, 7: 3, 8: 5, 9: 7}
        ring = [br[:, :], seg[:, 0:HALF], seg[:, HALF:S], yd_ps[:, :]]
        bank = lambda j: ring[0] if j < KC else ring[(j - KC) % 4]
        block = ctx.enter_context(nc.Block())

        if g + 1 < SSM_GROUPS:
            next_in = k.sem(f"y{g}_next_in")

            @block.sync
            def _(sp):
                sp.dma_start(k.w_first[:, :, :], ins["w_xbc"][xbc_tiles(g + 1)[0]]).then_inc(next_in, 16)
                sp.wait_ge(next_in, 16)

        def per_head(x, t, n=SSM_HD):
            return x[:, t, heads].unsqueeze(2).to_broadcast([P, HPG, n])

        def accumulate(dve, j):
            m, a = jobs[j]
            dst = k.y_ssm[:, m, a:a + HALF]
            dve.wait_ge(q["br_done"], j + 1)
            if g == 0:
                nc.vector.tensor_scalar(dst, bank(j), 1.0 / W_UP, None, ALU.mult).then_inc(q["br_out"], 1)
            else:
                nc.vector.scalar_tensor_tensor(dst, in0=bank(j), scalar=1.0 / W_UP, in1=dst,
                                               op0=ALU.mult, op1=ALU.add).then_inc(q["br_out"], 1)

        @block.gpsimd
        def _(pool):
            for t in range(TT):
                s = t % 2
                xs = k.x_ssm[:, t, :].rearrange("p (h d) -> p h d", d=SSM_HD)
                if t >= 2:
                    pool.wait_ge(q["seg_done"], t - 1)
                nc.gpsimd.tensor_tensor(A[:, s], per_head(k.adt, t, P),
                                        k.const("after").unsqueeze(1).to_broadcast([P, HPG, P]), ALU.mult) \
                    .then_inc(q["A_done"], 1)
                if t >= 2:
                    pool.wait_ge(q["yd_done"], t - 1)
                    pool.wait_ge(q["st_done"], t - 1)
                    pool.wait_ge(q["y_done"], t - 1)
                nc.gpsimd.tensor_tensor(xdt[:, s], xs, per_head(k.dt, t), ALU.mult)
                nc.gpsimd.tensor_tensor(xds[:, s], xs, per_head(k.e_after, t), ALU.mult).then_inc(q["pool_in"], 1)
                nc.gpsimd.tensor_tensor(xd[:, s], xs,
                                        k.d_skip[:, heads].unsqueeze(2).to_broadcast([P, HPG, SSM_HD]),
                                        ALU.mult).then_inc(q["xd_done"], 1)

        @block.tensor
        def _(pe):
            def segments(t):
                span = slice(t * P, (t + 1) * P)
                pe.wait_ge(q["A_done"], t + 1)
                if t:
                    pe.wait_ge(q["E_done"], t)
                for h in range(HPG):
                    last = nc.tensor.matmul(seg[:, h * P:(h + 1) * P], lhsT=A[:, t % 2, h, :], rhs=k.const("upto"),
                                            start=True, stop=True)
                last.then_inc(q["seg_done"], 1)
                if t:
                    pe.wait_ge(q["cbm_done"], t)
                nc.tensor.matmul(cb[:, :], lhsT=k.BT[:, span], rhs=k.CT[:, span], start=True, stop=True) \
                    .then_inc(q["cb_done"], 1)

            def z(t):
                if t > EARLY_Z:
                    pe.wait_ge(q["z_out"], t - EARLY_Z)
                for c in range(KC):
                    last = product(nc, br[:, :], part(k.hT, c, slice(t * P, (t + 1) * P)),
                                   part(k.ws_group, c), c == 0, c == KC - 1)
                last.then_inc(q["z_done"], 1)

            def transposes(t):
                pe.wait_ge(q["normed"], t + 1)
                if t:
                    pe.wait_ge(q["tr_low"], t)
                for c in range(4):
                    last = nc.tensor.transpose(tr[:, c * P:(c + 1) * P], k.z_ssm[:, t, c * P:(c + 1) * P],
                                               k.const("ident"))
                last.then_inc(q["tr_done"], 1)

            def branch(j):
                m, a = jobs[j]
                if j == 0:
                    pe.wait_ge(q["z_out"], TT - EARLY_Z)
                    pe.wait_ge(q["w_high"], 4)
                    pe.wait_ge(q["w_low"], 4)
                if j == 0 or j == KC:
                    pe.wait_ge(q["tr_high"], 4 + a // P)
                    pe.wait_ge(q["tr_low"], 4 + a // P)
                if 1 <= j <= KC:
                    pe.wait_ge(q["br_out"], j)
                elif j >= KC + 4:
                    pe.wait_ge(q["br_out"], j - 3)
                for c in range(4):
                    last = product(nc, bank(j), part(ws, c, slice(m * P, (m + 1) * P)),
                                   part(yT, c, slice(a, a + HALF)), c == 0, c == 3)
                last.then_inc(q["br_done"], 1)

            segments(0)
            for t in range(TT + 2):
                s = t % 2
                span = slice(t * P, (t + 1) * P)
                if t + 1 < TT:
                    segments(t + 1)
                if t < TT:
                    pe.wait_ge(q["pool_in"], t + 1)
                    if t:
                        pe.wait_ge(q["state_done"], t)
                        pe.wait_ge(q["yo_read"], t)
                        nc.tensor.matmul(yo_ps[:, :], lhsT=k.CT[:, span], rhs=state[:, :], start=True, stop=True) \
                            .then_inc(q["yo_done"], 1)
                    nc.tensor.matmul(st_ps[:, :], lhsT=k.B_tok[:, t, :], rhs=xds[:, s].rearrange("p h d -> p (h d)"),
                                     start=True, stop=True).then_inc(q["st_done"], 1)
                    if t + EARLY_Z < TT:
                        z(t + EARLY_Z)
                    if t in middle:
                        branch(middle[t])
                    pe.wait_ge(q["M_done"], t + 1)
                    if t:
                        pe.wait_ge(q["y_done"], t)
                    for h in range(HPG):
                        last = nc.tensor.matmul(yd_ps[:, h * SSM_HD:(h + 1) * SSM_HD], lhsT=M[:, s, h, :],
                                                rhs=xdt[:, s, h, :], start=True, stop=True)
                    last.then_inc(q["yd_done"], 1)
                elif t in middle:
                    branch(middle[t])
                if t >= 2:
                    transposes(t - 2)
                if t in end:
                    branch(end[t])
            pe.wait_ge(q["y_done"], TT)
            for j in range(KC, 2 * KC):
                branch(j)

        @block.scalar
        def _(act):
            def decay(t):
                act.wait_ge(q["seg_done"], t + 1)
                if t >= 2:
                    act.wait_ge(q["yd_done"], t - 1)
                nc.scalar.activation(E[:, t % 2], seg[:, :], ACT.Exp).then_inc(q["E_done"], 1)

            def silu_z(t):
                act.wait_ge(q["z_done"], t - EARLY_Z + 1)
                nc.scalar.activation(k.z_ssm[:, t, :], br[:, :], ACT.Silu, scale=1.0 / W_UP).then_inc(q["z_out"], 1)

            decay(0)
            act.wait_ge(q["small"], 2)
            for t in range(TT + 2):
                if t + 1 < TT:
                    decay(t + 1)
                if t + EARLY_Z < TT:
                    silu_z(t + EARLY_Z)
                if 1 <= t <= TT:
                    act.wait_ge(q["gated"], t)
                    nc.scalar.activation(sq[:, :], k.z_ssm[:, t - 1, :], ACT.Square,
                                         accum_out=ss[:, t - 1:t]).then_inc(q["squared"], 1)
                    act.wait_ge(q["squared"], t)
                    nc.scalar.activation(ss[:, t - 1:t], ss[:, t - 1:t], ACT.Sqrt, bias=eps[:, :],
                                         scale=1.0 / GW).then_inc(q["std"], 1)
                if t >= 2:
                    act.wait_ge(q["tr_done"], t - 1)
                    nc.scalar.copy(yT[:, 0, :, (t - 2) * P:(t - 1) * P],
                                   tr[:, :].rearrange("p (c q) -> p c q", q=P)).then_inc(q["tr_high"], 1)
                if t == TT - EARLY_Z:
                    act.wait_ge(k.w_branch_in, 16)
                    for c in range(4):
                        nc.scalar.activation(ws[:, 0, c], w[:, c], ACT.Copy, scale=gain[:, c:c + 1]) \
                            .then_inc(q["w_high"], 1)

        @block.vector
        def _(dve):
            step = chain(dve, q["dve_step"])
            v = nc.vector
            v.memset(eps[:, :], EPS).then_inc(q["small"], 1)
            v.tensor_scalar(gain[:, :], k.pv("ssm_norm_g_2", 4 * g, 4), W_UP, None, ALU.mult).then_inc(q["small"], 1)
            dve.wait_ge(q["small"], 2)
            def decayed(t):
                s = t % 2
                dve.wait_ge(q["cb_done"], t + 1)
                v.tensor_tensor(cbm[:, s], cb[:, :], k.const("upto"), ALU.mult).then_inc(q["cbm_done"], 1)
                dve.wait_ge(q["cbm_done"], t + 1)
                dve.wait_ge(q["E_done"], t + 1)
                v.tensor_tensor(M[:, s], E[:, s].rearrange("p (h l) -> p h l", l=P),
                                cbm[:, s].unsqueeze(1).to_broadcast([P, HPG, P]), ALU.mult).then_inc(q["M_done"], 1)

            decayed(0)
            for t in range(TT + 2):
                s = t % 2
                if t - 1 in end:
                    accumulate(dve, end[t - 1])
                if t < TT:
                    if t == 0:
                        dve.wait_ge(q["st_done"], t + 1)
                        v.tensor_copy(state[:, :], st_ps[:, :]).then_inc(q["state_done"], 1)
                    else:
                        sh = state[:, :].rearrange("p (h d) -> p h d", d=SSM_HD)
                        dve.wait_ge(q["yo_done"], t)
                        step(v.tensor_tensor(sh, sh, per_head(k.e_all, t), ALU.mult))
                        dve.wait_ge(q["st_done"], t + 1)
                        v.tensor_tensor(state[:, :], state[:, :], st_ps[:, :], ALU.add).then_inc(q["state_done"], 1)
                    yh = y[:, :].rearrange("p (h d) -> p h d", d=SSM_HD)
                    xdf = xd[:, s].rearrange("p h d -> p (h d)")
                    dve.wait_ge(q["xd_done"], t + 1)
                    if t:
                        step(v.tensor_tensor(yh, yo_ps[:, :].rearrange("p (h d) -> p h d", d=SSM_HD),
                                             per_head(k.e_cum, t), ALU.mult))
                        dve.sem_inc(q["yo_read"], 1)
                        step(v.tensor_tensor(y[:, :], y[:, :], xdf, ALU.add))
                        xdf = y[:, :]
                    else:
                        dve.sem_inc(q["yo_read"], 1)
                    if t + 1 < TT:
                        decayed(t + 1)
                    if t in middle:
                        accumulate(dve, middle[t])
                    dve.wait_ge(q["yd_done"], t + 1)
                    v.tensor_tensor(y[:, :], yd_ps[:, :], xdf, ALU.add).then_inc(q["y_done"], 1)
                    dve.wait_ge(q["y_done"], t + 1)
                    z = k.z_ssm[:, t, :]
                    if t >= EARLY_Z:
                        dve.wait_ge(q["z_out"], t - EARLY_Z + 1)
                    v.tensor_tensor(z, z, y[:, :], ALU.mult).then_inc(q["gated"], 1)
                    dve.wait_ge(q["gated"], t + 1)
                elif t in middle:
                    accumulate(dve, middle[t])
                if 1 <= t <= TT:
                    dve.wait_ge(q["std"], t)
                    step(v.reciprocal(ss[:, t - 1:t], ss[:, t - 1:t]))
                    v.tensor_scalar(k.z_ssm[:, t - 1, :], k.z_ssm[:, t - 1, :], ss[:, t - 1:t], None, ALU.mult) \
                        .then_inc(q["normed"], 1)
                if t >= 2:
                    dve.wait_ge(q["tr_high"], t - 1)
                    h = yT[:, 0, :, (t - 2) * P:(t - 1) * P]
                    v.tensor_tensor(yT[:, 1, :, (t - 2) * P:(t - 1) * P],
                                    tr[:, :].rearrange("p (c q) -> p c q", q=P), h, ALU.subtract) \
                        .then_inc(q["tr_low"], 1)
                if TT - EARLY_Z <= t < TT - EARLY_Z + 2:
                    for c in range(2 * (t - TT + EARLY_Z), 2 * (t - TT + EARLY_Z) + 2):
                        dve.wait_ge(q["w_high"], c + 1)
                        v.scalar_tensor_tensor(ws[:, 1, c], in0=w[:, c], scalar=gain[:, c:c + 1], in1=ws[:, 0, c],
                                               op0=ALU.mult, op1=ALU.subtract).then_inc(q["w_low"], 1)
            accumulate(dve, end[TT + 1])
            for j in range(KC, 2 * KC):
                accumulate(dve, j)


def merge_stage(k):
    nc, ins = k.nc, k.ins
    with ExitStack() as ctx:
        w = k.sb("mg_w", [P, 2, KC, P], ctx=ctx)
        ws = k.sb("mg_ws", [P, 2, 2, KC, P], F16, ctx=ctx)
        sig, att = k.sb("mg_sig", [P, 2, S], ctx=ctx), k.sb("mg_att", [P, KC, S], ctx=ctx)
        att_in = [k.sem(f"mg_att_in{j}") for j in range(KC)]
        sig_in = [k.sem(f"mg_sig_in{i}") for i in range(2)]
        acc = [k.ps(f"mg_ps{i}", [P, S], ctx=ctx) for i in range(2)]
        w_in = [k.sem(f"mg_w_in{i}") for i in range(2)]
        done, out, mul, added, high, low, m_high = (k.sem(f"mg_{n}") for n in (
            "done", "out", "mul", "added", "high", "low", "m_high"))
        late = KC - EARLY_GATES
        block = ctx.enter_context(nc.Block())

        @block.sync
        def _(sp):
            for i in range(2):
                sp.dma_start(w[:, i], ins["w_gates"][2 * KC + EARLY_GATES + i]).then_inc(w_in[i], 16)
            for j in range(KC):
                if j < EARLY_GATES:
                    if j >= 2:
                        sp.wait_ge(added, j - 1)
                    sp.dma_start(sig[:, j % 2], k.gates_dram[KC + j]).then_inc(sig_in[j % 2], 16)
                sp.dma_start(att[:, j, :], k.gates_dram[j]).then_inc(att_in[j], 16)
            for i in range(2, late):
                sp.wait_ge(high, i - 1)
                sp.wait_ge(low, i - 1)
                sp.dma_start(w[:, i % 2], ins["w_gates"][2 * KC + EARLY_GATES + i]).then_inc(w_in[i % 2], 16)
            for j in range(KC):
                sp.dma_start(k.next_w[:, j, :], ins["w_out_2"][j * P:(j + 1) * P, :]).then_inc(k.next_w_in, 16)

        @block.tensor
        def _(pe):
            for i in range(late):
                pe.wait_ge(high, i + 1)
                pe.wait_ge(low, i + 1)
                if i >= 2:
                    pe.wait_ge(out, i - 1)
                for a in range(0, S, HALF):
                    for c in range(KC):
                        last = product(nc, acc[i % 2][:, a:a + HALF], part(ws, i % 2, c),
                                       part(k.hT, c, slice(a, a + HALF)), c == 0, c == KC - 1)
                last.then_inc(done, 1)

        @block.scalar
        def _(act):
            def split(i):
                act.wait_ge(w_in[i % 2], 16 * (i // 2 + 1))
                if i >= 2:
                    act.wait_ge(done, i - 1)
                high_part(nc, ws[:, 0, i % 2], w[:, i % 2]).then_inc(high, 1)

            split(0)
            split(1)
            for j in range(KC):
                if j >= EARLY_GATES:
                    i = j - EARLY_GATES
                    if i and i + 1 < late:
                        split(i + 1)
                    act.wait_ge(done, i + 1)
                    act.wait_ge(added, j - 1)
                    nc.scalar.activation(sig[:, j % 2], acc[i % 2][:, :], ACT.Sigmoid,
                                         scale=1.0 / W_UP).then_inc(out, 1)
                act.wait_ge(added, j + 1)
                nc.scalar.copy(k.merged[:, 0, j, :], att[:, j, :]).then_inc(m_high, 1)

        @block.vector
        def _(dve):
            def split(i):
                dve.wait_ge(high, i + 1)
                low_part(nc, ws[:, 1, i % 2].rearrange("p c q -> p (c q)"), w[:, i % 2].rearrange("p c q -> p (c q)"),
                         ws[:, 0, i % 2].rearrange("p c q -> p (c q)")).then_inc(low, 1)

            split(0)
            split(1)
            for j in range(KC):
                if j >= EARLY_GATES:
                    i = j - EARLY_GATES
                    if i and i + 1 < late:
                        split(i + 1)
                    dve.wait_ge(out, i + 1)
                else:
                    dve.wait_ge(sig_in[j % 2], 16 * (j // 2 + 1))
                nc.vector.tensor_tensor(sig[:, j % 2], sig[:, j % 2], k.y_ssm[:, j, :], ALU.mult).then_inc(mul, 1)
                dve.wait_ge(mul, j + 1)
                dve.wait_ge(att_in[j], 16)
                nc.vector.tensor_tensor(att[:, j, :], att[:, j, :], sig[:, j % 2], ALU.add).then_inc(added, 1)
                dve.wait_ge(m_high, j + 1)
                nc.vector.tensor_tensor(k.merged[:, 1, j, :], att[:, j, :], k.merged[:, 0, j, :], ALU.subtract)


def mixer_program(nc, ins, out):
    with ExitStack() as ctx:
        k = Core(nc, ctx, ins)
        k.params, k.consts = k.sb("params", [P, PV_N]), k.sb("consts", [P, len(CONSTS), P])
        k.mod, k.gain = k.sb("mod", [P, 9 * KC]), k.sb("gain", [P, 3 * KC])
        k.csilu = k.sb("csilu", [P, 2, KC])
        k.x_dram = nc.dram_tensor("x_second", (S, D), F32, kind="Internal").ap()
        k.gates_dram = nc.dram_tensor("gate_tiles", (KC + EARLY_GATES, P, S), F32, kind="Internal").ap()
        k.hT = k.sb("hT", [P, 2, KC, S], F16)
        with ExitStack() as first:
            k.x_tok = k.sb("x_tok", [P, TT, D], ctx=first)
            alloc_routing(k, first)
            modulation_stage(k)
            with ExitStack() as c:
                k.y = k.sb("conv_y", [P, KC, S], ctx=c)
                norm_transpose_stage(k, "mix", k.x_tok, k.gain[:, 0:KC], k.mod[:, 0:KC])
                conv_stage(k)
                k.next_w, k.next_w_in = k.sb("conv_out_w", [P, KC, D], ctx=c), k.sem("conv_out_w_in")
                conv_norm_stage(k)
                token_projection_stage(k, "co", k.hT, k.mod[:, 2 * KC:3 * KC],
                                       pieces=range(FIRST_PIECES, MOD_PIECES))
            norm_transpose_stage(k, "ffn", k.x_tok, k.gain[:, KC:2 * KC], k.mod[:, 3 * KC:4 * KC],
                                 normed_dram=k.normed_dram)
            k.clear_semaphores()
            router_stage(k)
            experts_stage(k)
            combine_stage(k)
            norm_transpose_stage(k, "two", k.x_tok, k.gain[:, 2 * KC:3 * KC], k.mod[:, 6 * KC:7 * KC],
                                 raw_dram=k.x_dram)
        k.clear_semaphores()
        second_block(k, out)


def second_block(k, out):
    ctx = k.ctx
    k.dt_raw, k.widx = k.sb("dt_raw", [P, TT, SSM_HEADS]), k.sb("widx", [P, TT, IDX_HEADS])
    with ExitStack() as att:
        k.z_att = k.sb("z_att", [P, KC, S], ctx=att)
        k.qT, k.kT = k.sb("qT", [P, HEADS, S], ctx=att), k.sb("kT", [P, KV_HEADS, S], ctx=att)
        k.v_tok = k.sb("v_tok", [P, TT, KV_HEADS * HD], ctx=att)
        k.bias = k.sb("bias", [P, TT * (TT + 1) // 2 * P], BF16, ctx=att)
        with ExitStack() as idx:
            k.qidxT, k.kidxT = k.sb("qidxT", [P, 2, S], ctx=idx), k.sb("kidxT", [P, S], ctx=idx)
            with ExitStack() as q_weights:
                k.ws_q = k.sb("ws_q", [P, KC, S], ctx=q_weights)
                qkv_stage(k)
            select_stage(k)
        attention_stage(k)
        branch_att_stage(k)
    k.clear_semaphores()
    with ExitStack() as s:
        k.y_ssm = k.sb("y_ssm", [P, KC, S], ctx=s)
        with ExitStack() as grp:
            k.dt, k.adt, k.e_cum, k.e_after, k.e_all = (
                k.sb(n, [P, TT, SSM_HEADS], ctx=grp) for n in ("dt", "adt", "e_cum", "e_after", "e_all"))
            k.d_skip = k.sb("d_skip", [P, SSM_HEADS], ctx=grp)
            step_sizes_stage(k)
            k.x_ssm, k.z_ssm = k.sb("x_ssm", [P, TT, GW], ctx=grp), k.sb("z_ssm", [P, TT, GW], ctx=grp)
            k.B_tok = k.sb("B_tok", [P, TT, SSM_N], ctx=grp)
            k.BT, k.CT = k.sb("BT", [P, S], ctx=grp), k.sb("CT", [P, S], ctx=grp)
            k.w_group, k.ws_group = k.sb("w_group", [P, KC, GW], ctx=grp), k.sb("ws_group", [P, 2, KC, GW], F16, ctx=grp)
            k.w_first = k.sb("w_first", [P, KC, P], ctx=grp)
            k.yT = k.sb("yT", [P, 2, 4, S], F16, ctx=grp)
            for g in range(SSM_GROUPS):
                k.w_branch_in = k.sem(f"w_branch_in{g}")
                ssm_inputs_stage(k, g)
                ssm_scan_stage(k, g)
                k.clear_semaphores()
        k.merged = k.sb("merged", [P, 2, KC, S], F16, ctx=s)
        k.next_w, k.next_w_in = k.sb("out_w", [P, KC, D], ctx=s), k.sem("out_w_in")
        merge_stage(k)
        k.x_tok = k.y_ssm
        token_projection_stage(k, "fin", k.merged, k.mod[:, 8 * KC:9 * KC], out_dram=out, x_from=k.x_dram)


def layout(inputs):
    f = np.ascontiguousarray
    d = {n: np.asarray(v) for n, v in inputs.items()}

    def columns(name, n):
        v = d[name]
        if name == "conv_w_dw":
            return v[0].reshape(CONV, KC, P).transpose(2, 1, 0).reshape(P, n)
        if name == "conv_w_2":
            return v[0].reshape(SSM_CONV, 24, P).transpose(2, 1, 0).reshape(P, n)
        return v.reshape(-1, P).T

    def tiles(w):
        return f(w.reshape(KC, P, w.shape[1] // P, P).transpose(2, 1, 0, 3))

    q0, z0, i0, zs0, x0, dt0, g0 = 0, 1536, 2560, 2884, 4932, 8004, 8036
    w = d["w_in_2"][0]
    consts, freq = constant_tables()
    return {
        "x": d["x"][0], "params": f(np.concatenate([columns(n, m) for n, m in PV_FIELDS], axis=1)),
        "consts": consts, "freq": freq, "rows": row_constants(),
        "token_ids": f(np.arange(S, dtype=np.float32).reshape(TT, P).T),
        "ada_w": d["ada_w"][0], "ada_w_2": d["ada_w_2"][0],
        "conv_w_in": tiles(d["conv_w_in"][0]), "conv_w_out": d["conv_w_out"][0],
        "router_w": f(np.concatenate([d["moe_w_rg"][0], d["moe_w_re"][0]], axis=1)),
        "router_b": f(np.concatenate([d["moe_b_rg"][0], d["moe_b_re"][0]])),
        "moe_w_gate": d["moe_w_gate"][0], "moe_w_up": d["moe_w_up"][0], "moe_w_down": d["moe_w_down"][0],
        "final_g": d["final_g"], "positions": f(d["positions_2"][0].reshape(TT, P).T),
        "q_norm_g": d["q_norm_g_2"][0], "k_norm_g": d["k_norm_g_2"][0],
        "idx_ln_g": d["idx_k_ln_g_2"][0], "idx_ln_b": d["idx_k_ln_b_2"][0],
        "w_tok": f(np.concatenate([w[:, q0:z0], w[:, i0:zs0], w[:, dt0:g0]], axis=1)),
        "w_gates": tiles(np.concatenate([w[:, z0:i0], w[:, g0:]], axis=1)),
        "w_xbc": tiles(w[:, x0:dt0]), "w_z": f(w[:, zs0:x0]),
        "dt_bias": d["dt_bias_2"][0], "a_log": d["a_log_2"][0], "d_skip": d["d_skip_2"][0],
        "w_branch_att": tiles(d["w_branch_att_2"][0]), "w_branch_ssm": d["w_branch_ssm_2"][0],
        "w_out_2": d["w_out_2"][0],
    }


def kernel(**inputs):
    import concourse.bacc as bacc
    from concourse.bass_utils import run_bass_kernel_spmd

    nc = bacc.Bacc("TRN2", target_bir_lowering=False, num_devices=1)
    arrays, ins = {}, {}
    for name, a in layout(inputs).items():
        arrays[f"in_{name}"] = a
        ins[name] = nc.dram_tensor(f"in_{name}", a.shape, mybir.dt.from_np(a.dtype), kind="ExternalInput").ap()
    out = nc.dram_tensor("out_x", (S, D), F32, kind="ExternalOutput").ap()
    mixer_program(nc, ins, out)
    r = run_bass_kernel_spmd(nc, [arrays], core_ids=[0])
    return r.results[0]["out_x"].reshape(1, S, D)
```
